# Optimizing a Trainium2 kernel written in Bass

```python
import jax, jax.numpy as jnp
from jax import lax
import numpy as np
import math

D_MODEL = 1024
BATCH = 1
SEQ = 512
DEPTH = 1

HG_HEADS = 8
HG_DK = 128
HG_DV = D_MODEL // HG_HEADS
HG_CHUNK = 64
RET_HEADS = 8
RET_DV = D_MODEL // RET_HEADS
RET_DK = RET_DV // 2
RET_CHUNK = 128
ROPE_BASE = 10000.0
EPS = 1e-6

HG_Q = HG_HEADS * HG_DK
HG_V = HG_HEADS * HG_DV
RET_Q = RET_HEADS * RET_DK
RET_V = RET_HEADS * RET_DV
SPLITS = [HG_Q, HG_Q, HG_V, HG_V, RET_Q, RET_Q, RET_V, RET_V, D_MODEL, D_MODEL]
D_IN = sum(SPLITS)


def rms_norm(x, g):
    xf = x.astype(jnp.float32)
    y = xf * lax.rsqrt(jnp.mean(xf * xf, axis=-1, keepdims=True) + EPS)
    return (y * g.astype(jnp.float32)).astype(x.dtype)

def head_rms_norm(o, g):
    H, d = o.shape[-2], o.shape[-1]
    y = o * lax.rsqrt(jnp.mean(o * o, axis=-1, keepdims=True) + EPS)
    y = y * g.astype(jnp.float32).reshape(H, d)
    return y.reshape(o.shape[0], o.shape[1], H * d)

def rotary(t, pos):
    dk = t.shape[-1]
    inv_freq = 1.0 / (ROPE_BASE ** jnp.linspace(0.0, 1.0, dk // 2, dtype=jnp.float32))
    ang = pos.astype(jnp.float32)[:, None] * inv_freq[None, :]
    cos = jnp.cos(ang)[None, :, None, :]
    sin = jnp.sin(ang)[None, :, None, :]
    t1, t2 = t[..., : dk // 2], t[..., dk // 2:]
    return jnp.concatenate([t1 * cos - t2 * sin, t1 * sin + t2 * cos], axis=-1)

def hgrn2_chunkwise(q, fpre, v, lb):
    B, L, H, dk = q.shape
    dv = v.shape[-1]
    C = HG_CHUNK
    N = L // C
    q = jax.nn.silu(q)
    lbh = lb.astype(jnp.float32).reshape(H, dk)
    f = lbh + (1.0 - lbh) * jax.nn.sigmoid(fpre)
    k = 1.0 - f
    logf = jnp.log(f)

    def to_chunks(t):
        return t.reshape(B, N, C, H, t.shape[-1]).transpose(1, 0, 3, 2, 4)

    mask = jnp.tril(jnp.ones((C, C), dtype=bool))[:, :, None]

    def step(S, inp):
        qc, kc, lfc, vc = inp
        b = jnp.cumsum(lfc, axis=2)
        inter = jnp.einsum('bhtd,bhde->bhte', qc * jnp.exp(b), S)
        diff = b[:, :, :, None, :] - b[:, :, None, :, :]
        decay = jnp.exp(jnp.where(mask, diff, -jnp.inf))
        A = jnp.einsum('bhtsd,bhsd->bhts', qc[:, :, :, None, :] * decay, kc)
        intra = jnp.einsum('bhts,bhse->bhte', A, vc)
        b_last = b[:, :, -1:, :]
        S_new = jnp.exp(b_last[:, :, 0, :])[..., None] * S + jnp.einsum(
            'bhsd,bhse->bhde', kc * jnp.exp(b_last - b), vc)
        return S_new, inter + intra

    S0 = jnp.zeros((B, H, dk, dv), jnp.float32)
    _, o = lax.scan(step, S0, (to_chunks(q), to_chunks(k), to_chunks(logf), to_chunks(v)))
    return o.transpose(1, 0, 3, 2, 4).reshape(B, L, H, dv)

def retention_chunkwise(q, k, v):
    B, L, H, dk = q.shape
    dv = v.shape[-1]
    C = RET_CHUNK
    N = L // C
    log_gamma = jnp.log(1.0 - jnp.exp2(-5.0 - jnp.arange(H, dtype=jnp.float32)))
    k = k * (dk ** -0.5)
    qc = q.reshape(B, N, C, H, dk).transpose(0, 3, 1, 2, 4)
    kc = k.reshape(B, N, C, H, dk).transpose(0, 3, 1, 2, 4)
    vc = v.reshape(B, N, C, H, dv).transpose(0, 3, 1, 2, 4)
    idx = jnp.arange(C, dtype=jnp.float32)
    rel = idx[:, None] - idx[None, :]
    Dm = jnp.where(rel >= 0, jnp.exp(log_gamma[:, None, None] * jnp.maximum(rel, 0.0)), 0.0)
    scores = jnp.einsum('bhnid,bhnjd->bhnij', qc, kc) * Dm[:, None]
    intra = jnp.einsum('bhnij,bhnje->bhnie', scores, vc)
    zeta = jnp.exp(log_gamma[:, None] * (C - 1.0 - idx))
    chunk_state = jnp.einsum('bhnjd,bhnje->bhnde', kc * zeta[:, None, :, None], vc)
    chunk_decay = jnp.exp(log_gamma * C)[None, :, None, None]

    def step(R, s):
        return chunk_decay * R + s, R

    R0 = jnp.zeros((B, H, dk, dv), jnp.float32)
    _, R_prev = lax.scan(step, R0, chunk_state.transpose(2, 0, 1, 3, 4))
    R_prev = R_prev.transpose(1, 2, 0, 3, 4)
    xi = jnp.exp(log_gamma[:, None] * (idx + 1.0))
    cross = jnp.einsum('bhnid,bhnde->bhnie', qc * xi[:, None, :, None], R_prev)
    return (intra + cross).transpose(0, 2, 3, 1, 4).reshape(B, L, H, dv)

def first_inputs(seed: int = 0) -> dict:
    key = jax.random.key(seed)
    ks = jax.random.split(key, 12)
    f32 = jnp.float32
    x = jax.random.normal(ks[0], (BATCH, SEQ, D_MODEL), f32)
    c = jax.random.normal(ks[1], (BATCH, D_MODEL), f32)
    norm_g = 1.0 + 0.05 * jax.random.normal(ks[2], (DEPTH, D_MODEL), f32)
    w_ada = 0.5 * D_MODEL ** -0.5 * jax.random.normal(ks[3], (DEPTH, D_MODEL, 3 * D_MODEL), f32)
    b_ada = 0.02 * jax.random.normal(ks[4], (DEPTH, 3 * D_MODEL), f32)
    w_in = D_MODEL ** -0.5 * jax.random.normal(ks[5], (DEPTH, D_MODEL, D_IN), f32)
    hg_lb_logits = 0.5 * jax.random.normal(ks[6], (DEPTH + 1, HG_Q), f32)
    hg_norm_g = 1.0 + 0.05 * jax.random.normal(ks[7], (DEPTH, HG_V), f32)
    ret_norm_g = 1.0 + 0.05 * jax.random.normal(ks[8], (DEPTH, RET_V), f32)
    w_out = D_MODEL ** -0.5 * jax.random.normal(ks[9], (DEPTH, D_MODEL, D_MODEL), f32)
    final_g = 1.0 + 0.05 * jax.random.normal(ks[10], (D_MODEL,), f32)
    return {"x": x, "c": c, "norm_g": norm_g, "w_ada": w_ada, "b_ada": b_ada,
            "w_in": w_in, "hg_lb_logits": hg_lb_logits, "hg_norm_g": hg_norm_g,
            "ret_norm_g": ret_norm_g, "w_out": w_out, "final_g": final_g}

def first_block(x, c, norm_g, w_ada, b_ada, w_in, hg_lb_logits, hg_norm_g, ret_norm_g, w_out, final_g):
    B, L, D = x.shape
    pos = jnp.arange(L, dtype=jnp.int32)
    lower_bounds = jnp.cumsum(jax.nn.softmax(hg_lb_logits.astype(jnp.float32), axis=0), axis=0)
    offsets = np.cumsum([0] + SPLITS)[1:-1].tolist()
    for layer in range(DEPTH):
        mod = jax.nn.silu(c) @ w_ada[layer] + b_ada[layer]
        shift, scale, gate = jnp.split(mod[:, None, :], 3, axis=-1)
        h = rms_norm(x, norm_g[layer]) * (1.0 + scale) + shift
        proj = h @ w_in[layer]
        (hq, hf, hi, hz, rq, rk, rv, rz, ga, gb) = jnp.split(proj, offsets, axis=-1)
        f32 = jnp.float32
        oA = hgrn2_chunkwise(hq.astype(f32).reshape(B, L, HG_HEADS, HG_DK),
                             hf.astype(f32).reshape(B, L, HG_HEADS, HG_DK),
                             hi.astype(f32).reshape(B, L, HG_HEADS, HG_DV),
                             lower_bounds[layer])
        uA = head_rms_norm(oA, hg_norm_g[layer]) * jax.nn.silu(hz.astype(f32))
        qB = rotary(rq.astype(f32).reshape(B, L, RET_HEADS, RET_DK), pos)
        kB = rotary(rk.astype(f32).reshape(B, L, RET_HEADS, RET_DK), pos)
        oB = retention_chunkwise(qB, kB, rv.astype(f32).reshape(B, L, RET_HEADS, RET_DV))
        uB = head_rms_norm(oB, ret_norm_g[layer]) * jax.nn.silu(rz.astype(f32))
        m = (jax.nn.sigmoid(ga.astype(f32)) * uA + jax.nn.sigmoid(gb.astype(f32)) * uB).astype(x.dtype)
        x = x + gate * (m @ w_out[layer])
    return rms_norm(x, final_g)


DEPTH_2 = 2

N_A_LAYERS = DEPTH_2 // 2
N_B_LAYERS = DEPTH_2 - N_A_LAYERS
CONV_WIDTH = 31
HEAD_DIM = 64
N_HEADS = D_MODEL // HEAD_DIM
N_KV_HEADS = N_HEADS // 4
GROUP = N_HEADS // N_KV_HEADS
WINDOW = 128
BLOCK = 128
N_BUCKETS = 32
MAX_DISTANCE = 128
D_FF = -(-8 * D_MODEL // (3 * 256)) * 256
NEG_INF = -1e30


def rmsnorm(x, g):
    xf = x.astype(jnp.float32)
    xf = xf * lax.rsqrt(jnp.mean(xf * xf, axis=-1, keepdims=True) + EPS)
    return (xf * g.astype(jnp.float32)).astype(x.dtype)

def layernorm(x, g, b):
    xf = x.astype(jnp.float32)
    mu = jnp.mean(xf, axis=-1, keepdims=True)
    var = jnp.mean(jnp.square(xf - mu), axis=-1, keepdims=True)
    y = (xf - mu) * lax.rsqrt(var + EPS) * g.astype(jnp.float32) + b.astype(jnp.float32)
    return y.astype(x.dtype)

def swiglu_ffn(x, w_up, w_down):
    gate, up = jnp.split(x @ w_up, 2, axis=-1)
    return (jax.nn.silu(gate) * up) @ w_down

def conformer_conv(x, w_pw1, b_pw1, w_dw, b_dw, ln_g, ln_b, w_pw2, b_pw2):
    a = jax.nn.glu(x @ w_pw1 + b_pw1, axis=-1)
    y = lax.conv_general_dilated(
        a, w_dw[:, None, :].astype(a.dtype), window_strides=(1,),
        padding=((CONV_WIDTH - 1, 0),),
        dimension_numbers=('NWC', 'WIO', 'NWC'),
        feature_group_count=D_MODEL) + b_dw
    y = jax.nn.silu(layernorm(y, ln_g, ln_b))
    return y @ w_pw2 + b_pw2

def t5_causal_bucket(dist):
    max_exact = N_BUCKETS // 2
    d = jnp.maximum(dist, 0)
    log_ratio = jnp.log(jnp.maximum(d, 1).astype(jnp.float32) / max_exact) / math.log(MAX_DISTANCE / max_exact)
    large = max_exact + (log_ratio * (N_BUCKETS - max_exact)).astype(jnp.int32)
    large = jnp.minimum(large, N_BUCKETS - 1)
    return jnp.where(d < max_exact, d, large)

def banded_sink_attention(q, k, v, sinks, rel_bias):
    B, S = q.shape[0], q.shape[1]
    nb = S // BLOCK
    qb = q.reshape(B, nb, BLOCK, N_KV_HEADS, GROUP, HEAD_DIM)
    kb = k.reshape(B, nb, BLOCK, N_KV_HEADS, HEAD_DIM)
    vb = v.reshape(B, nb, BLOCK, N_KV_HEADS, HEAD_DIM)
    pad = ((0, 0), (1, 0), (0, 0), (0, 0), (0, 0))
    k_band = jnp.concatenate([jnp.pad(kb, pad)[:, :-1], kb], axis=2)
    v_band = jnp.concatenate([jnp.pad(vb, pad)[:, :-1], vb], axis=2)

    s = jnp.einsum('bnqhgd,bnkhd->bnhgqk', qb, k_band,
                   preferred_element_type=jnp.float32) * (HEAD_DIM ** -0.5)

    qi = jnp.arange(BLOCK, dtype=jnp.int32)
    kj = jnp.arange(2 * BLOCK, dtype=jnp.int32)
    dist = qi[:, None] + BLOCK - kj[None, :]
    in_window = (dist >= 0) & (dist < WINDOW)
    bias = rel_bias.astype(jnp.float32)[t5_causal_bucket(dist)]
    bias = jnp.transpose(bias, (2, 0, 1)).reshape(N_KV_HEADS, GROUP, BLOCK, 2 * BLOCK)
    key_pos = (jnp.arange(nb, dtype=jnp.int32)[:, None] - 1) * BLOCK + kj[None, :]
    mask = in_window[None, :, :] & (key_pos >= 0)[:, None, :]

    s = jnp.where(mask[None, :, None, None], s + bias, NEG_INF)
    sink = sinks.astype(jnp.float32).reshape(N_KV_HEADS, GROUP, 1, 1)
    m = jnp.maximum(jnp.max(s, axis=-1, keepdims=True), sink)
    p = jnp.exp(s - m)
    probs = p / (jnp.sum(p, axis=-1, keepdims=True) + jnp.exp(sink - m))
    o = jnp.einsum('bnhgqk,bnkhd->bnqhgd', probs.astype(v.dtype), v_band)
    return o.reshape(B, S, N_HEADS * HEAD_DIM)

def second_inputs(seed: int = 0) -> dict:
    key = jax.random.key(seed)
    ks = jax.random.split(key, 24)
    f32 = jnp.float32
    D, HD, KVD = D_MODEL, N_HEADS * HEAD_DIM, N_KV_HEADS * HEAD_DIM
    nrm = lambda k, shape, scale: jax.random.normal(k, shape, f32) * scale
    gain = lambda k, shape: 1.0 + 0.05 * jax.random.normal(k, shape, f32)
    return {
        "x": jax.random.normal(ks[0], (BATCH, SEQ, D), f32),
        "norm_mix": gain(ks[1], (DEPTH_2, D)),
        "norm_ffn": gain(ks[2], (DEPTH_2, D)),
        "conv_w_pw1": nrm(ks[3], (N_A_LAYERS, D, 2 * D), D ** -0.5),
        "conv_b_pw1": nrm(ks[4], (N_A_LAYERS, 2 * D), 0.02),
        "conv_w_dw": nrm(ks[5], (N_A_LAYERS, CONV_WIDTH, D), CONV_WIDTH ** -0.5),
        "conv_b_dw": nrm(ks[6], (N_A_LAYERS, D), 0.02),
        "conv_ln_g": gain(ks[7], (N_A_LAYERS, D)),
        "conv_ln_b": nrm(ks[8], (N_A_LAYERS, D), 0.02),
        "conv_w_pw2": nrm(ks[9], (N_A_LAYERS, D, D), D ** -0.5),
        "conv_b_pw2": nrm(ks[10], (N_A_LAYERS, D), 0.02),
        "norm_kv": gain(ks[11], (D,)),
        "w_kv": nrm(ks[12], (D, 2 * KVD), D ** -0.5),
        "w_q": nrm(ks[13], (N_B_LAYERS, D, HD), D ** -0.5),
        "w_o": nrm(ks[14], (N_B_LAYERS, HD, D), HD ** -0.5),
        "sinks": nrm(ks[15], (N_B_LAYERS, N_HEADS), 0.5),
        "rel_bias": nrm(ks[16], (N_BUCKETS, N_HEADS), 0.5),
        "ffn_w_up": nrm(ks[17], (DEPTH_2, D, 2 * D_FF), D ** -0.5),
        "ffn_w_down": nrm(ks[18], (DEPTH_2, D_FF, D), D_FF ** -0.5),
        "norm_final": gain(ks[19], (D,)),
    }

def second_block(x, norm_mix, norm_ffn, conv_w_pw1, conv_b_pw1, conv_w_dw, conv_b_dw,
              conv_ln_g, conv_ln_b, conv_w_pw2, conv_b_pw2, norm_kv, w_kv, w_q, w_o,
              sinks, rel_bias, ffn_w_up, ffn_w_down, norm_final):
    B, S = x.shape[0], x.shape[1]
    h = x
    k_shared = v_shared = None
    for l in range(DEPTH_2):
        if l < N_A_LAYERS:
            i = l
            h = h + conformer_conv(rmsnorm(h, norm_mix[l]), conv_w_pw1[i], conv_b_pw1[i],
                                   conv_w_dw[i], conv_b_dw[i], conv_ln_g[i], conv_ln_b[i],
                                   conv_w_pw2[i], conv_b_pw2[i])
        else:
            if l == N_A_LAYERS:
                kv = rmsnorm(h, norm_kv) @ w_kv
                k_flat, v_flat = jnp.split(kv, 2, axis=-1)
                k_shared = k_flat.reshape(B, S, N_KV_HEADS, HEAD_DIM)
                v_shared = v_flat.reshape(B, S, N_KV_HEADS, HEAD_DIM)
            j = l - N_A_LAYERS
            q = (rmsnorm(h, norm_mix[l]) @ w_q[j]).reshape(B, S, N_HEADS, HEAD_DIM)
            attn = banded_sink_attention(q, k_shared, v_shared, sinks[j], rel_bias)
            h = h + attn @ w_o[j]
        h = h + swiglu_ffn(rmsnorm(h, norm_ffn[l]), ffn_w_up[l], ffn_w_down[l])
    return rmsnorm(h, norm_final)


def setup_inputs(seed=0):
    out = dict(first_inputs(seed))
    for name, value in second_inputs(seed + 1).items():
        if name != "x":
            out[name + "_2"] = value
    return out


def reference(
    x, c, norm_g, w_ada, b_ada, w_in, hg_lb_logits, hg_norm_g, ret_norm_g, w_out, final_g,
    norm_mix_2, norm_ffn_2, conv_w_pw1_2, conv_b_pw1_2, conv_w_dw_2, conv_b_dw_2, conv_ln_g_2,
    conv_ln_b_2, conv_w_pw2_2, conv_b_pw2_2, norm_kv_2, w_kv_2, w_q_2, w_o_2, sinks_2,
    rel_bias_2, ffn_w_up_2, ffn_w_down_2, norm_final_2,
):
    x = first_block(
        x, c, norm_g, w_ada, b_ada, w_in, hg_lb_logits, hg_norm_g, ret_norm_g, w_out, final_g,
    )
    return second_block(
        x, norm_mix_2, norm_ffn_2, conv_w_pw1_2, conv_b_pw1_2, conv_w_dw_2, conv_b_dw_2,
        conv_ln_g_2, conv_ln_b_2, conv_w_pw2_2, conv_b_pw2_2, norm_kv_2, w_kv_2, w_q_2, w_o_2,
        sinks_2, rel_bias_2, ffn_w_up_2, ffn_w_down_2, norm_final_2,
    )


_drawn_inputs = setup_inputs


def setup_inputs(seed=0):
    import zlib

    import numpy as np

    out = dict(_drawn_inputs(seed))
    spreads = {}
    factors = {'norm_g': 3.268,
     'b_ada': 3.12,
     'hg_lb_logits': 7.003,
     'hg_norm_g': 8.0,
     'ret_norm_g': 8.0,
     'conv_b_pw1_2': 3.627,
     'conv_ln_b_2': 3.868,
     'norm_kv_2': 4.274,
     'sinks_2': 8.0}
    for name, (base, spread) in spreads.items():
        noise = np.random.default_rng([zlib.crc32(name.encode()), seed]).standard_normal(out[name].shape)
        drawn = base * np.exp(spread * noise) if base else spread * noise
        out[name] = __import__('jax').numpy.asarray(drawn.astype(out[name].dtype))
    for name, factor in factors.items():
        out[name] = (out[name] * factor).astype(out[name].dtype)
    return out
```

```python
from contextlib import ExitStack

import numpy as np
import concourse.bass as bass
from concourse import mybir

F32 = mybir.dt.float32
F32R = mybir.dt.float32r
I32 = mybir.dt.int32
ACT = mybir.ActivationFunctionType
ALU = mybir.AluOpType
AX_X = mybir.AxisListType.X

P = 128
T = 512
D = 1024
KC = D // P
NT = T // P
SLOTS = 4
EPS = 1e-6

HEADS = 8
PAIRS = HEADS // 2
LEVELS = 7
TINY = 1e-19
RET_DK = 64

TAPS = 31
PAD = TAPS - 1
FF_CHUNKS = 22
FF_PARTS = (8, 8, 6)
AH = 16
KVH = 4
HD = 64
BAND = 256
REACH = 383
NEG = -1e30

ADA_CHUNKS = 2 * KC
PAIR_CHUNKS = 20


def phase_starts():
    sizes = [("ada", ADA_CHUNKS), ("pairs", PAIRS * PAIR_CHUNKS), ("w_out", KC), ("pw1", 2 * KC), ("pw2", KC)]
    for layer in range(2):
        if layer == 1:
            sizes += [("kv", 4), ("q", KC), ("w_o", KC)]
        for part, n in enumerate(FF_PARTS):
            sizes += [(f"up{layer}{part}", 2 * n), (f"down{layer}{part}", KC)]
    at, starts = 0, {}
    for name, n in sizes:
        assert n % SLOTS == 0
        starts[name] = at
        at += n // SLOTS
    return starts, at


START, QUADS = phase_starts()

VEC = {}
_at = 0
for _name, _n in (("norm_g", KC), ("b_ada", 3 * KC), ("lb0", KC), ("lb1", KC), ("hg_norm_g", KC),
                  ("ret_norm_g", KC), ("norm_mix", 2 * KC), ("norm_ffn", 2 * KC), ("b_pw1", 2 * KC),
                  ("w_dw", TAPS * KC), ("b_dw", KC), ("ln_g", KC), ("ln_b", KC), ("b_pw2", KC),
                  ("norm_kv", KC), ("norm_final", KC), ("final_g", KC), ("c", KC)):
    VEC[_name] = _at
    _at += _n
VECS = _at
CONSTS = 16 * 7
PAIR_STEPS = 20


class Steps:

    def __init__(self, eng, sem):
        self.eng, self.sem = eng, sem
        self.base, self.local, self.i, self.per = 0, 0, None, 0

    def enter(self, i, per):
        self.base, self.local, self.i, self.per = self.base + self.local, 0, i, per

    def leave(self, trips):
        assert self.local == self.per, (self.local, self.per)
        self.base, self.local, self.i, self.per = self.base + trips * self.per, 0, None, 0

    def mark(self, ins):
        ins.then_inc(self.sem, 1)
        self.local += 1
        return self.local

    def wait(self, local=None):
        v = self.base + (self.local if local is None else local)
        self.eng.wait_ge(self.sem, v if self.i is None else self.i * self.per + v)

    def done(self, ins):
        self.mark(ins)
        self.wait()


def program(nc, weights, xT, vec_in, sinks_in, rel_in, rot_in, ret_tab, lvl_in, eye_in, tri_in, hot_in, ident_in,
            rel_scratch, outT):
    ctx = ExitStack()
    with ctx:
        def sb(name, shape, dt=F32, where=ctx):
            return where.enter_context(nc.sbuf_tensor(name, shape, dt))

        def sem(name):
            return ctx.enter_context(nc.semaphore(name))

        w_raw = sb("w_raw", [P, SLOTS, D])
        w_hi = sb("w_hi", [P, SLOTS, D], F32R)
        w_lo = sb("w_lo", [P, SLOTS, D], F32R)
        xa_hi = sb("xa_hi", [P, KC, T], F32R)
        xa_lo = sb("xa_lo", [P, KC, T], F32R)
        vec = sb("vec", [P, VECS])
        ones = sb("ones", [P, P])
        ident = sb("ident", [P, P])
        eps_col = sb("eps_col", [P, 1])
        mod = sb("mod", [P, 3 * KC])
        sq = sb("sq", [P, 2, T])
        lnv = sb("lnv", [P, T])
        rstd = sb("rstd", [P, T])
        hbuf = sb("hbuf", [P, 4, T])
        sink = sb("sink", [P, AH])
        neg_max = sb("neg_max", [P, 2, NT])
        row_max = sb("row_max", [P, 2, NT])
        row_sum = sb("row_sum", [P, 2, NT])
        row_inv = sb("row_inv", [P, 2, NT])
        sink_exp = sb("sink_exp", [P, 2, NT])

        first = ExitStack()
        mixed = sb("mixed", [P, KC, T], where=first)
        kt = sb("kt", [P, LEVELS, T], where=first)
        qt = sb("qt", [P, LEVELS, T // 2], where=first)
        q = sb("q", [P, 2, T], where=first)
        key = sb("key", [P, 2, T], where=first)
        cum = sb("cum", [P, 2, T], where=first)
        forget = sb("forget", [P, 2, T], where=first)
        q_far = sb("q_far", [P, 6, P], where=first)
        k_far = sb("k_far", [P, 3, P], where=first)
        val = sb("val", [P, NT, 2, 2 * P], where=first)
        rqk = sb("rqk", [P, 2, T], where=first)
        gates = sb("gates", [P, 4, T], where=first)
        unit = sb("unit", [P, 2, T], where=first)
        reset = sb("reset", [P, T], where=first)
        tri = sb("tri", [P, T], where=first)
        rot = sb("rot", [P, P], where=first)
        lvl_mask = sb("lvl_mask", [P, LEVELS, P // 2], I32, where=first)
        eye_mask = sb("eye_mask", [P, P], I32, where=first)
        lower = sb("lower", [P, KC], where=first)
        one_minus = sb("one_minus", [P, KC], where=first)
        mix_gain = sb("mix_gain", [P, KC], where=first)
        lbt = sb("lbt", [P, 4, KC], where=first)
        c_act = sb("c_act", [P, KC], where=first)
        c_pair = sb("c_pair", [P, KC, 2], F32R, where=first)
        start = ExitStack()
        x0 = sb("x0", [P, KC, T], where=start)
        start.close()
        at_h = sb("at_h", [P, NT * (T + P)], where=first)
        at_r = sb("at_r", [P, NT * (T + P)], where=first)
        first.close()

        second = ExitStack()
        xb_hi = sb("xb_hi", [P, KC, T], F32R, where=second)
        xb_lo = sb("xb_lo", [P, KC, T], F32R, where=second)
        res = sb("res", [P, KC, T], where=second)
        bias = sb("bias", [P, AH, BAND], where=second)
        hot = sb("hot", [33, REACH + 1], where=second)
        rel = sb("rel", [33, AH], where=second)
        rel_rows = sb("rel_rows", [AH, REACH + 1], where=second)
        conv_mem = ExitStack()
        glu = sb("glu", [P, KC, PAD + T], where=conv_mem)
        conv = sb("conv", [P, KC, T], where=conv_mem)
        conv_mem.close()
        attn_mem = ExitStack()
        kT = sb("kT", [P, 2, T], where=attn_mem)
        vtok = sb("vtok", [P, NT, KVH * HD], where=attn_mem)
        qT = sb("qT", [P, 2, T], where=attn_mem)
        scores = sb("scores", [P, 2, NT, BAND], where=attn_mem)
        pT = sb("pT", [P, 2, 2 * NT - 1, P], where=attn_mem)
        attn_mem.close()
        end_mem = ExitStack()
        y = sb("y", [P, KC, T], where=end_mem)
        end_mem.close()
        second.close()

        gps = ctx.enter_context(nc.psum_tensor("gps", [P, SLOTS, T], F32))
        aps = ctx.enter_context(nc.psum_tensor("aps", [P, 4, T], F32))

        raw_in = [sem(f"raw_in{j}") for j in range(SLOTS)]
        hi_ready = [sem(f"hi_ready{j}") for j in range(SLOTS)]
        lo_ready = [sem(f"lo_ready{j}") for j in range(SLOTS)]
        tile_done = [sem(f"tile_done{j}") for j in range(SLOTS)]
        evicted = [sem(f"evicted{j}") for j in range(SLOTS)]
        bank_full = [sem(f"bank_full{b}") for b in range(4)]
        taken = [sem(f"taken{b}") for b in range(4)]
        act_own = sem("act_own")
        dve_own = sem("dve_own")
        consts_in = sem("consts_in")
        x_in = sem("x_in")
        tabs_in = sem("tabs_in")
        res_in = sem("res_in")
        hot_in_sem = sem("hot_in_sem")
        made = sem("made")
        c_sig = sem("c_sig")
        c_ready = sem("c_ready")
        lb_shift = sem("lb_shift")
        lb_exp = sem("lb_exp")
        mod_ready = sem("mod_ready")
        sq_ready = sem("sq_ready")
        sum_done = sem("sum_done")
        rstd_ready = sem("rstd_ready")
        h_ready = sem("h_ready")
        xh_ready = sem("xh_ready")
        x_ready = sem("x_ready")
        f_ready = sem("f_ready")
        logf_ready = sem("logf_ready")
        q_sig = sem("q_sig")
        exps_ready = sem("exps_ready")
        decay_ready = sem("decay_ready")
        prep_done = sem("prep_done")
        rot_ready = sem("rot_ready")
        passed = sem("passed")
        osq_ready = sem("osq_ready")
        hnorm = sem("hnorm")
        gate_sig = sem("gate_sig")
        gates_used = sem("gates_used")
        mixed_ready = sem("mixed_ready")
        m_hi = sem("m_hi")
        m_lo = sem("m_lo")
        rel_full = sem("rel_full")
        rel_copied = sem("rel_copied")
        rel_out = sem("rel_out")
        bias_in = sem("bias_in")
        res_ready = sem("res_ready")
        conv_done = sem("conv_done")
        mean_done = sem("mean_done")
        center_done = sem("center_done")
        s_full = sem("s_full")
        s_taken = sem("s_taken")
        max_ready = sem("max_ready")
        exp_ready = sem("exp_ready")
        p_ready = sem("p_ready")
        pt_full = sem("pt_full")
        pt_ready = sem("pt_ready")
        o_full = sem("o_full")
        o_hi = sem("o_hi")
        o_lo = sem("o_lo")
        ff_hi = sem("ff_hi")
        ff_lo = sem("ff_lo")
        y_ready = sem("y_ready")
        out_done = sem("out_done")

        def vcol(name, c=0):
            return vec[:, VEC[name] + c:VEC[name] + c + 1]

        def vdyn(name, c):
            return vec[:, bass.ds(c + VEC[name], 1)]

        def diag(at):
            return at[:, :].rearrange("p (t s) -> p t s", s=T + P)[:, :, 0:P]

        def halves(ap, level):
            size = P >> level
            v = ap.rearrange("p (n s) -> p n s", s=size)
            h = size // 2
            return v[:, :, 0:h], v[:, :, h:size], v[:, :, h - 1:h].to_broadcast([P, T // size, h])

        FAR = ((0, 0, 3), (1, 3, 5), (2, 5, 6))
        LEVEL_BANKS = ((0, 1), (2, 3), (4, 5), (6,))
        RMS_MIX, RMS_FIRST, RMS_CONV_IN, RMS_LN, RMS_FF0, RMS_ATTN, RMS_FF1, RMS_LAST = range(8)
        X_MIX, X_CONV_IN, X_PW2, X_FF0, X_KV, X_Q, X_FF1 = range(7)
        BUILD_OF = {X_MIX: RMS_MIX, X_CONV_IN: RMS_CONV_IN, X_PW2: RMS_LN, X_FF0: RMS_FF0, X_KV: RMS_ATTN,
                    X_Q: RMS_ATTN, X_FF1: RMS_FF1}
        U_LV = (0, 17)
        U_ROT = 7
        U_SC = (9, 24)
        U_AV = ((13, 14), (28, 29))
        U_NORM = ((15, 16), (30, 31))
        USES = 8

        block = ctx.enter_context(nc.Block())

        @block.sync
        def _(sp):
            with sp.Fori(0, QUADS) as i:
                for j in range(SLOTS):
                    sp.wait_ge(lo_ready[j], i + 1)
                    sp.dma_start(w_raw[:, j, :], weights[bass.ds(i * SLOTS + j, 1)].rearrange("a p c -> p (a c)"))\
                      .then_inc(raw_in[j], 16)
            for c in range(KC):
                sp.wait_ge(y_ready, c + 1)
                sp.dma_start(outT[c * P:(c + 1) * P, :], y[:, c, :]).then_inc(out_done, 16)
            sp.wait_ge(out_done, 16 * KC)

        @block.gpsimd
        def _(pool):
            for j in range(SLOTS):
                pool.sem_inc(lo_ready[j], 1)
            with pool.Fori(0, QUADS) as i:
                for j in range(SLOTS):
                    pool.wait_ge(hi_ready[j], i + 1)
                    nc.gpsimd.tensor_tensor(w_lo[:, j, :], w_raw[:, j, :], w_hi[:, j, :].bitcast(F32), ALU.subtract)\
                      .then_inc(lo_ready[j], 1)

        @block.scalar
        def _(act):
            own = Steps(act, act_own)

            def w_high(I, j):
                act.wait_ge(raw_in[j], I * 16 + 16)
                act.wait_ge(tile_done[j], I + 1)
                nc.scalar.copy(w_hi[:, j, :], w_raw[:, j, :]).then_inc(hi_ready[j], 1)

            def ahead(I, j):
                if not isinstance(I, int) or I * SLOTS + j + 3 < QUADS * SLOTS:
                    w_high(I + (j + 3) // SLOTS, (j + 3) % SLOTS)

            def full(I, j):
                act.wait_ge(tile_done[j], I + 2)
                return gps[:, j, :]

            def rms_square(n, c, src):
                if 8 * n + c >= 2:
                    act.wait_ge(sum_done, 8 * n + c - 1)
                nc.scalar.activation(sq[:, c % 2, :], src, ACT.Square).then_inc(sq_ready, 1)

            def rms_finish(n):
                act.wait_ge(sum_done, 8 * n + 8)
                own.done(nc.scalar.activation(lnv[:], aps[:, 0, :], ACT.Ln, bias=eps_col[:], scale=1.0 / D))
                nc.scalar.activation(rstd[:], lnv[:], ACT.Exp, scale=-0.5).then_inc(rstd_ready, 1)

            def x_high(b, dst, shift=False):
                for c in range(KC):
                    act.wait_ge(h_ready, 8 * b + c + 1)
                    if shift:
                        ins = nc.scalar.activation(dst[:, c, :], hbuf[:, c % 4, :], ACT.Identity, bias=mod[:, c:c + 1])
                    else:
                        ins = nc.scalar.copy(dst[:, c, :], hbuf[:, c % 4, :])
                    ins.then_inc(xh_ready, 1)

            act.dma_start(vec[:], vec_in).then_inc(consts_in, 16)
            act.dma_start(x0[:], xT.rearrange("(k p) t -> p k t", p=P)).then_inc(x_in, 16)
            act.dma_start(lvl_mask[:], lvl_in.rearrange("p (l c) -> p l c", l=LEVELS)).then_inc(consts_in, 16)
            act.dma_start(eye_mask[:], eye_in).then_inc(consts_in, 16)
            act.dma_start(tri[:], tri_in).then_inc(consts_in, 16)
            act.dma_start(rot[:], rot_in).then_inc(consts_in, 16)
            act.dma_start(ident[:], ident_in).then_inc(consts_in, 16)
            act.dma_start(sink[:], sinks_in.to_broadcast([P, AH])).then_inc(consts_in, 16)

            act.wait_ge(consts_in, CONSTS)
            nc.scalar.activation(c_act[:], vec[:, VEC["c"]:VEC["c"] + KC], ACT.Sigmoid).then_inc(c_sig, 1)
            act.wait_ge(lb_shift, 1)
            nc.scalar.activation(lbt[:, 2:4, :], lbt[:, 0:2, :], ACT.Exp).then_inc(lb_exp, 1)
            for j in range(3):
                w_high(0, j)
            act.wait_ge(x_in, 16)
            for c in range(KC):
                rms_square(RMS_MIX, c, x0[:, c, :])
            act.wait_ge(made, 1)
            rms_finish(RMS_MIX)
            with act.Fori(0, ADA_CHUNKS // SLOTS) as i:
                for j in range(SLOTS):
                    ahead(i, j)
            x_high(X_MIX, xa_hi, shift=True)

            with act.Fori(0, PAIRS) as p:
                def at(c):
                    return p * (PAIR_CHUNKS // SLOTS) + (START["pairs"] + c // SLOTS)

                def chunk(c):
                    ahead(at(c), c % SLOTS)
                    return full(at(c), c % SLOTS)

                def bank(u):
                    act.wait_ge(bank_full[u % 4], p * USES + (u // 4 + 1))
                    return aps[:, u % 4, :]

                def decays(e):
                    act.wait_ge(exps_ready, p * 2 + (e + 1))
                    nc.scalar.activation(kt[:], kt[:], ACT.Exp)
                    nc.scalar.activation(hbuf[:, 0, :], hbuf[:, 0, :], ACT.Exp)
                    nc.scalar.activation(hbuf[:, 1, :], cum[:, e, :], ACT.Exp).then_inc(decay_ready, 1)

                def far_scores(e):
                    u = U_LV[e] + 5
                    nc.scalar.copy(at_h[:, P:T], bank(u)[:, 0:3 * P]).then_inc(taken[u % 4], 1)
                    b = bank(u + 1)
                    nc.scalar.copy(at_h[:, T + 2 * P:2 * T], b[:, 0:2 * P])
                    nc.scalar.copy(at_h[:, 2 * T + 3 * P:3 * T], b[:, 2 * P:3 * P]).then_inc(taken[(u + 1) % 4], 1)

                def head_square(e, r):
                    nc.scalar.activation(hbuf[:, 2 + r, :], bank(U_AV[e][r]), ACT.Square).then_inc(osq_ready, 1)

                def head_rstd(e, r):
                    u, dst = U_NORM[e][r], (lnv, rstd)[r]
                    if e:
                        uo = U_AV[0][r]
                        act.wait_ge(taken[uo % 4], p * USES + (uo // 4 + 2))
                    nc.scalar.activation(dst[:], bank(u), ACT.Ln, bias=eps_col[:], scale=1.0 / P).then_inc(taken[u % 4], 1)
                    act.wait_ge(taken[u % 4], p * USES + (u // 4 + 2))
                    nc.scalar.activation(dst[:], dst[:], ACT.Exp, scale=-0.5).then_inc(hnorm, 1)

                for e in range(2):
                    nc.scalar.activation(forget[:, e, :], chunk(e), ACT.Sigmoid).then_inc(evicted[e], 1)
                act.wait_ge(gates_used, p * 4 + 1)
                for e in range(2):
                    nc.scalar.activation(sq[:, e, :], chunk(2 + e), ACT.Sigmoid).then_inc(q_sig, 1)
                act.wait_ge(f_ready, p + 1)
                nc.scalar.activation(forget[:], forget[:], ACT.Ln).then_inc(logf_ready, 1)
                act.wait_ge(mixed_ready, p + 1)
                act.dma_start(gates[:], ret_tab[bass.ds(p, 1)].rearrange("a p n t -> p (a n) t")).then_inc(tabs_in, 16)
                decays(0)

                def values(c, r):
                    ahead(at(c), c % SLOTS)
                    ahead(at(c + 1), (c + 1) % SLOTS)
                    for n in range(2):
                        b = full(at(c + n), (c + n) % SLOTS)
                        nc.scalar.copy(val[:, 2 * n:2 * n + 2, r, :], b.rearrange("p (t v) -> p t v", t=2))\
                          .then_inc(evicted[(c + n) % SLOTS], 1)

                values(4, 0)
                for n in range(2):
                    nc.scalar.copy(rqk[:, n, :], chunk(6 + n)).then_inc(evicted[2 + n], 1)
                far_scores(0)
                decays(1)
                values(8, 1)
                for c in (10, 11):
                    ahead(at(c), c % SLOTS)

                def gate_product(c, e, first):
                    b = chunk(c)
                    if first:
                        k = c - 12 if c == 12 or c == 13 else c - 14
                        if c >= 16:
                            act.wait_ge(gates_used, p * 4 + (1 + e + 1))
                        nc.scalar.activation(sq[:, e, :], b, ACT.Sigmoid).then_inc(gate_sig, 1)
                    else:
                        act.wait_ge(evicted[(c - 2) % SLOTS], at(c - 2) + 2)
                        nc.scalar.activation(sq[:, e, :], b, ACT.Sigmoid).then_inc(evicted[c % SLOTS], 1)

                gate_product(12, 0, True)
                head_square(0, 0)
                gate_product(13, 1, True)
                gate_product(14, 0, False)
                head_square(0, 1)
                gate_product(15, 1, False)
                head_rstd(0, 0)
                head_rstd(0, 1)
                gate_product(16, 0, True)
                far_scores(1)
                gate_product(17, 1, True)
                gate_product(18, 0, False)
                head_square(1, 0)
                gate_product(19, 1, False)
                head_square(1, 1)
                head_rstd(1, 0)
                head_rstd(1, 1)

            act.wait_ge(mixed_ready, PAIRS + 1)
            act.dma_start(res[:], xT.rearrange("(k p) t -> p k t", p=P)).then_inc(res_in, 16)
            act.dma_start(hot[:], hot_in).then_inc(hot_in_sem, 16)
            act.dma_start(rel[0:32, :], rel_in).then_inc(hot_in_sem, 16)
            for c in range(KC):
                nc.scalar.copy(xa_hi[:, c, :], mixed[:, c, :]).then_inc(m_hi, 1)
            residual = [0]

            def residual_squares(phase, n):
                for c in range(KC):
                    ahead(START[phase] + c // SLOTS, c % SLOTS)
                    act.wait_ge(evicted[c % SLOTS], START[phase] + c // SLOTS + 2)
                    rms_square(n, c, res[:, c, :])
                rms_finish(n)

            residual_squares("w_out", RMS_FIRST)
            act.wait_ge(rel_copied, 2)
            act.dma_start(rel_scratch, rel_rows[:, None, :].to_broadcast([AH, P, REACH + 1])).then_inc(rel_out, 16)
            act.wait_ge(rel_out, 16)
            band = bass.AP(rel_scratch.tensor, P - 1, [[REACH, P], [P * (REACH + 1), AH], [1, BAND]])
            act.dma_start(bias[:], band).then_inc(bias_in, 16)
            for c in range(KC):
                act.wait_ge(res_ready, c + 1)
                rms_square(RMS_CONV_IN, c, res[:, c, :])
            rms_finish(RMS_CONV_IN)
            x_high(X_CONV_IN, xa_hi)
            with act.Fori(0, KC // 2) as i:
                I = i + START["pw1"]
                for n in range(2):
                    ahead(I, 2 * n)
                    ahead(I, 2 * n + 1)
                    act.wait_ge(evicted[2 * n], I + 1)
                    nc.scalar.activation(sq[:, n, :], full(I, 2 * n + 1), ACT.Sigmoid,
                                         bias=vdyn("b_pw1", i * 2 + (KC + n))).then_inc(evicted[2 * n + 1], 1)
            for c in range(KC):
                act.wait_ge(center_done, c + 1)
                rms_square(RMS_LN, c, conv[:, c, :])
            rms_finish(RMS_LN)
            for c in range(KC):
                act.wait_ge(h_ready, 8 * X_PW2 + c + 1)
                nc.scalar.activation(conv[:, c, :], hbuf[:, c % 4, :], ACT.Silu, bias=vcol("ln_b", c))
                nc.scalar.activation(xa_hi[:, c, :], hbuf[:, c % 4, :], ACT.Silu, bias=vcol("ln_b", c))\
                  .then_inc(xh_ready, 1)
            residual_squares("pw2", RMS_FF0)

            def ffn(layer, n_next):
                for part, n in enumerate(FF_PARTS):
                    f0 = layer * FF_CHUNKS + sum(FF_PARTS[:part])
                    with act.Fori(0, n // 2) as i:
                        I = i + START[f"up{layer}{part}"]
                        for m in range(2):
                            ahead(I, 2 * m)
                            act.wait_ge(evicted[2 * m + 1], I + 1)
                            nc.scalar.activation(sq[:, m, :], full(I, 2 * m), ACT.Silu).then_inc(evicted[2 * m], 1)
                            ahead(I, 2 * m + 1)
                            act.wait_ge(evicted[2 * m + 1], I + 2)
                            nc.scalar.copy(xb_hi[:, bass.ds(i * 2 + m, 1), :], hbuf[:, 2 * m:2 * m + 1, :]).then_inc(ff_hi, 1)
                    if part < len(FF_PARTS) - 1:
                        with act.Fori(0, KC // SLOTS) as i:
                            for j in range(SLOTS):
                                ahead(i + START[f"down{layer}{part}"], j)
                residual_squares(f"down{layer}{len(FF_PARTS) - 1}", n_next)

            x_high(X_FF0, xa_hi)
            ffn(0, RMS_ATTN)
            x_high(X_KV, xa_hi)
            x_high(X_Q, xb_hi)
            I = START["kv"]
            for j in range(2):
                ahead(I, j)
                nc.scalar.copy(kT[:, j, :], full(I, j)).then_inc(evicted[j], 1)
            ahead(I, 2)
            ahead(I, 3)
            for n in range(2):
                nc.scalar.copy(vtok[:, 2 * n:2 * n + 2, :], full(I, 2 + n).rearrange("p (t v) -> p t v", t=2))\
                  .then_inc(evicted[2 + n], 1)

            def attention_out(c):
                for e in range(2):
                    hh = 2 * c + e
                    act.wait_ge(pt_full, hh + 1)
                    nc.scalar.copy(pT[:, e, 0:4, :], aps[:, 2 * e, :].rearrange("p (n t) -> p n t", t=P))
                    nc.scalar.copy(pT[:, e, 4:7, :], aps[:, 2 * e + 1, 0:3 * P].rearrange("p (n t) -> p n t", t=P))\
                      .then_inc(pt_ready, 1)
                act.wait_ge(o_full, c + 1)
                nc.scalar.copy(xa_hi[:, c, :], aps[:, 0, :]).then_inc(o_hi, 1)

            def attention_exp(c):
                for e in range(2):
                    hh = 2 * c + e
                    act.wait_ge(max_ready, hh + 1)
                    for n in range(NT):
                        s = scores[:, e, n, P if n == 0 else 0:BAND]
                        nc.scalar.activation(s, s, ACT.Exp, bias=neg_max[:, e, n:n + 1],
                                             accum_out=row_sum[:, e, n:n + 1])
                    nc.scalar.activation(sink_exp[:, e, :], neg_max[:, e, :], ACT.Exp, bias=sink[:, hh:hh + 1])\
                      .then_inc(exp_ready, 1)

            for c in range(KC + 1):
                if c < KC:
                    I, j = START["q"] + c // SLOTS, c % SLOTS
                    ahead(I, j)
                    nc.scalar.mul(qT[:, c % 2, :], full(I, j), HD ** -0.5).then_inc(evicted[j], 1)
                if c >= 1:
                    attention_out(c - 1)
                if c < KC:
                    attention_exp(c)
            residual_squares("w_o", RMS_FF1)
            x_high(X_FF1, xa_hi)
            ffn(1, RMS_LAST)

        @block.vector
        def _(dve):
            own = Steps(dve, dve_own)
            TT, TS, STT = nc.vector.tensor_tensor, nc.vector.tensor_scalar, nc.vector.scalar_tensor_tensor

            def full(I, j):
                dve.wait_ge(tile_done[j], I + 2)
                return gps[:, j, :]

            for j in range(SLOTS):
                dve.sem_inc(evicted[j], 1)
                dve.sem_inc(taken[j], 1)
            dve.sem_inc(gates_used, 1)
            dve.sem_inc(mixed_ready, 1)
            dve.sem_inc(ff_lo, 2)

            def x_build(b, src, gain, hi, lo, shift=False, through=None):
                dve.wait_ge(rstd_ready, BUILD_OF[b] + 1)

                def h(c):
                    STT(hbuf[:, c % 4, :], src[:, c, :], gain(c), rstd[:], ALU.mult, ALU.mult).then_inc(h_ready, 1)

                if b > 0:
                    dve.wait_ge(x_ready, 8 * b)
                for c in range(3):
                    h(c)
                for c in range(KC):
                    dve.wait_ge(xh_ready, 8 * b + c + 1)
                    high = hi[:, c, :].bitcast(F32)
                    dve.wait_ge(h_ready, 8 * b + c + 1)
                    if through is not None:
                        TT(lo[:, c, :], through[:, c, :], high, ALU.subtract).then_inc(x_ready, 1)
                    elif shift:
                        STT(lo[:, c, :], hbuf[:, c % 4, :], mod[:, c:c + 1], high, ALU.add, ALU.subtract)\
                            .then_inc(x_ready, 1)
                    else:
                        TT(lo[:, c, :], hbuf[:, c % 4, :], high, ALU.subtract).then_inc(x_ready, 1)
                    if c + 3 < KC:
                        if c > 0:
                            dve.wait_ge(x_ready, 8 * b + c)
                        h(c + 3)

            nc.vector.memset(ones[:], 1.0)
            nc.vector.memset(eps_col[:], EPS).then_inc(made, 1)
            own.done(nc.vector.memset(reset[:], 1.0))
            own.done(nc.vector.memset(reset[:, :].rearrange("p (t s) -> p t s", s=P)[:, :, 0:1], 0.0))
            dve.wait_ge(consts_in, CONSTS)
            l0, l1 = (vec[:, VEC[n]:VEC[n] + KC] for n in ("lb0", "lb1"))
            own.done(TT(lbt[:, 2, :], l0, l1, ALU.max))
            TT(lbt[:, 0, :], l0, lbt[:, 2, :], ALU.subtract)
            TT(lbt[:, 1, :], l1, lbt[:, 2, :], ALU.subtract).then_inc(lb_shift, 1)
            dve.wait_ge(c_sig, 1)
            own.done(TT(c_act[:], c_act[:], vec[:, VEC["c"]:VEC["c"] + KC], ALU.mult))
            own.done(nc.vector.tensor_copy(c_pair[:, :, 0], c_act[:]))
            TT(c_pair[:, :, 1], c_act[:], c_pair[:, :, 0].bitcast(F32), ALU.subtract).then_inc(c_ready, 1)
            dve.wait_ge(lb_exp, 1)
            own.done(TT(lbt[:, 0, :], lbt[:, 2, :], lbt[:, 3, :], ALU.add))
            own.done(nc.vector.reciprocal(lbt[:, 1, :], lbt[:, 0, :]))
            own.done(TT(lower[:], lbt[:, 2, :], lbt[:, 1, :], ALU.mult))
            own.done(TS(one_minus[:], lower[:], -1.0, 1.0, ALU.mult, ALU.add))
            with dve.Fori(0, ADA_CHUNKS // SLOTS) as i:
                for j in range(SLOTS):
                    b = full(i, j)
                    TS(mod[:, bass.ds(i * SLOTS + j, 1)], b[:, 0:1], b[:, 1:2], vdyn("b_ada", i * SLOTS + j),
                       ALU.add, ALU.add).then_inc(evicted[j], 1)
            for j in range(SLOTS):
                dve.wait_ge(evicted[j], START["pairs"] + 1)
            own.done(STT(mix_gain[:], mod[:, KC:2 * KC], 1.0, vec[:, VEC["norm_g"]:VEC["norm_g"] + KC], ALU.add, ALU.mult))
            x_build(X_MIX, x0, lambda c: mix_gain[:, c:c + 1], xa_hi, xa_lo, shift=True)
            own.done(nc.vector.memset(at_h[:], 0.0))

            with dve.Fori(0, PAIRS) as p:
                own.enter(p, PAIR_STEPS)

                def at(c):
                    return p * (PAIR_CHUNKS // SLOTS) + (START["pairs"] + c // SLOTS)

                def chunk(c):
                    return full(at(c), c % SLOTS)

                def was_evicted(c):
                    dve.wait_ge(evicted[c % SLOTS], at(c) + 2)

                def bank(u):
                    dve.wait_ge(bank_full[u % 4], p * USES + (u // 4 + 1))
                    return aps[:, u % 4, :]

                def was_taken(u):
                    dve.wait_ge(taken[u % 4], p * USES + (u // 4 + 2))

                def exponents(e):
                    x = cum[:, e, :]
                    for level in range(LEVELS):
                        left, right, mid = halves(x, level)
                        to_left, to_right, _ = halves(kt[:, level, :], level)
                        TT(to_left, mid, left, ALU.subtract)
                        TT(to_right, right, mid, ALU.subtract)
                    tiles = x.rearrange("p (t s) -> p t s", s=P)
                    TT(hbuf[:, 0, :].rearrange("p (t s) -> p t s", s=P),
                       tiles[:, :, P - 1:P].to_broadcast([P, NT, P]), tiles, ALU.subtract).then_inc(exps_ready, 1)

                def decayed(e):
                    dve.wait_ge(decay_ready, p * 2 + (e + 1))
                    qe, ke, grow = q[:, e, :], key[:, e, :], hbuf[:, 1, :]
                    for level in range(LEVELS):
                        _, right, _ = halves(qe, level)
                        _, dec, _ = halves(kt[:, level, :], level)
                        h = (P >> level) // 2
                        last = TT(qt[:, level, :].rearrange("p (n h) -> p n h", h=h), right, dec, ALU.mult)
                    TT(k_far[:, :, :], ke[:, 0:3 * P].rearrange("p (t s) -> p t s", s=P),
                       hbuf[:, 0, 0:3 * P].rearrange("p (t s) -> p t s", s=P), ALU.mult)
                    TT(q_far[:, 0, :], qe[:, P:2 * P], grow[:, P:2 * P], ALU.mult)
                    TT(q_far[:, 3, :], qe[:, 2 * P:3 * P], grow[:, 2 * P:3 * P], ALU.mult)
                    own.done(TT(q_far[:, 5, :], qe[:, 3 * P:], grow[:, 3 * P:], ALU.mult))
                    TS(q_far[:, 1, :], q_far[:, 3, :], grow[:, 2 * P - 1:2 * P], None, ALU.mult)
                    own.done(TS(q_far[:, 4, :], q_far[:, 5, :], grow[:, 3 * P - 1:3 * P], None, ALU.mult))
                    TS(q_far[:, 2, :], q_far[:, 4, :], grow[:, 2 * P - 1:2 * P], None, ALU.mult)
                    TT(kt[:], kt[:], ke[:, None, :].to_broadcast([P, LEVELS, T]), ALU.mult).then_inc(prep_done, 1)

                def near_scores(e):
                    u = U_LV[e]
                    for n, levels in enumerate(LEVEL_BANKS):
                        b = bank(u + n)
                        dve.sem_inc(passed, 1)
                        for m, level in enumerate(levels):
                            h = (P >> level) // 2
                            out = diag(at_h).rearrange("p t (n s) -> p t n s", s=2 * h)[:, :, :, h:]
                            mask = lvl_mask[:, level, :].rearrange("p (n h) -> p n h", h=h)[:, None, :, :]
                            data = b[:, m * T // 2:(m + 1) * T // 2].rearrange("p (t n h) -> p t n h", t=NT, h=h)
                            ins = nc.vector.copy_predicated(out, mask.to_broadcast([P, NT, P // 2 // h, h]), data)
                            if m < len(levels) - 1:
                                own.done(ins)
                                dve.sem_inc(passed, 1)
                            else:
                                ins.then_inc(taken[(u + n) % 4], 1)
                                was_taken(u + n)
                    u += len(LEVEL_BANKS)
                    b = bank(u)
                    dve.sem_inc(passed, 1)
                    nc.vector.copy_predicated(diag(at_h), eye_mask[:, None, :].to_broadcast([P, NT, P]),
                                              b.rearrange("p (t s) -> p t s", s=P)).then_inc(taken[u % 4], 1)

                def causal(e):
                    for j in range(NT):
                        u = U_SC[e] + j
                        n = T - j * P
                        TT(at_r[:, j * (T + P):(j + 1) * T], bank(u)[:, 0:n], tri[:, 0:n], ALU.mult).then_inc(taken[u % 4], 1)

                def normalize(e, r, dst):
                    u = U_AV[e][r]
                    dve.wait_ge(hnorm, p * 4 + (2 * e + r + 1))
                    TT(dst, aps[:, u % 4, :], (lnv, rstd)[r][:], ALU.mult).then_inc(taken[u % 4], 1)
                    was_taken(u)

                def z_gate(c, e, r, gain):
                    dve.wait_ge(gate_sig, p * 4 + (2 * r + e + 1))
                    STT(gates[:, 2 * r + e, :], gps[:, c % SLOTS, :], vdyn(gain, p * 2 + e), sq[:, e, :],
                        ALU.mult, ALU.mult).then_inc(evicted[c % SLOTS], 1)

                def branch_gate(c, e, r):
                    was_evicted(c)
                    was_evicted(c - 2)
                    TT(gates[:, 2 * r + e, :], gates[:, 2 * r + e, :], sq[:, e, :], ALU.mult).then_inc(gates_used, 1)

                for e in range(2):
                    was_evicted(e)
                    own.mark(TS(forget[:, e, :], forget[:, e, :], one_minus[:, bass.ds(p * 2 + e, 1)],
                                lower[:, bass.ds(p * 2 + e, 1)], ALU.mult, ALU.add))
                own.wait()
                own.done(TS(key[:], forget[:], -1.0, 1.0, ALU.mult, ALU.add))
                TS(forget[:], forget[:], TINY, None, ALU.max).then_inc(f_ready, 1)
                for e in range(2):
                    dve.wait_ge(q_sig, p * 2 + (e + 1))
                    TT(q[:, e, :], gps[:, 2 + e, :], sq[:, e, :], ALU.mult).then_inc(evicted[2 + e], 1)
                dve.wait_ge(logf_ready, p + 1)
                for e in range(2):
                    own.mark(nc.vector.tensor_tensor_scan(cum[:, e, :], reset[:], forget[:, e, :], 0.0, ALU.mult, ALU.add))
                own.wait()
                exponents(0)
                for e in range(2):
                    was_evicted(2 + e)
                decayed(0)
                near_scores(0)
                bank(U_LV[0] + 6)
                exponents(1)
                decayed(1)
                dve.wait_ge(tabs_in, p * 16 + 16)
                for n in range(2):
                    was_evicted(6 + n)
                    u = U_ROT + n
                    TT(unit[:, n, :], bank(u), gates[:, 2 * n + 1, :], ALU.mult).then_inc(taken[u % 4], 1)
                    own.done(TT(rqk[:, n, :], rqk[:, n, :], gates[:, 2 * n, :], ALU.mult))
                    was_taken(u)
                    TT(rqk[:, n, :], rqk[:, n, :], unit[:, n, :], ALU.add).then_inc(rot_ready, 1)
                for e in range(2):
                    c = 10 + e
                    b = chunk(c)
                    TS(mod[:, bass.ds(p * 2 + (2 * KC + e), 1)], b[:, 0:1], b[:, 1:2], vdyn("b_ada", p * 2 + (2 * KC + e)),
                       ALU.add, ALU.add).then_inc(evicted[c % SLOTS], 1)
                dve.wait_ge(rot_ready, p * 2 + 2)
                z_gate(12, 0, 0, "hg_norm_g")
                causal(0)
                z_gate(13, 1, 0, "hg_norm_g")
                branch_gate(14, 0, 0)
                branch_gate(15, 1, 0)
                normalize(0, 0, unit[:, 0, :])
                normalize(0, 1, unit[:, 1, :])
                dve.wait_ge(gates_used, p * 4 + 3)
                TT(gates[:, 0, :], gates[:, 0, :], unit[:, 0, :], ALU.mult)
                z_gate(16, 0, 1, "ret_norm_g")
                near_scores(1)
                z_gate(17, 1, 1, "ret_norm_g")
                causal(1)
                branch_gate(18, 0, 1)
                branch_gate(19, 1, 1)
                dve.wait_ge(gates_used, p * 4 + 5)
                own.done(TT(gates[:, 2, :], gates[:, 2, :], unit[:, 1, :], ALU.mult))
                for r in range(2):
                    normalize(1, r, unit[:, r, :])
                    own.done(TT(gates[:, 2 * r + 1, :], gates[:, 2 * r + 1, :], unit[:, r, :], ALU.mult))
                TT(mixed[:, bass.ds(p * 2, 2), :], gates[:, 0:2, :], gates[:, 2:4, :], ALU.add).then_inc(mixed_ready, 1)
                own.leave(PAIRS)

            for c in range(KC):
                dve.wait_ge(m_hi, c + 1)
                dve.wait_ge(mixed_ready, PAIRS + 1)
                TT(xa_lo[:, c, :], mixed[:, c, :], xa_hi[:, c, :].bitcast(F32), ALU.subtract).then_inc(m_lo, 1)
            nc.vector.memset(rel[32:33, :], NEG).then_inc(rel_copied, 1)
            dve.wait_ge(rel_full, 1)
            nc.vector.tensor_copy(rel_rows[:], aps[0:AH, 3, 0:REACH + 1]).then_inc(rel_copied, 1)
            nc.vector.memset(glu[:, :, 0:PAD], 0.0)
            dve.wait_ge(res_in, 16)
            for j in range(2):
                dve.wait_ge(evicted[2 + j], START["w_out"] + 1)

            def residual_add(phase, scale=None, shift=None):
                for c in range(KC):
                    I, j = START[phase] + c // SLOTS, c % SLOTS
                    b = full(I, j)
                    if scale is not None:
                        ins = STT(res[:, c, :], b, scale(c), res[:, c, :], ALU.mult, ALU.add)
                    elif shift is not None:
                        ins = STT(res[:, c, :], b, shift(c), res[:, c, :], ALU.add, ALU.add)
                    else:
                        ins = TT(res[:, c, :], b, res[:, c, :], ALU.add)
                    ins.then_inc(evicted[j], 1)

            residual_add("w_out", scale=lambda c: mod[:, 2 * KC + c:2 * KC + c + 1])
            dve.wait_ge(rstd_ready, RMS_FIRST + 1)
            for c in range(KC):
                STT(res[:, c, :], res[:, c, :], vcol("final_g", c), rstd[:], ALU.mult, ALU.mult).then_inc(res_ready, 1)
            dve.wait_ge(res_ready, KC)
            x_build(X_CONV_IN, res, lambda c: vcol("norm_mix", c), xa_hi, xa_lo)
            with dve.Fori(0, KC // 2) as i:
                own.enter(i, 2 * TAPS)
                I = i + START["pw1"]
                for n in range(2):
                    c = i * 2 + n
                    dve.wait_ge(evicted[2 * n + 1], I + 2)
                    STT(glu[:, bass.ds(c, 1), PAD:], gps[:, 2 * n:2 * n + 1, :], vdyn("b_pw1", c), sq[:, n:n + 1, :],
                        ALU.add, ALU.mult).then_inc(evicted[2 * n], 1)
                for n in range(2):
                    dve.wait_ge(evicted[2 * n], I + 2)
                for k in range(TAPS):
                    for n in range(2):
                        c = i * 2 + n
                        out, src = conv[:, bass.ds(c, 1), :], glu[:, bass.ds(c, 1), k:k + T]
                        w = vdyn("w_dw", c + k * KC)
                        if k == 0:
                            own.mark(TS(out, src, w, vdyn("b_dw", c), ALU.mult, ALU.add))
                            continue
                        own.wait(own.local - 1)
                        ins = STT(out, src, w, out, ALU.mult, ALU.add)
                        own.mark(ins)
                own.leave(KC // 2)
            own.wait()
            nc.vector.tensor_copy(row_max[:, 0, 0:1], conv[:, KC - 1, 0:1]).then_inc(conv_done, 1)
            dve.wait_ge(mean_done, KC)
            for c in range(KC):
                STT(conv[:, c, :], aps[:, 1, :], -1.0 / D, conv[:, c, :], ALU.mult, ALU.add).then_inc(center_done, 1)
            dve.wait_ge(center_done, KC)
            x_build(X_PW2, conv, lambda c: vcol("ln_g", c), xa_hi, xa_lo, through=conv)
            residual_add("pw2", shift=lambda c: vcol("b_pw2", c))

            def ffn(layer):
                for part, n in enumerate(FF_PARTS):
                    f0 = layer * FF_CHUNKS + sum(FF_PARTS[:part])
                    with dve.Fori(0, n // 2) as i:
                        I = i + START[f"up{layer}{part}"]
                        for m in range(2):
                            dve.wait_ge(evicted[2 * m], I + 2)
                            dve.wait_ge(tile_done[2 * m + 1], I + 2)
                            dve.wait_ge(ff_lo, i * 2 + (f0 + m + 1))
                            TT(hbuf[:, 2 * m, :], gps[:, 2 * m + 1, :], sq[:, m, :], ALU.mult).then_inc(evicted[2 * m + 1], 1)
                            dve.wait_ge(ff_hi, i * 2 + (f0 + m + 1))
                            TT(xb_lo[:, bass.ds(i * 2 + m, 1), :], hbuf[:, 2 * m:2 * m + 1, :],
                               xb_hi[:, bass.ds(i * 2 + m, 1), :].bitcast(F32), ALU.subtract).then_inc(ff_lo, 1)
                    if part < len(FF_PARTS) - 1:
                        with dve.Fori(0, KC // SLOTS) as i:
                            for j in range(SLOTS):
                                r = res[:, bass.ds(i * SLOTS + j, 1), :]
                                b = full(i + START[f"down{layer}{part}"], j)
                                TT(r, gps[:, j:j + 1, :], r, ALU.add).then_inc(evicted[j], 1)
                residual_add(f"down{layer}{len(FF_PARTS) - 1}")

            x_build(X_FF0, res, lambda c: vcol("norm_ffn", c), xa_hi, xa_lo)
            ffn(0)
            x_build(X_KV, res, lambda c: vcol("norm_kv", c), xa_hi, xa_lo)
            x_build(X_Q, res, lambda c: vcol("norm_mix", KC + c), xb_hi, xb_lo)
            own.done(nc.vector.memset(scores[:, :, 0, 0:P], NEG))
            dve.wait_ge(bias_in, 16)

            def attention_max(c):
                for e in range(2):
                    hh = 2 * c + e
                    dve.wait_ge(s_full, hh + 1)
                    TT(scores[:, e, 0, P:], aps[:, 2 * e, P:2 * P], bias[:, hh, P:], ALU.add)
                    TT(scores[:, e, 1, :], aps[:, 2 * e, 2 * P:], bias[:, hh, :], ALU.add)
                    TT(scores[:, e, 2:4, :], aps[:, 2 * e + 1, :].rearrange("p (n k) -> p n k", n=2),
                       bias[:, hh:hh + 1, :].to_broadcast([P, 2, BAND]), ALU.add).then_inc(s_taken, 1)
                    dve.wait_ge(s_taken, hh + 1)
                    own.done(nc.vector.tensor_reduce(row_max[:, e, :], scores[:, e, :, :], AX_X, ALU.max))
                    TS(neg_max[:, e, :], row_max[:, e, :], sink[:, hh:hh + 1], -1.0, ALU.max, ALU.mult)\
                        .then_inc(max_ready, 1)

            def attention_probs(c):
                for e in range(2):
                    hh = 2 * c + e
                    dve.wait_ge(exp_ready, hh + 1)
                    own.done(TT(row_max[:, e, :], row_sum[:, e, :], sink_exp[:, e, :], ALU.add))
                    own.done(nc.vector.reciprocal(row_inv[:, e, :], row_max[:, e, :]))
                    TS(scores[:, e, 0, P:], scores[:, e, 0, P:], row_inv[:, e, 0:1], None, ALU.mult)
                    TT(scores[:, e, 1:, :], scores[:, e, 1:, :], row_inv[:, e, 1:, None].to_broadcast([P, 3, BAND]), ALU.mult)\
                        .then_inc(p_ready, 1)

            def attention_low(c):
                dve.wait_ge(o_hi, c + 1)
                TT(xa_lo[:, c, :], aps[:, 0, :], xa_hi[:, c, :].bitcast(F32), ALU.subtract).then_inc(o_lo, 1)

            for c in range(KC + 1):
                if c >= 1:
                    attention_low(c - 1)
                if c < KC:
                    attention_max(c)
                    attention_probs(c)
            residual_add("w_o")
            x_build(X_FF1, res, lambda c: vcol("norm_ffn", KC + c), xa_hi, xa_lo)
            ffn(1)
            dve.wait_ge(rstd_ready, RMS_LAST + 1)
            for c in range(KC):
                STT(y[:, c, :], res[:, c, :], vcol("norm_final", c), rstd[:], ALU.mult, ALU.mult).then_inc(y_ready, 1)

        @block.tensor
        def _(pe):
            mm = nc.tensor.matmul
            for j in range(SLOTS):
                pe.sem_inc(tile_done[j], 1)

            def ready(I, j):
                pe.wait_ge(lo_ready[j], I + 2)
                pe.wait_ge(evicted[j], I + 1)

            def dense(I, j, x, blocks=KC, operand=None):
                ready(I, j)
                for k in range(blocks):
                    if operand is not None:
                        operand(k)
                    w = slice(k * P, (k + 1) * P)
                    mm(gps[:, j, :], w_hi[:, j, w], x[0][:, k, :], start=k == 0, stop=False)
                    mm(gps[:, j, :], w_hi[:, j, w], x[1][:, k, :], start=False, stop=False)
                    last = mm(gps[:, j, :], w_lo[:, j, w], x[0][:, k, :], start=False, stop=k == blocks - 1)
                last.then_inc(tile_done[j], 1)

            def dense_tokens(I, j, x):
                ready(I, j)
                ready(I, j + 1)
                for t in range(NT):
                    tok = slice(t * P, (t + 1) * P)
                    for n0, n1 in (((0, 2),) if t < NT - 1 else ((0, 1), (1, 2))):
                        out = gps[:, j + t // 2, (2 * (t % 2) + n0) * P:(2 * (t % 2) + n1) * P]
                        for k in range(KC):
                            w = slice(k * P, (k + 1) * P)
                            wh, wl = w_hi[:, j + n0:j + n1, w], w_lo[:, j + n0:j + n1, w]
                            mm(out, x[0][:, k, tok], wh, start=k == 0, stop=False)
                            mm(out, x[1][:, k, tok], wh, start=False, stop=False)
                            last = mm(out, x[0][:, k, tok], wl, start=False, stop=k == KC - 1)
                        if t == NT - 1:
                            last.then_inc(tile_done[j + n0], 1)

            def ada(I, j):
                ready(I, j)
                for k in range(KC):
                    w = slice(k * P, (k + 1) * P)
                    mm(gps[:, j, 0:2], w_hi[:, j, w], c_pair[:, k, :], start=k == 0, stop=False)
                    last = mm(gps[:, j, 0:2], w_lo[:, j, w], c_pair[:, k, :], start=False, stop=k == KC - 1)
                last.then_inc(tile_done[j], 1)

            def sum_squares(n, c):
                pe.wait_ge(sq_ready, 8 * n + c + 1)
                mm(aps[:, 0, :], ones[:], sq[:, c % 2, :], start=c == 0, stop=c == KC - 1).then_inc(sum_done, 1)

            def x_wait(b):
                return lambda k: pe.wait_ge(x_ready, 8 * b + k + 1)

            xa, xb = (xa_hi, xa_lo), (xb_hi, xb_lo)
            pe.wait_ge(made, 1)
            for c in range(KC):
                sum_squares(RMS_MIX, c)
            pe.wait_ge(c_ready, 1)
            with pe.Fori(0, ADA_CHUNKS // SLOTS) as i:
                for j in range(SLOTS):
                    ada(i, j)
            pe.wait_ge(consts_in, CONSTS)

            with pe.Fori(0, PAIRS) as p:
                def at(c):
                    return p * (PAIR_CHUNKS // SLOTS) + (START["pairs"] + c // SLOTS)

                def feature(c):
                    dense(at(c), c % SLOTS, xa, operand=x_wait(X_MIX) if c == 0 else None)

                def bank(u):
                    pe.wait_ge(taken[u % 4], p * USES + (u // 4 + 1))
                    return aps[:, u % 4, :]

                def was_taken(u):
                    pe.wait_ge(taken[u % 4], p * USES + (u // 4 + 2))

                def hgrn_scores(e):
                    pe.wait_ge(prep_done, p * 2 + (e + 1))
                    u = U_LV[e]
                    for n, levels in enumerate(LEVEL_BANKS):
                        b = bank(u + n)
                        for m, level in enumerate(levels):
                            for t in range(NT):
                                h = P // 2
                                o = m * T // 2 + t * h
                                last = mm(b[:, o:o + h], kt[:, level, t * P:(t + 1) * P], qt[:, level, t * h:(t + 1) * h],
                                          start=True, stop=True)
                        last.then_inc(bank_full[(u + n) % 4], 1)
                    u += len(LEVEL_BANKS)
                    b = bank(u)
                    for t in range(NT):
                        s = slice(t * P, (t + 1) * P)
                        last = mm(b[:, s], key[:, e, s], q[:, e, s], start=True, stop=True)
                    last.then_inc(bank_full[u % 4], 1)
                    b = bank(u + 1)
                    mm(b[:, 0:3 * P], k_far[:, 0, :], q_far[:, 0:3, :].rearrange("p n t -> p (n t)"), start=True, stop=True)\
                        .then_inc(bank_full[(u + 1) % 4], 1)
                    b = bank(u + 2)
                    mm(b[:, 0:2 * P], k_far[:, 1, :], q_far[:, 3:5, :].rearrange("p n t -> p (n t)"), start=True, stop=True)
                    mm(b[:, 2 * P:3 * P], k_far[:, 2, :], q_far[:, 5, :], start=True, stop=True)\
                        .then_inc(bank_full[(u + 2) % 4], 1)

                def rotate():
                    for n in range(2):
                        u = U_ROT + n
                        pe.wait_ge(evicted[2 + n], at(6 + n) + 2)
                        mm(bank(u), rot[:], rqk[:, n, :], start=True, stop=True).then_inc(bank_full[u % 4], 1)

                def ret_scores(e):
                    pe.wait_ge(rot_ready, p * 2 + 2)
                    rows = slice(e * RET_DK, (e + 1) * RET_DK)
                    for j in range(NT):
                        u = U_SC[e] + j
                        mm(bank(u)[:, 0:T - j * P], rqk[rows, 1, j * P:(j + 1) * P], rqk[rows, 0, j * P:],
                           start=True, stop=True).then_inc(bank_full[u % 4], 1)

                def attend(e, r):
                    if r == 0:
                        for u in range(U_LV[e], U_LV[e] + 7):
                            if u >= U_LV[e] + 3:
                                was_taken(u)
                    else:
                        for j in range(NT):
                            was_taken(U_SC[e] + j)
                    u = U_AV[e][r]
                    b, at_x = bank(u), (at_h, at_r)[r]
                    for n in range(2):
                        c = (4, 8)[r] + n
                        pe.wait_ge(evicted[c % SLOTS], at(c) + 2)
                    for j in range(NT):
                        last = mm(b[:, j * P:], val[:, j, r, e * P:(e + 1) * P], at_x[:, j * (T + P):(j + 1) * T],
                                  start=j == 0, stop=j == NT - 1)
                    last.then_inc(bank_full[u % 4], 1)

                def head_sum(e, r):
                    u = U_NORM[e][r]
                    pe.wait_ge(osq_ready, p * 4 + (2 * e + r + 1))
                    mm(bank(u), ones[:], hbuf[:, 2 + r, :], start=True, stop=True).then_inc(bank_full[u % 4], 1)

                for c in range(4):
                    feature(c)
                dense_tokens(at(4), 0, xa)
                feature(6)
                feature(7)
                hgrn_scores(0)
                dense_tokens(at(8), 0, xa)
                rotate()
                ada(at(10), 2)
                ada(at(11), 3)
                feature(12)
                ret_scores(0)
                attend(0, 0)
                feature(13)
                feature(14)
                attend(0, 1)
                feature(15)
                head_sum(0, 0)
                head_sum(0, 1)
                feature(16)
                hgrn_scores(1)
                feature(17)
                ret_scores(1)
                feature(18)
                attend(1, 0)
                feature(19)
                attend(1, 1)
                head_sum(1, 0)
                head_sum(1, 1)

            pe.wait_ge(hot_in_sem, 32)
            pe.wait_ge(rel_copied, 1)
            mm(aps[0:AH, 3, 0:REACH + 1], rel[:], hot[:], start=True, stop=True).then_inc(rel_full, 1)

            def residual(phase, x, n, blocks=KC, operand=None):
                for c in range(KC):
                    dense(START[phase] + c // SLOTS, c % SLOTS, x, blocks, operand if c == 0 else None)
                    if c >= 1:
                        sum_squares(n, c - 1)
                sum_squares(n, KC - 1)

            residual("w_out", xa, RMS_FIRST, operand=lambda k: pe.wait_ge(m_lo, k + 1))
            for c in range(KC):
                sum_squares(RMS_CONV_IN, c)
            with pe.Fori(0, KC // 2) as i:
                for j in range(SLOTS):
                    dense(i + START["pw1"], j, xa, operand=x_wait(X_CONV_IN) if j == 0 else None)
            pe.wait_ge(conv_done, 1)
            for c in range(KC):
                mm(aps[:, 1, :], ones[:], conv[:, c, :], start=c == 0, stop=c == KC - 1).then_inc(mean_done, 1)
            for c in range(KC):
                sum_squares(RMS_LN, c)
            residual("pw2", xa, RMS_FF0, operand=x_wait(X_PW2))

            def ffn(layer, b, n_next):
                for part, n in enumerate(FF_PARTS):
                    f0 = layer * FF_CHUNKS + sum(FF_PARTS[:part])
                    with pe.Fori(0, n // 2) as i:
                        for j in range(SLOTS):
                            dense(i + START[f"up{layer}{part}"], j, xa, operand=x_wait(b) if j == 0 else None)
                    hidden = lambda k: pe.wait_ge(ff_lo, f0 + k + 3)
                    down = f"down{layer}{part}"
                    if part < len(FF_PARTS) - 1:
                        with pe.Fori(0, KC // SLOTS) as i:
                            for j in range(SLOTS):
                                dense(i + START[down], j, xb, n, hidden if j == 0 else None)
                    else:
                        residual(down, xb, n_next, n, hidden)

            ffn(0, X_FF0, RMS_ATTN)
            I = START["kv"]
            for j in range(2):
                dense(I, j, xa, operand=x_wait(X_KV) if j == 0 else None)
            dense_tokens(I, 2, xa)

            def band_scores(c):
                for e in range(2):
                    hh = 2 * c + e
                    rows = slice(e * HD, (e + 1) * HD)
                    if e == 0:
                        pe.wait_ge(evicted[c % SLOTS], START["q"] + c // SLOTS + 2)
                        if c >= 1:
                            pe.wait_ge(o_lo, c)
                    if hh >= 2:
                        pe.wait_ge(pt_ready, hh - 1)
                    for n in range(NT):
                        k0 = max(n - 1, 0) * P
                        o = (n % 2) * BAND + (P if n == 0 else 0)
                        last = mm(aps[:, 2 * e + n // 2, o:(n % 2 + 1) * BAND], qT[rows, c % 2, n * P:(n + 1) * P],
                                  kT[rows, c // 4, k0:(n + 1) * P], start=True, stop=True)
                    last.then_inc(s_full, 1)

            def band_values(c):
                for e in range(2):
                    hh = 2 * c + e
                    pe.wait_ge(p_ready, hh + 1)
                    for x in range(2 * NT - 1):
                        n, half = (x + 1) // 2, (x + 1) % 2
                        last = nc.tensor.transpose(aps[:, 2 * e + x // 4, (x % 4) * P:(x % 4 + 1) * P],
                                                   scores[:, e, n, half * P:(half + 1) * P], ident[:])
                    last.then_inc(pt_full, 1)
                pe.wait_ge(pt_ready, 2 * c + 2)
                for e in range(2):
                    g = 2 * (c // 4) + e
                    for n in range(NT):
                        tiles = [(n, 0)] if n == 0 else [(n - 1, 2 * n - 1), (n, 2 * n)]
                        for m, (kb, x) in enumerate(tiles):
                            last = mm(aps[e * HD:(e + 1) * HD, 0, n * P:(n + 1) * P], vtok[:, kb, g * HD:(g + 1) * HD],
                                      pT[:, e, x, :], start=m == 0, stop=m == len(tiles) - 1)
                last.then_inc(o_full, 1)

            for c in range(KC + 1):
                if c < KC:
                    dense(START["q"] + c // SLOTS, c % SLOTS, xb, operand=x_wait(X_Q) if c == 0 else None)
                if c >= 1:
                    band_values(c - 1)
                if c < KC:
                    band_scores(c)
            residual("w_o", xa, RMS_FF1, operand=lambda k: pe.wait_ge(o_lo, k + 1))
            ffn(1, X_FF1, RMS_LAST)



def chunk(w):
    blocks = w.shape[0] // P
    out = np.zeros((P, KC * P), np.float32)
    out[:, :blocks * P] = w.reshape(blocks, P, P).transpose(1, 0, 2).reshape(P, blocks * P)
    return out


def head_order():
    group = AH // KVH
    return [(2 * (c // group) + e) * group + c % group for c in range(KC) for e in range(2)]


def weight_stream(w_ada, w_in, w_out, pw1, pw2, w_kv, w_q, w_o, up, down):
    def cols(w, c):
        return w[:, c * P:(c + 1) * P]

    def tokens(w, c):
        return [cols(w, c), cols(w, c + 1)]

    out = [cols(w_ada, c) for c in range(ADA_CHUNKS)]
    hq, hf, hi, hz = 0, KC, 2 * KC, 3 * KC
    rq, rk = 4 * KC, 4 * KC + KC // 2
    rv, rz, ga, gb = (5 * KC + n * KC for n in range(4))
    for p in range(PAIRS):
        a, b = 2 * p, 2 * p + 1
        out += [cols(w_in, hf + a), cols(w_in, hf + b), cols(w_in, hq + a), cols(w_in, hq + b)]
        out += tokens(w_in, hi + a) + [cols(w_in, rq + p), cols(w_in, rk + p)] + tokens(w_in, rv + a)
        out += [cols(w_ada, 2 * KC + a), cols(w_ada, 2 * KC + b)]
        for z, g in ((hz, ga), (rz, gb)):
            out += [cols(w_in, z + a), cols(w_in, z + b), cols(w_in, g + a), cols(w_in, g + b)]
    out += [cols(w_out, c) for c in range(KC)]
    for c in range(KC):
        out += [cols(pw1, c), cols(pw1, KC + c)]
    out += [cols(pw2, c) for c in range(KC)]
    heads = head_order()
    for layer in range(2):
        if layer == 1:
            out += [cols(w_kv, c) for c in range(4)]
            wq = w_q.reshape(D, AH, HD)[:, heads].reshape(D, D)
            wo = w_o.reshape(AH, HD, D)[heads].reshape(D, D)
            out += [cols(wq, c) for c in range(KC)] + [cols(wo, c) for c in range(KC)]
        f = 0
        for n in FF_PARTS:
            for c in range(f, f + n):
                out += [cols(up[layer], c), cols(up[layer], FF_CHUNKS + c)]
            out += [cols(down[layer][f * P:(f + n) * P], c) for c in range(KC)]
            f += n
    assert len(out) == QUADS * SLOTS
    return np.stack([chunk(w) for w in out])


def shape_constants():
    lin = np.linspace(0.0, 1.0, RET_DK // 2, dtype=np.float32)
    inv = (np.float32(1.0) / np.power(np.float32(10000.0), lin)).astype(np.float32)
    ang = (np.arange(T, dtype=np.float32)[:, None] * inv[None, :]).astype(np.float32)
    cos, sin = (np.tile(f(ang.astype(np.float64)).T, (2, 1)) for f in (np.cos, np.sin))
    tab = np.zeros((PAIRS, P, 4, T))
    t = np.arange(T)
    for h in range(HEADS):
        rows = slice((h % 2) * RET_DK, (h % 2 + 1) * RET_DK)
        gamma = 1.0 - 2.0 ** (-5.0 - h)
        tab[h // 2, rows, 0], tab[h // 2, rows, 1] = cos * gamma ** t, sin * gamma ** t
        back = gamma ** (-t) * RET_DK ** -0.5
        tab[h // 2, rows, 2], tab[h // 2, rows, 3] = cos * back, sin * back
    rot = np.zeros((P, P), np.float32)
    half = RET_DK // 2
    for o in (0, RET_DK):
        for i in range(half):
            rot[o + half + i, o + i] = -1.0
            rot[o + i, o + half + i] = 1.0
    lvl = np.zeros((P, LEVELS, P // 2), np.int32)
    for level in range(LEVELS):
        size = P >> level
        right = [t for t in range(P) if t % size >= size // 2]
        for x, t_ in enumerate(right):
            for s in range(t_ // size * size, t_ // size * size + size // 2):
                lvl[s, level, x] = 1
    tri = (np.arange(T)[None, :] >= np.arange(P)[:, None]).astype(np.float32)
    hot = np.zeros((33, REACH + 1), np.float32)
    exact = 16
    for u in range(REACH + 1):
        d = BAND - 1 - u
        if not 0 <= d < P:
            hot[32, u] = 1.0
            continue
        log = np.float32(np.log(np.float32(max(d, 1)) / np.float32(exact))) / np.float32(np.log(P / exact))
        large = min(exact + int(np.float32(log * np.float32(32 - exact))), 31)
        hot[d if d < exact else large, u] = 1.0
    return {"rot": rot, "ret_tab": tab.astype(np.float32), "lvl": lvl.reshape(P, -1), "eye": np.eye(P, dtype=np.int32),
            "tri": tri, "hot": hot, "ident": np.eye(P, dtype=np.float32)}


def kernel(**inputs):
    import concourse.bacc as bacc
    from concourse.bass_utils import run_bass_kernel_spmd

    a = {k: np.asarray(v) for k, v in inputs.items()}
    columns = {
        "norm_g": a["norm_g"], "b_ada": a["b_ada"], "lb0": a["hg_lb_logits"][0], "lb1": a["hg_lb_logits"][1],
        "hg_norm_g": a["hg_norm_g"], "ret_norm_g": a["ret_norm_g"], "norm_mix": a["norm_mix_2"],
        "norm_ffn": a["norm_ffn_2"], "b_pw1": a["conv_b_pw1_2"], "w_dw": a["conv_w_dw_2"], "b_dw": a["conv_b_dw_2"],
        "ln_g": a["conv_ln_g_2"], "ln_b": a["conv_ln_b_2"], "b_pw2": a["conv_b_pw2_2"], "norm_kv": a["norm_kv_2"],
        "norm_final": a["norm_final_2"], "final_g": a["final_g"], "c": a["c"],
    }
    heads = head_order()
    arrays = {
        "weights": weight_stream(a["w_ada"][0], a["w_in"][0], a["w_out"][0], a["conv_w_pw1_2"][0], a["conv_w_pw2_2"][0],
                                 a["w_kv_2"], a["w_q_2"][0], a["w_o_2"][0], a["ffn_w_up_2"], a["ffn_w_down_2"]),
        "xT": np.ascontiguousarray(a["x"][0].T),
        "vec_in": np.ascontiguousarray(np.concatenate([columns[n].reshape(-1) for n in VEC]).reshape(VECS, P).T),
        "sinks_in": np.ascontiguousarray(a["sinks_2"].reshape(1, AH)[:, heads]),
        "rel_in": np.ascontiguousarray(a["rel_bias_2"][:, heads]),
    }
    arrays |= {f"{k}_in" if k != "ret_tab" else k: v for k, v in shape_constants().items()}
    nc = bacc.Bacc("TRN2", target_bir_lowering=False, num_devices=1)
    aps = {k: nc.dram_tensor(f"{k}_dram", v.shape, mybir.dt.from_np(v.dtype), kind="ExternalInput").ap()
           for k, v in arrays.items()}
    scratch = nc.dram_tensor("rel_scratch_dram", (AH, P, REACH + 1), F32, kind="Internal").ap()
    outT = nc.dram_tensor("outT_dram", (D, T), F32, kind="ExternalOutput").ap()
    program(nc, rel_scratch=scratch, outT=outT, **aps)
    r = run_bass_kernel_spmd(nc, [{f"{k}_dram": v for k, v in arrays.items()}], core_ids=[0])
    return np.ascontiguousarray(np.asarray(r.results[0]["outT_dram"]).T)[None]
```

```python
from contextlib import ExitStack

import numpy as np
import concourse.bass as bass
from concourse import mybir

F32 = mybir.dt.float32
F32R = mybir.dt.float32r
I32 = mybir.dt.int32
ACT = mybir.ActivationFunctionType
ALU = mybir.AluOpType
AX_X = mybir.AxisListType.X

P = 128
T = 512
D = 1024
KC = D // P
NT = T // P
SLOTS = 4
EPS = 1e-6

HEADS = 8
PAIRS = HEADS // 2
LEVELS = 7
TINY = 1e-19
RET_DK = 64

TAPS = 31
PAD = TAPS - 1
FF_CHUNKS = 22
FF_PARTS = (8, 8, 6)
AH = 16
KVH = 4
HD = 64
BAND = 256
REACH = 383
NEG = -1e30

ADA_CHUNKS = 2 * KC
ADA_LOAD = 2
DVE_CONV = 5
GLU_LOOP = DVE_CONV // 2
PE_CONV = KC - DVE_CONV
TAP_GROUP = 8
TAP_GROUPS = -(-TAPS // TAP_GROUP)

PAIR_CHUNKS = 20


def phase_starts():
    sizes = [("pairs", PAIRS * PAIR_CHUNKS), ("w_out", KC), ("pw1", 2 * KC), ("pw2", KC)]
    for layer in range(2):
        if layer == 1:
            sizes += [("kv", 4), ("q", KC), ("w_o", KC)]
        for part, n in enumerate(FF_PARTS):
            sizes += [(f"up{layer}{part}", 2 * n), (f"down{layer}{part}", KC)]
    at, starts = 0, {}
    for name, n in sizes:
        assert n % SLOTS == 0
        starts[name] = at
        at += n // SLOTS
    return starts, at


START, QUADS = phase_starts()

VEC = {}
_at = 0
for _name, _n in (("norm_g", KC), ("b_ada", 3 * KC), ("lb0", KC), ("lb1", KC), ("hg_norm_g", KC),
                  ("ret_norm_g", KC), ("norm_mix", 2 * KC), ("norm_ffn", 2 * KC), ("b_pw1", 2 * KC),
                  ("w_dw", TAPS * KC), ("b_dw", KC), ("ln_g", KC), ("ln_b", KC), ("b_pw2", KC),
                  ("norm_kv", KC), ("norm_final", KC), ("final_g", KC), ("c", KC)):
    VEC[_name] = _at
    _at += _n
VECS = _at
CONSTS = 16 * 6
LN = "natural_log"
PAIR_STEPS = 21


class Steps:

    def __init__(self, eng, sem):
        self.eng, self.sem = eng, sem
        self.base, self.local, self.i, self.per = 0, 0, None, 0

    def enter(self, i, per):
        self.base, self.local, self.i, self.per = self.base + self.local, 0, i, per

    def leave(self, trips):
        assert self.local == self.per, (self.local, self.per)
        self.base, self.local, self.i, self.per = self.base + trips * self.per, 0, None, 0

    def mark(self, ins):
        ins.then_inc(self.sem, 1)
        self.local += 1
        return self.local

    def wait(self, local=None):
        v = self.base + (self.local if local is None else local)
        self.eng.wait_ge(self.sem, v if self.i is None else self.i * self.per + v)

    def done(self, ins):
        self.mark(ins)
        self.wait()


def program(nc, weights, ada_in, c_in, xT, vec_in, sinks_in, rel_in, rot_in, ret_tab, lvl_in, eye_in, tri_in, hot_in, ident_in,
            rel_scratch, outT):
    ctx = ExitStack()
    with ctx:
        def sb(name, shape, dt=F32, where=ctx):
            return where.enter_context(nc.sbuf_tensor(name, shape, dt))

        def sem(name):
            return ctx.enter_context(nc.semaphore(name))

        w_raw = sb("w_raw", [P, SLOTS, D])
        w_hi = sb("w_hi", [P, SLOTS, D], F32R)
        w_lo = sb("w_lo", [P, SLOTS, D], F32R)
        xa_mem = ExitStack()
        diag_hi = sb("diag_hi", [P, TAP_GROUPS * TAP_GROUP, P], F32R, where=xa_mem)
        low_mem = ExitStack()
        diag_lo = sb("diag_lo", [P, TAP_GROUPS * TAP_GROUP, P], F32R, where=low_mem)
        low_mem.close()
        x0 = sb("x0", [P, KC, T], where=xa_mem)
        xa_mem.close()
        xa_hi = sb("xa_hi", [P, KC, T], F32R)
        xa_lo = sb("xa_lo", [P, KC, T], F32R)
        vec = sb("vec", [P, VECS])
        ones = sb("ones", [P, P])
        ident = sb("ident", [P, P])
        eps_col = sb("eps_col", [P, 1])
        mod = sb("mod", [P, 3 * KC])
        conv_gain = sb("conv_gain", [P, KC])
        r_col = sb("r_col", [P, 2, NT])
        sq = sb("sq", [P, 2, T])
        lnv = sb("lnv", [P, T])
        rstd = sb("rstd", [P, T])
        hbuf = sb("hbuf", [P, 4, T])
        sink = sb("sink", [P, AH])
        neg_max = sb("neg_max", [P, 2, NT])
        row_max = sb("row_max", [P, 2, NT])
        row_sum = sb("row_sum", [P, 2, NT])
        row_inv = sb("row_inv", [P, 2, NT])
        sink_exp = sb("sink_exp", [P, 2, NT])

        first = ExitStack()
        reset = sb("reset", [P, T], where=first)
        tri = sb("tri", [P, T], where=first)
        rot = sb("rot", [P, P], where=first)
        lvl_mask = sb("lvl_mask", [P, LEVELS, P // 2], I32, where=first)
        eye_mask = sb("eye_mask", [P, P], I32, where=first)
        lower = sb("lower", [P, KC], where=first)
        one_minus = sb("one_minus", [P, KC], where=first)
        mix_gain = sb("mix_gain", [P, KC], where=first)
        lbt = sb("lbt", [P, 4, KC], where=first)
        c_act = sb("c_act", [P, KC], where=first)
        c_pair = sb("c_pair", [P, KC, 2], F32R, where=first)
        ada_mem = ExitStack()
        ada_w = sb("ada_w", [P, ADA_CHUNKS, D], where=ada_mem)
        c_wide = sb("c_wide", [P, 2, D], where=ada_mem)
        ada_mem.close()
        mixed = sb("mixed", [P, KC, T], where=first)
        kt = sb("kt", [P, LEVELS, T], where=first)
        qt = sb("qt", [P, LEVELS, T // 2], where=first)
        q = sb("q", [P, 2, T], where=first)
        key = sb("key", [P, 2, T], where=first)
        cum = sb("cum", [P, 2, T], where=first)
        forget = sb("forget", [P, 2, T], where=first)
        q_far = sb("q_far", [P, 6, P], where=first)
        k_far = sb("k_far", [P, 3, P], where=first)
        val = sb("val", [P, NT, 2, 2 * P], where=first)
        rqk = sb("rqk", [P, 2, T], where=first)
        gates = sb("gates", [P, 4, T], where=first)
        unit = sb("unit", [P, 2, T], where=first)
        at_h = sb("at_h", [P, NT * (T + P)], where=first)
        at_r = sb("at_r", [P, NT * (T + P)], where=first)
        first.close()

        second = ExitStack()
        xb_hi = sb("xb_hi", [P, KC, T], F32R, where=second)
        xb_lo = sb("xb_lo", [P, KC, T], F32R, where=second)
        res = sb("res", [P, KC, T], where=second)
        bias = sb("bias", [P, AH, BAND], where=second)
        conv_mem = ExitStack()
        glu = sb("glu", [P, KC, PAD + T], where=conv_mem)
        early_mem = ExitStack()
        hot = sb("hot", [33, REACH + 1], where=early_mem)
        rel = sb("rel", [33, AH], where=early_mem)
        rel_rows = sb("rel_rows", [AH, REACH + 1], where=early_mem)
        early_mem.close()
        glu_hi = sb("glu_hi", [P, 2, PAD + T], F32R, where=conv_mem)
        glu_lo = sb("glu_lo", [P, 2, PAD + T], F32R, where=conv_mem)
        tap_hi = sb("tap_hi", [P, TAP_GROUPS * TAP_GROUP, PE_CONV], F32R, where=conv_mem)
        tap_lo = sb("tap_lo", [P, TAP_GROUPS * TAP_GROUP, PE_CONV], F32R, where=conv_mem)
        conv = sb("conv", [P, KC, T], where=conv_mem)
        conv_mem.close()
        attn_mem = ExitStack()
        kT = sb("kT", [P, 2, T], where=attn_mem)
        vtok = sb("vtok", [P, NT, KVH * HD], where=attn_mem)
        qT = sb("qT", [P, 2, T], where=attn_mem)
        scores = sb("scores", [P, 2, NT, BAND], where=attn_mem)
        pT = sb("pT", [P, 2, 2 * NT - 1, P], where=attn_mem)
        attn_mem.close()
        end_mem = ExitStack()
        y = sb("y", [P, KC, T], where=end_mem)
        end_mem.close()
        second.close()

        gps = ctx.enter_context(nc.psum_tensor("gps", [P, SLOTS, T], F32))
        aps = ctx.enter_context(nc.psum_tensor("aps", [P, 4, T], F32))

        raw_in = [sem(f"raw_in{j}") for j in range(SLOTS)]
        hi_ready = [sem(f"hi_ready{j}") for j in range(SLOTS)]
        lo_ready = [sem(f"lo_ready{j}") for j in range(SLOTS)]
        tile_done = [sem(f"tile_done{j}") for j in range(SLOTS)]
        evicted = [sem(f"evicted{j}") for j in range(SLOTS)]
        bank_full = [sem(f"bank_full{b}") for b in range(4)]
        taken = [sem(f"taken{b}") for b in range(4)]
        act_own = sem("act_own")
        dve_own = sem("dve_own")
        consts_in = sem("consts_in")
        vec_loaded = sem("vec_loaded")
        c_loaded = sem("c_loaded")
        ada_loaded = [sem(f"ada_loaded{n}") for n in range(ADA_CHUNKS // ADA_LOAD)]
        c_wide_ready = sem("c_wide_ready")
        x_in = sem("x_in")
        tabs_in = sem("tabs_in")
        res_in = sem("res_in")
        hot_in_sem = sem("hot_in_sem")
        made = sem("made")
        c_sig = sem("c_sig")
        c_ready = sem("c_ready")
        lb_shift = sem("lb_shift")
        lb_exp = sem("lb_exp")
        mod_ready = sem("mod_ready")
        sq_ready = sem("sq_ready")
        sq_used = sem("sq_used")
        double_ready = sem("double_ready")
        second_ready = sem("second_ready")
        both_ready = sem("both_ready")
        sum_done = sem("sum_done")
        rstd_ready = sem("rstd_ready")
        h_ready = sem("h_ready")
        xh_ready = sem("xh_ready")
        x_ready = sem("x_ready")
        f_ready = sem("f_ready")
        logf_ready = sem("logf_ready")
        q_sig = sem("q_sig")
        exps_ready = sem("exps_ready")
        decay_ready = sem("decay_ready")
        prep_done = sem("prep_done")
        rot_ready = sem("rot_ready")
        passed = sem("passed")
        osq_ready = sem("osq_ready")
        hnorm = sem("hnorm")
        gate_sig = sem("gate_sig")
        gates_used = sem("gates_used")
        mixed_ready = sem("mixed_ready")
        m_hi = sem("m_hi")
        m_lo = sem("m_lo")
        rel_full = sem("rel_full")
        rel_copied = sem("rel_copied")
        rel_out = sem("rel_out")
        bias_in = sem("bias_in")
        res_ready = sem("res_ready")
        scaled = sem("scaled")
        sig_ready = sem("sig_ready")
        glu_ready = sem("glu_ready")
        glu_high = sem("glu_high")
        glu_low = sem("glu_low")
        taps_high = sem("taps_high")
        taps_ready = sem("taps_ready")
        diag_ready = sem("diag_ready")
        diag_used = sem("diag_used")
        conv_full = sem("conv_full")
        conv_copied = sem("conv_copied")
        conv_done = sem("conv_done")
        conv_sum = sem("conv_sum")
        mean_done = sem("mean_done")
        center_done = sem("center_done")
        s_full = sem("s_full")
        s_taken = sem("s_taken")
        max_ready = sem("max_ready")
        exp_ready = sem("exp_ready")
        p_ready = sem("p_ready")
        pt_full = sem("pt_full")
        pt_ready = sem("pt_ready")
        o_full = sem("o_full")
        o_hi = sem("o_hi")
        o_lo = sem("o_lo")
        silu_ready = sem("silu_ready")
        ff_ready = sem("ff_ready")
        ff_hi = sem("ff_hi")
        ff_lo = sem("ff_lo")
        y_ready = sem("y_ready")
        out_done = sem("out_done")

        def vcol(name, c=0):
            return vec[:, VEC[name] + c:VEC[name] + c + 1]

        def vdyn(name, c):
            return vec[:, bass.ds(c + VEC[name], 1)]

        def diag(at):
            return at[:, :].rearrange("p (t s) -> p t s", s=T + P)[:, :, 0:P]

        def halves(ap, level):
            size = P >> level
            v = ap.rearrange("p (n s) -> p n s", s=size)
            h = size // 2
            return v[:, :, 0:h], v[:, :, h:size], v[:, :, h - 1:h].to_broadcast([P, T // size, h])

        FAR = ((0, 0, 3), (1, 3, 5), (2, 5, 6))
        LEVEL_BANKS = ((0, 1), (2, 3), (4, 5), (6,))
        RMS_MIX, RMS_FIRST, RMS_LN, RMS_FF0, RMS_ATTN, RMS_FF1, RMS_LAST = range(7)
        SUMS = {}
        USED = {}
        for n in range(7):
            SUMS[n] = SUMS.get(n - 1, 0) + (KC if n in (RMS_MIX, RMS_LN) else 1)
            USED[n] = USED.get(n - 1, 0) + (KC - 2 if n - 1 in (RMS_FIRST, RMS_FF0, RMS_ATTN, RMS_FF1) else 0)
        X_MIX, X_CONV_IN, X_PW2, X_FF0, X_KV, X_Q, X_FF1 = range(7)
        H_BUILDS = {X_MIX: (RMS_MIX, 0), X_PW2: (RMS_LN, 1)}
        U_LV = (0, 17)
        U_ROT = 7
        U_SC = (9, 24)
        U_AV = ((13, 14), (28, 29))
        U_NORM = ((15, 16), (30, 31))
        USES = 8

        block = ctx.enter_context(nc.Block())

        @block.sync
        def _(sp):
            for n in range(ADA_CHUNKS // ADA_LOAD):
                c = slice(n * ADA_LOAD, (n + 1) * ADA_LOAD)
                sp.dma_start(ada_w[:, c, :], ada_in[c].rearrange("c p k -> p c k")).then_inc(ada_loaded[n], 16)
            with sp.Fori(0, QUADS) as i:
                for j in range(SLOTS):
                    sp.wait_ge(lo_ready[j], i + 1)
                    sp.dma_start(w_raw[:, j, :], weights[bass.ds(i * SLOTS + j, 1)].rearrange("a p c -> p (a c)"))\
                      .then_inc(raw_in[j], 16)
            for c in range(KC):
                sp.wait_ge(y_ready, c + 1)
                sp.dma_start(outT[c * P:(c + 1) * P, :], y[:, c, :]).then_inc(out_done, 16)
            sp.wait_ge(out_done, 16 * KC)

        @block.gpsimd
        def _(pool):
            TT = nc.gpsimd.tensor_tensor
            for j in range(SLOTS):
                pool.sem_inc(lo_ready[j], 1)

            def w_low(I, j):
                pool.wait_ge(hi_ready[j], I + 1)
                TT(w_lo[:, j, :], w_raw[:, j, :], w_hi[:, j, :].bitcast(F32), ALU.subtract).then_inc(lo_ready[j], 1)

            with pool.Fori(0, START["pw1"]) as i:
                for j in range(SLOTS):
                    w_low(i, j)
            for j in range(3):
                w_low(START["pw1"], j)

            def scale(I, n, c):
                at = bass.ds(c, 1)
                pool.wait_ge(evicted[2 * n + 1], I + 2)
                pool.sem_inc(passed, 1)
                TT(glu[:, at, PAD:], glu[:, at, PAD:], lnv[:, None, :], ALU.mult)
                TT(conv[:, at, :], conv[:, at, :], lnv[:, None, :], ALU.mult).then_inc(scaled, 1)

            def diagonals(g, m):
                k = slice(g * TAP_GROUP, (g + 1) * TAP_GROUP) if isinstance(g, int) else bass.ds(g * TAP_GROUP, TAP_GROUP)
                shape = [P, TAP_GROUP, P]
                for diag, tap in ((diag_hi, tap_hi), (diag_lo, tap_lo)):
                    last = TT(diag[:, k, :], ident[:, None, :].to_broadcast(shape),
                              tap[:, k, m:m + 1].bitcast(F32).to_broadcast(shape), ALU.mult)
                last.then_inc(diag_ready, 1)

            pool.wait_ge(both_ready, 1)
            pool.wait_ge(taps_ready, 1)
            with pool.Fori(0, GLU_LOOP) as i:
                I = i + START["pw1"]
                w_low(I, 3)
                w_low(I + 1, 0)
                scale(I, 0, i * 2)
                w_low(I + 1, 1)
                w_low(I + 1, 2)
                scale(I, 1, i * 2 + 1)
                diagonals(i, 0)
            I = START["pw1"] + GLU_LOOP

            def product(m):
                c = DVE_CONV + m
                pool.wait_ge(sig_ready, c + 1)
                TT(glu[:, c, PAD:], glu[:, c, PAD:], conv[:, c, :], ALU.mult).then_inc(glu_ready, 1)

            def low(m):
                pool.wait_ge(glu_high, m + 1)
                TT(glu_lo[:, m % 2, :], glu[:, DVE_CONV + m, :], glu_hi[:, m % 2, :].bitcast(F32), ALU.subtract)\
                    .then_inc(glu_low, 1)

            w_low(I, 3)
            w_low(I + 1, 0)
            scale(I, 0, DVE_CONV - 1)
            w_low(I + 1, 1)
            w_low(I + 1, 2)
            scale(I, 1, DVE_CONV)
            product(0)
            w_low(I + 1, 3)
            w_low(I + 2, 0)
            scale(I + 1, 0, DVE_CONV + 1)
            low(0)
            product(1)
            diagonals(GLU_LOOP, 0)
            w_low(I + 2, 1)
            w_low(I + 2, 2)
            scale(I + 1, 1, DVE_CONV + 2)
            low(1)
            product(2)
            for g in range(GLU_LOOP + 1, TAP_GROUPS):
                diagonals(g, 0)
            for m in range(1, PE_CONV):
                for g in range(TAP_GROUPS):
                    if g < TAP_GROUPS - 1:
                        pool.wait_ge(diag_used, (m - 1) * (TAP_GROUPS - 1) + g + 1)
                    else:
                        pool.wait_ge(conv_full, m)
                    diagonals(g, m)
                if m == 1:
                    low(PE_CONV - 1)
            total = hbuf[:, 3, :]
            pool.wait_ge(conv_done, 1 + GLU_LOOP)
            for n, c in enumerate((1, 2, 3, 4, DVE_CONV)):
                if c == DVE_CONV:
                    pool.wait_ge(conv_copied, 1)
                if n > 0:
                    pool.wait_ge(conv_sum, n)
                TT(total, conv[:, 0, :] if n == 0 else total, conv[:, c, :], ALU.add).then_inc(conv_sum, 1)
            w_low(START["pw2"], 3)
            with pool.Fori(START["pw2"] + 1, QUADS) as i:
                for j in range(SLOTS):
                    w_low(i, j)

        @block.scalar
        def _(act):
            own = Steps(act, act_own)

            def w_high(I, j):
                act.wait_ge(raw_in[j], I * 16 + 16)
                act.wait_ge(tile_done[j], I + 1)
                nc.scalar.copy(w_hi[:, j, :], w_raw[:, j, :]).then_inc(hi_ready[j], 1)

            def ahead(I, j):
                if not isinstance(I, int) or I * SLOTS + j + 3 < QUADS * SLOTS:
                    w_high(I + (j + 3) // SLOTS, (j + 3) % SLOTS)

            def full(I, j):
                act.wait_ge(tile_done[j], I + 2)
                return gps[:, j, :]

            def tables():
                nc.scalar.preload_act_table_set(LN)

            def rms_square(n, c, src):
                if c >= 2:
                    act.wait_ge(sum_done, SUMS[n] - KC + c - 1)
                nc.scalar.activation(sq[:, c % 2, :], src, ACT.Square).then_inc(sq_ready, 1)

            def rms_finish(n):
                act.wait_ge(sum_done, SUMS[n])
                own.done(nc.scalar.activation(lnv[:], aps[:, 0, :], ACT.Ln, bias=eps_col[:], scale=1.0 / D))
                nc.scalar.activation(rstd[:], lnv[:], ACT.Exp, scale=-0.5).then_inc(rstd_ready, 1)

            def gain_high(dst, c, gain):
                nc.scalar.mul(dst[:, c, :], res[:, c, :], gain(c)).then_inc(xh_ready, 1)

            act.dma_start(vec[:], vec_in).then_inc(vec_loaded, 16)
            act.dma_start(c_wide[:, 0, :], c_in.to_broadcast([P, D])).then_inc(c_loaded, 16)
            act.dma_start(x0[:], xT.rearrange("(k p) t -> p k t", p=P)).then_inc(x_in, 16)
            act.dma_start(lvl_mask[:], lvl_in.rearrange("p (l c) -> p l c", l=LEVELS)).then_inc(consts_in, 16)
            act.dma_start(eye_mask[:], eye_in).then_inc(consts_in, 16)
            act.dma_start(tri[:], tri_in).then_inc(consts_in, 16)
            act.dma_start(rot[:], rot_in).then_inc(consts_in, 16)
            act.dma_start(ident[:], ident_in).then_inc(consts_in, 16)
            act.dma_start(sink[:], sinks_in.to_broadcast([P, AH])).then_inc(consts_in, 16)

            act.wait_ge(vec_loaded, 16)
            nc.scalar.activation(c_act[:], vec[:, VEC["c"]:VEC["c"] + KC], ACT.Sigmoid).then_inc(c_sig, 1)
            act.wait_ge(c_loaded, 16)
            nc.scalar.activation(c_wide[:, 1, :], c_wide[:, 0, :], ACT.Sigmoid).then_inc(c_wide_ready, 1)
            act.wait_ge(lb_shift, 1)
            nc.scalar.activation(lbt[:, 2:4, :], lbt[:, 0:2, :], ACT.Exp).then_inc(lb_exp, 1)
            act.wait_ge(x_in, 16)
            for c in range(KC):
                rms_square(RMS_MIX, c, x0[:, c, :])
            tables()
            act.wait_ge(made, 1)
            rms_finish(RMS_MIX)
            for j in range(3):
                w_high(0, j)
            for c in range(KC):
                act.wait_ge(h_ready, c + 1)
                nc.scalar.activation(xa_hi[:, c, :], hbuf[:, c % 4, :], ACT.Identity, bias=mod[:, c:c + 1])\
                  .then_inc(xh_ready, 1)

            with act.Fori(0, PAIRS) as p:
                def at(c):
                    return p * (PAIR_CHUNKS // SLOTS) + (START["pairs"] + c // SLOTS)

                def chunk(c):
                    ahead(at(c), c % SLOTS)
                    return full(at(c), c % SLOTS)

                def bank(u):
                    act.wait_ge(bank_full[u % 4], p * USES + (u // 4 + 1))
                    return aps[:, u % 4, :]

                def decays(e):
                    act.wait_ge(exps_ready, p * 2 + (e + 1))
                    nc.scalar.activation(kt[:], kt[:], ACT.Exp)
                    nc.scalar.activation(hbuf[:, 0, :], hbuf[:, 0, :], ACT.Exp)
                    nc.scalar.activation(hbuf[:, 1, :], cum[:, e, :], ACT.Exp).then_inc(decay_ready, 1)

                def far_scores(e):
                    u = U_LV[e] + 5
                    nc.scalar.copy(at_h[:, P:T], bank(u)[:, 0:3 * P]).then_inc(taken[u % 4], 1)
                    b = bank(u + 1)
                    nc.scalar.copy(at_h[:, T + 2 * P:2 * T], b[:, 0:2 * P])
                    nc.scalar.copy(at_h[:, 2 * T + 3 * P:3 * T], b[:, 2 * P:3 * P]).then_inc(taken[(u + 1) % 4], 1)

                def head_square(e, r):
                    nc.scalar.activation(hbuf[:, 2 + r, :], bank(U_AV[e][r]), ACT.Square).then_inc(osq_ready, 1)

                def head_rstd(e):
                    for r, dst in enumerate((lnv, rstd)):
                        u = U_NORM[e][r]
                        if e:
                            uo = U_AV[0][r]
                            act.wait_ge(taken[uo % 4], p * USES + (uo // 4 + 2))
                        nc.scalar.activation(dst[:], bank(u), ACT.Ln, bias=eps_col[:], scale=1.0 / P)\
                            .then_inc(taken[u % 4], 1)
                    for r, dst in enumerate((lnv, rstd)):
                        u = U_NORM[e][r]
                        act.wait_ge(taken[u % 4], p * USES + (u // 4 + 2))
                        nc.scalar.activation(dst[:], dst[:], ACT.Exp, scale=-0.5).then_inc(hnorm, 1)

                for e in range(2):
                    nc.scalar.activation(forget[:, e, :], chunk(e), ACT.Sigmoid).then_inc(evicted[e], 1)
                act.wait_ge(gates_used, p * 4 + 1)
                for e in range(2):
                    nc.scalar.activation(sq[:, e, :], chunk(2 + e), ACT.Sigmoid).then_inc(q_sig, 1)
                tables()
                act.wait_ge(f_ready, p + 1)
                nc.scalar.activation(forget[:], forget[:], ACT.Ln).then_inc(logf_ready, 1)
                act.wait_ge(mixed_ready, p * 2 + 1)
                act.dma_start(gates[:], ret_tab[bass.ds(p, 1)].rearrange("a p n t -> p (a n) t")).then_inc(tabs_in, 16)
                ahead(at(4), 0)
                decays(0)

                def values(c, r):
                    if c > 4:
                        ahead(at(c), c % SLOTS)
                    full(at(c + 1), (c + 1) % SLOTS)
                    act.sem_inc(tile_done[c % SLOTS], 1)
                    ahead(at(c + 1), (c + 1) % SLOTS)
                    for n in range(2):
                        b = gps[:, (c + n) % SLOTS, :]
                        nc.scalar.copy(val[:, 2 * n:2 * n + 2, r, :], b.rearrange("p (t v) -> p t v", t=2))\
                          .then_inc(evicted[(c + n) % SLOTS], 1)

                values(4, 0)
                for n in range(2):
                    nc.scalar.copy(rqk[:, n, :], chunk(6 + n)).then_inc(evicted[2 + n], 1)
                far_scores(0)
                decays(1)
                values(8, 1)
                for c in (10, 11):
                    ahead(at(c), c % SLOTS)

                def gate_product(c, e, first):
                    b = chunk(c)
                    if first:
                        k = c - 12 if c == 12 or c == 13 else c - 14
                        if c >= 16:
                            act.wait_ge(gates_used, p * 4 + (1 + e + 1))
                        nc.scalar.activation(sq[:, e, :], b, ACT.Sigmoid).then_inc(gate_sig, 1)
                    else:
                        act.wait_ge(evicted[(c - 2) % SLOTS], at(c - 2) + 2)
                        nc.scalar.activation(sq[:, e, :], b, ACT.Sigmoid).then_inc(evicted[c % SLOTS], 1)

                gate_product(12, 0, True)
                gate_product(13, 1, True)
                head_square(0, 0)
                gate_product(14, 0, False)
                head_square(0, 1)
                gate_product(15, 1, False)
                tables()
                head_rstd(0)
                gate_product(16, 0, True)
                far_scores(1)
                gate_product(17, 1, True)
                head_square(1, 0)
                head_square(1, 1)
                gate_product(18, 0, False)
                tables()
                head_rstd(1)
                gate_product(19, 1, False)

            act.dma_start(res[:], xT.rearrange("(k p) t -> p k t", p=P)).then_inc(res_in, 16)
            for c in range(KC):
                if c in (0, KC - 1):
                    act.wait_ge(mixed_ready, 2 * PAIRS + (0 if c == 0 else 1))
                nc.scalar.copy(xa_hi[:, c, :], mixed[:, c, :]).then_inc(m_hi, 1)
            act.dma_start(hot[:], hot_in).then_inc(hot_in_sem, 16)
            act.dma_start(rel[0:32, :], rel_in).then_inc(hot_in_sem, 16)
            taps = vec[:, VEC["w_dw"]:VEC["w_dw"] + TAP_GROUPS * TAP_GROUP * KC].rearrange("p (k c) -> p k c", c=KC)
            nc.scalar.copy(tap_hi[:], taps[:, :, DVE_CONV:]).then_inc(taps_high, 1)

            def residual(phase, n, gain=None, dst=None, double=None):
                tables()
                for c in range(KC):
                    ahead(START[phase] + c // SLOTS, c % SLOTS)
                    act.wait_ge(evicted[c % SLOTS], START[phase] + c // SLOTS + 2)
                    if gain is not None:
                        gain_high(dst, c, gain)
                    if c >= 2:
                        act.wait_ge(sq_used, USED[n] + max(1, c - 2))
                    square = nc.scalar.activation(sq[:, c % 2, :], res[:, c, :], ACT.Square)
                    if double is not None:
                        square = nc.scalar.activation(hbuf[:, c % 2, :], res[:, c, :], ACT.Square, scale=double(c))
                    square.then_inc(sq_ready, 1)

            residual("w_out", RMS_FIRST, lambda c: conv_gain[:, c:c + 1], xb_hi, lambda c: vcol("final_g", c))
            act.wait_ge(sum_done, SUMS[RMS_FIRST])
            own.done(nc.scalar.activation(lnv[:], aps[:, 0, :], ACT.Ln, bias=eps_col[:], scale=1.0 / D))
            nc.scalar.activation(rstd[:], lnv[:], ACT.Exp, scale=-0.5)
            nc.scalar.activation(sq[:, 0, :], lnv[:], ACT.Exp, scale=-1.0).then_inc(rstd_ready, 1)
            act.wait_ge(double_ready, 1)
            act.wait_ge(rstd_ready, RMS_FIRST + 1)
            own.done(nc.scalar.activation(lnv[:], sq[:, 1, :], ACT.Ln, bias=eps_col[:], scale=1.0 / D))
            nc.scalar.activation(sq[:, 0, :], lnv[:], ACT.Exp, scale=-0.5).then_inc(second_ready, 1)
            act.wait_ge(rel_copied, 2)
            act.dma_start(rel_scratch, rel_rows[:, None, :].to_broadcast([AH, P, REACH + 1])).then_inc(rel_out, 16)

            def glu_halves(I, n, c):
                ahead(I, 2 * n)
                ahead(I, 2 * n + 1)
                at = bass.ds(c, 1)
                full(I, 2 * n)
                nc.scalar.copy(glu[:, at, PAD:], gps[:, 2 * n:2 * n + 1, :]).then_inc(evicted[2 * n], 1)
                full(I, 2 * n + 1)
                nc.scalar.copy(conv[:, at, :], gps[:, 2 * n + 1:2 * n + 2, :]).then_inc(evicted[2 * n + 1], 1)

            def glu_gate(c):
                act.wait_ge(scaled, c + 1)
                gate = conv[:, bass.ds(c, 1), :]
                nc.scalar.activation(gate, gate, ACT.Sigmoid, bias=vdyn("b_pw1", c + KC)).then_inc(sig_ready, 1)

            with act.Fori(0, GLU_LOOP) as i:
                I = i + START["pw1"]
                for n in range(2):
                    glu_halves(I, n, i * 2 + n)
                    glu_gate(i * 2 + n)
            glu_halves(START["pw1"] + GLU_LOOP, 0, DVE_CONV - 1)
            glu_gate(DVE_CONV - 1)
            act.wait_ge(rel_out, 16)
            band = bass.AP(rel_scratch.tensor, P - 1, [[REACH, P], [P * (REACH + 1), AH], [1, BAND]])
            act.dma_start(bias[:], band).then_inc(bias_in, 16)

            def split_high(m):
                act.wait_ge(glu_ready, m + 1)
                nc.scalar.copy(glu_hi[:, m % 2, :], glu[:, DVE_CONV + m, :]).then_inc(glu_high, 1)

            for m in range(PE_CONV):
                c = DVE_CONV + m
                glu_halves(START["pw1"] + c // 2, c % 2, c)
                if m > 0:
                    split_high(m - 1)
                act.wait_ge(scaled, c + 1)
                value = glu[:, c, PAD:]
                nc.scalar.activation(value, value, ACT.Identity, bias=vcol("b_pw1", c))
                glu_gate(c)

            def conv_out(m):
                act.wait_ge(conv_full, m + 1)
                nc.scalar.activation(conv[:, DVE_CONV + m, :], aps[:, 2 + m % 2, :], ACT.Identity, bias=vcol("b_dw", DVE_CONV + m))\
                  .then_inc(conv_copied, 1)

            conv_out(0)
            split_high(PE_CONV - 1)
            for m in range(1, PE_CONV):
                conv_out(m)
            tables()
            for c in range(KC):
                act.wait_ge(center_done, c + 1)
                rms_square(RMS_LN, c, conv[:, c, :])
            rms_finish(RMS_LN)
            for c in range(KC):
                act.wait_ge(h_ready, KC + c + 1)
                nc.scalar.activation(conv[:, c, :], hbuf[:, c % 4, :], ACT.Silu, bias=vcol("ln_b", c))
                nc.scalar.activation(xa_hi[:, c, :], hbuf[:, c % 4, :], ACT.Silu, bias=vcol("ln_b", c))\
                  .then_inc(xh_ready, 1)
            ffn_gain = lambda layer: lambda c: vcol("norm_ffn", layer * KC + c)
            residual("pw2", RMS_FF0, ffn_gain(0), xb_hi)
            rms_finish(RMS_FF0)

            def ffn(layer, hidden, n_next, gain=None, dst=None):
                for part, n in enumerate(FF_PARTS):
                    f0 = layer * FF_CHUNKS + sum(FF_PARTS[:part])
                    with act.Fori(0, n // 2) as i:
                        I = i + START[f"up{layer}{part}"]
                        for m in range(2):
                            ahead(I, 2 * m)
                            act.wait_ge(evicted[2 * m], I + 2)
                            nc.scalar.activation(sq[:, m, :], sq[:, m, :], ACT.Silu).then_inc(silu_ready, 1)
                            ahead(I, 2 * m + 1)
                            act.wait_ge(ff_ready, i * 2 + (f0 + m + 1))
                            nc.scalar.copy(hidden[:, bass.ds(i * 2 + m, 1), :], hbuf[:, 2 * m:2 * m + 1, :]).then_inc(ff_hi, 1)
                    if part < len(FF_PARTS) - 1:
                        with act.Fori(0, KC // SLOTS) as i:
                            for j in range(SLOTS):
                                ahead(i + START[f"down{layer}{part}"], j)
                residual(f"down{layer}{len(FF_PARTS) - 1}", n_next, gain, dst)

            ffn(0, xa_hi, RMS_ATTN, lambda c: vcol("norm_kv", c), xb_hi)
            I = START["kv"]
            ahead(I, 0)
            for c in range(KC):
                gain_high(xa_hi, c, lambda c: vcol("norm_mix", KC + c))
            ahead(I, 1)
            act.wait_ge(sum_done, SUMS[RMS_ATTN])
            own.done(nc.scalar.activation(r_col[:, 0, :], aps[:, 2, 0:NT], ACT.Ln, bias=eps_col[:], scale=1.0 / D))
            own.done(nc.scalar.activation(r_col[:, 1, :], r_col[:, 0, :], ACT.Exp, scale=-0.5))
            rms_finish(RMS_ATTN)
            ahead(I, 2)
            full(I, 3)
            act.sem_inc(tile_done[2], 1)
            ahead(I, 3)
            for t in range(NT):
                ins = nc.scalar.mul(vtok[:, t, :], gps[:, 2 + t // 2, (t % 2) * 2 * P:(t % 2 + 1) * 2 * P], r_col[:, 1, t:t + 1])
                if t % 2:
                    ins.then_inc(evicted[2 + t // 2], 1)

            def attention_out(c):
                for e in range(2):
                    hh = 2 * c + e
                    act.wait_ge(pt_full, hh + 1)
                    nc.scalar.copy(pT[:, e, 0:4, :], aps[:, 2 * e, :].rearrange("p (n t) -> p n t", t=P))
                    nc.scalar.copy(pT[:, e, 4:7, :], aps[:, 2 * e + 1, 0:3 * P].rearrange("p (n t) -> p n t", t=P))\
                      .then_inc(pt_ready, 1)
                act.wait_ge(o_full, c + 1)
                nc.scalar.copy(xb_hi[:, c, :], gps[:, (c + 3) % SLOTS, :]).then_inc(o_hi, 1)

            def attention_exp(c):
                for e in range(2):
                    hh = 2 * c + e
                    act.wait_ge(max_ready, hh + 1)
                    for n in range(NT):
                        s = scores[:, e, n, P if n == 0 else 0:BAND]
                        nc.scalar.activation(s, s, ACT.Exp, bias=neg_max[:, e, n:n + 1],
                                             accum_out=row_sum[:, e, n:n + 1])
                    nc.scalar.activation(sink_exp[:, e, :], neg_max[:, e, :], ACT.Exp, bias=sink[:, hh:hh + 1])\
                      .then_inc(exp_ready, 1)

            for c in range(KC + 1):
                if c < KC:
                    ahead(START["q"] + c // SLOTS, c % SLOTS)
                if c >= 1:
                    attention_out(c - 1)
                if c < KC:
                    attention_exp(c)
            residual("w_o", RMS_FF1, ffn_gain(1), xa_hi)
            rms_finish(RMS_FF1)
            ffn(1, xb_hi, RMS_LAST)
            rms_finish(RMS_LAST)

        @block.vector
        def _(dve):
            own = Steps(dve, dve_own)
            TT, TS, STT = nc.vector.tensor_tensor, nc.vector.tensor_scalar, nc.vector.scalar_tensor_tensor

            def full(I, j):
                dve.wait_ge(tile_done[j], I + 2)
                return gps[:, j, :]

            for j in range(SLOTS):
                dve.sem_inc(evicted[j], 1)
                dve.sem_inc(taken[j], 1)
            dve.sem_inc(gates_used, 1)
            dve.sem_inc(mixed_ready, 1)
            dve.sem_inc(ff_lo, 2)

            def x_build(b, src, gain, hi, lo, shift=False, through=None):
                norm, before = H_BUILDS[b]
                dve.wait_ge(rstd_ready, norm + 1)

                def h(c):
                    STT(hbuf[:, c % 4, :], src[:, c, :], gain(c), rstd[:], ALU.mult, ALU.mult).then_inc(h_ready, 1)

                for c in range(3):
                    h(c)
                for c in range(KC):
                    dve.wait_ge(xh_ready, KC * b + c + 1)
                    high = hi[:, c, :].bitcast(F32)
                    dve.wait_ge(h_ready, KC * before + c + 1)
                    if through is not None:
                        TT(lo[:, c, :], through[:, c, :], high, ALU.subtract).then_inc(x_ready, 1)
                    elif shift:
                        STT(lo[:, c, :], hbuf[:, c % 4, :], mod[:, c:c + 1], high, ALU.add, ALU.subtract)\
                            .then_inc(x_ready, 1)
                    if c + 3 < KC:
                        if c > 0:
                            dve.wait_ge(x_ready, KC * b + c)
                        h(c + 3)

            def gain_low(b, c, gain, hi, lo):
                dve.wait_ge(xh_ready, KC * b + c + 1)
                STT(lo[:, c, :], res[:, c, :], gain(c), hi[:, c, :].bitcast(F32), ALU.mult, ALU.subtract).then_inc(x_ready, 1)

            nc.vector.memset(ones[:], 1.0)
            nc.vector.memset(eps_col[:], EPS).then_inc(made, 1)
            own.done(nc.vector.memset(reset[:], 1.0))
            own.done(nc.vector.memset(reset[:, :].rearrange("p (t s) -> p t s", s=P)[:, :, 0:1], 0.0))
            dve.wait_ge(vec_loaded, 16)
            l0, l1 = (vec[:, VEC[n]:VEC[n] + KC] for n in ("lb0", "lb1"))
            own.done(TT(lbt[:, 2, :], l0, l1, ALU.max))
            TT(lbt[:, 0, :], l0, lbt[:, 2, :], ALU.subtract)
            TT(lbt[:, 1, :], l1, lbt[:, 2, :], ALU.subtract).then_inc(lb_shift, 1)
            dve.wait_ge(c_sig, 1)
            own.done(TT(c_act[:], c_act[:], vec[:, VEC["c"]:VEC["c"] + KC], ALU.mult))
            own.done(nc.vector.tensor_copy(c_pair[:, :, 0], c_act[:]))
            TT(c_pair[:, :, 1], c_act[:], c_pair[:, :, 0].bitcast(F32), ALU.subtract).then_inc(c_ready, 1)
            dve.wait_ge(lb_exp, 1)
            own.done(TT(lbt[:, 0, :], lbt[:, 2, :], lbt[:, 3, :], ALU.add))
            own.done(nc.vector.reciprocal(lbt[:, 1, :], lbt[:, 0, :]))
            own.done(TT(lower[:], lbt[:, 2, :], lbt[:, 1, :], ALU.mult))
            own.done(TS(one_minus[:], lower[:], -1.0, 1.0, ALU.mult, ALU.add))
            own.done(TT(conv_gain[:], vec[:, VEC["final_g"]:VEC["final_g"] + KC], vec[:, VEC["norm_mix"]:VEC["norm_mix"] + KC],
                        ALU.mult))
            dve.wait_ge(c_wide_ready, 1)
            own.done(TT(c_wide[:, 0, :], c_wide[:, 0, :], c_wide[:, 1, :], ALU.mult))
            for n in range(ADA_CHUNKS):
                if n % ADA_LOAD == 0:
                    dve.wait_ge(ada_loaded[n // ADA_LOAD], 16)
                c = (n + KC) % ADA_CHUNKS
                own.mark(nc.vector.tensor_tensor_reduce(
                    ada_w[:, n, :], ada_w[:, n, :], c_wide[:, 0, :], op0=ALU.mult, op1=ALU.add, scale=1.0,
                    scalar=vcol("b_ada", c), accum_out=mod[:, c:c + 1]))
            own.wait()
            own.done(STT(mix_gain[:], mod[:, KC:2 * KC], 1.0, vec[:, VEC["norm_g"]:VEC["norm_g"] + KC], ALU.add, ALU.mult))
            x_build(X_MIX, x0, lambda c: mix_gain[:, c:c + 1], xa_hi, xa_lo, shift=True)
            own.done(nc.vector.memset(at_h[:], 0.0))

            with dve.Fori(0, PAIRS) as p:
                own.enter(p, PAIR_STEPS)

                def at(c):
                    return p * (PAIR_CHUNKS // SLOTS) + (START["pairs"] + c // SLOTS)

                def chunk(c):
                    return full(at(c), c % SLOTS)

                def was_evicted(c):
                    dve.wait_ge(evicted[c % SLOTS], at(c) + 2)

                def bank(u):
                    dve.wait_ge(bank_full[u % 4], p * USES + (u // 4 + 1))
                    return aps[:, u % 4, :]

                def was_taken(u):
                    dve.wait_ge(taken[u % 4], p * USES + (u // 4 + 2))

                def exponents(e):
                    x = cum[:, e, :]
                    for level in range(LEVELS):
                        left, right, mid = halves(x, level)
                        to_left, to_right, _ = halves(kt[:, level, :], level)
                        TT(to_left, mid, left, ALU.subtract)
                        TT(to_right, right, mid, ALU.subtract)
                    tiles = x.rearrange("p (t s) -> p t s", s=P)
                    TT(hbuf[:, 0, :].rearrange("p (t s) -> p t s", s=P),
                       tiles[:, :, P - 1:P].to_broadcast([P, NT, P]), tiles, ALU.subtract).then_inc(exps_ready, 1)

                def decayed(e):
                    dve.wait_ge(decay_ready, p * 2 + (e + 1))
                    qe, ke, grow = q[:, e, :], key[:, e, :], hbuf[:, 1, :]
                    for level in range(LEVELS):
                        _, right, _ = halves(qe, level)
                        _, dec, _ = halves(kt[:, level, :], level)
                        h = (P >> level) // 2
                        last = TT(qt[:, level, :].rearrange("p (n h) -> p n h", h=h), right, dec, ALU.mult)
                    TT(k_far[:, :, :], ke[:, 0:3 * P].rearrange("p (t s) -> p t s", s=P),
                       hbuf[:, 0, 0:3 * P].rearrange("p (t s) -> p t s", s=P), ALU.mult)
                    TT(q_far[:, 0, :], qe[:, P:2 * P], grow[:, P:2 * P], ALU.mult)
                    TT(q_far[:, 3, :], qe[:, 2 * P:3 * P], grow[:, 2 * P:3 * P], ALU.mult)
                    own.done(TT(q_far[:, 5, :], qe[:, 3 * P:], grow[:, 3 * P:], ALU.mult))
                    TS(q_far[:, 1, :], q_far[:, 3, :], grow[:, 2 * P - 1:2 * P], None, ALU.mult)
                    own.done(TS(q_far[:, 4, :], q_far[:, 5, :], grow[:, 3 * P - 1:3 * P], None, ALU.mult))
                    TS(q_far[:, 2, :], q_far[:, 4, :], grow[:, 2 * P - 1:2 * P], None, ALU.mult)
                    TT(kt[:], kt[:], ke[:, None, :].to_broadcast([P, LEVELS, T]), ALU.mult).then_inc(prep_done, 1)

                def near_scores(e):
                    u = U_LV[e]
                    for n, levels in enumerate(LEVEL_BANKS):
                        b = bank(u + n)
                        dve.sem_inc(passed, 1)
                        for m, level in enumerate(levels):
                            h = (P >> level) // 2
                            out = diag(at_h).rearrange("p t (n s) -> p t n s", s=2 * h)[:, :, :, h:]
                            mask = lvl_mask[:, level, :].rearrange("p (n h) -> p n h", h=h)[:, None, :, :]
                            data = b[:, m * T // 2:(m + 1) * T // 2].rearrange("p (t n h) -> p t n h", t=NT, h=h)
                            ins = nc.vector.copy_predicated(out, mask.to_broadcast([P, NT, P // 2 // h, h]), data)
                            if m < len(levels) - 1:
                                own.done(ins)
                                dve.sem_inc(passed, 1)
                            else:
                                ins.then_inc(taken[(u + n) % 4], 1)
                                was_taken(u + n)
                    u += len(LEVEL_BANKS)
                    b = bank(u)
                    dve.sem_inc(passed, 1)
                    nc.vector.copy_predicated(diag(at_h), eye_mask[:, None, :].to_broadcast([P, NT, P]),
                                              b.rearrange("p (t s) -> p t s", s=P)).then_inc(taken[u % 4], 1)

                def causal(e):
                    for j in range(NT):
                        u = U_SC[e] + j
                        n = T - j * P
                        TT(at_r[:, j * (T + P):(j + 1) * T], bank(u)[:, 0:n], tri[:, 0:n], ALU.mult).then_inc(taken[u % 4], 1)

                def normalize(e, r, dst):
                    u = U_AV[e][r]
                    dve.wait_ge(hnorm, p * 4 + (2 * e + r + 1))
                    TT(dst, aps[:, u % 4, :], (lnv, rstd)[r][:], ALU.mult).then_inc(taken[u % 4], 1)
                    was_taken(u)

                def z_gate(c, e, r, gain):
                    dve.wait_ge(gate_sig, p * 4 + (2 * r + e + 1))
                    STT(gates[:, 2 * r + e, :], gps[:, c % SLOTS, :], vdyn(gain, p * 2 + e), sq[:, e, :],
                        ALU.mult, ALU.mult).then_inc(evicted[c % SLOTS], 1)

                def branch_gate(c, e, r):
                    was_evicted(c)
                    was_evicted(c - 2)
                    TT(gates[:, 2 * r + e, :], gates[:, 2 * r + e, :], sq[:, e, :], ALU.mult).then_inc(gates_used, 1)

                for e in range(2):
                    was_evicted(e)
                    own.mark(TS(forget[:, e, :], forget[:, e, :], one_minus[:, bass.ds(p * 2 + e, 1)],
                                lower[:, bass.ds(p * 2 + e, 1)], ALU.mult, ALU.add))
                own.wait()
                own.done(TS(key[:], forget[:], -1.0, 1.0, ALU.mult, ALU.add))
                TS(forget[:], forget[:], TINY, None, ALU.max).then_inc(f_ready, 1)
                for e in range(2):
                    dve.wait_ge(q_sig, p * 2 + (e + 1))
                    TT(q[:, e, :], gps[:, 2 + e, :], sq[:, e, :], ALU.mult).then_inc(evicted[2 + e], 1)
                dve.wait_ge(logf_ready, p + 1)
                for e in range(2):
                    own.mark(nc.vector.tensor_tensor_scan(cum[:, e, :], reset[:], forget[:, e, :], 0.0, ALU.mult, ALU.add))
                own.wait()
                exponents(0)
                for e in range(2):
                    was_evicted(2 + e)
                decayed(0)
                near_scores(0)
                bank(U_LV[0] + 6)
                exponents(1)
                decayed(1)
                dve.wait_ge(tabs_in, p * 16 + 16)
                for n in range(2):
                    was_evicted(6 + n)
                    u = U_ROT + n
                    TT(unit[:, n, :], bank(u), gates[:, 2 * n + 1, :], ALU.mult).then_inc(taken[u % 4], 1)
                    own.done(TT(rqk[:, n, :], rqk[:, n, :], gates[:, 2 * n, :], ALU.mult))
                    was_taken(u)
                    TT(rqk[:, n, :], rqk[:, n, :], unit[:, n, :], ALU.add).then_inc(rot_ready, 1)
                for e in range(2):
                    c = 10 + e
                    b = chunk(c)
                    TS(mod[:, bass.ds(p * 2 + (2 * KC + e), 1)], b[:, 0:1], b[:, 1:2], vdyn("b_ada", p * 2 + (2 * KC + e)),
                       ALU.add, ALU.add).then_inc(evicted[c % SLOTS], 1)
                dve.wait_ge(rot_ready, p * 2 + 2)
                z_gate(12, 0, 0, "hg_norm_g")
                z_gate(13, 1, 0, "hg_norm_g")
                causal(0)
                branch_gate(14, 0, 0)
                branch_gate(15, 1, 0)
                normalize(0, 0, unit[:, 0, :])
                normalize(0, 1, unit[:, 1, :])
                dve.wait_ge(gates_used, p * 4 + 3)

                def take_norm(e, r):
                    own.done(TT(gates[:, 2 * r + e, :], gates[:, 2 * r + e, :], unit[:, r, :], ALU.mult))

                take_norm(0, 0)
                z_gate(16, 0, 1, "ret_norm_g")
                near_scores(1)
                was_evicted(16)
                take_norm(0, 1)
                z_gate(17, 1, 1, "ret_norm_g")
                causal(1)
                branch_gate(18, 0, 1)
                dve.wait_ge(gates_used, p * 4 + 4)
                TT(mixed[:, bass.ds(p * 2, 1), :], gates[:, 0:1, :], gates[:, 2:3, :], ALU.add).then_inc(mixed_ready, 1)
                normalize(1, 0, unit[:, 0, :])
                take_norm(1, 0)
                was_evicted(17)
                normalize(1, 1, unit[:, 1, :])
                take_norm(1, 1)
                branch_gate(19, 1, 1)
                dve.wait_ge(gates_used, p * 4 + 5)
                TT(mixed[:, bass.ds(p * 2 + 1, 1), :], gates[:, 1:2, :], gates[:, 3:4, :], ALU.add).then_inc(mixed_ready, 1)
                own.leave(PAIRS)

            for c in range(KC):
                dve.wait_ge(m_hi, c + 1)
                dve.wait_ge(mixed_ready, 2 * PAIRS + 1)
                TT(xa_lo[:, c, :], mixed[:, c, :], xa_hi[:, c, :].bitcast(F32), ALU.subtract).then_inc(m_lo, 1)
            nc.vector.memset(rel[32:33, :], NEG).then_inc(rel_copied, 1)
            nc.vector.memset(glu[:, :, 0:PAD], 0.0)
            taps = vec[:, VEC["w_dw"]:VEC["w_dw"] + TAP_GROUPS * TAP_GROUP * KC].rearrange("p (k c) -> p k c", c=KC)
            dve.wait_ge(taps_high, 1)
            TT(tap_lo[:], taps[:, :, DVE_CONV:], tap_hi[:].bitcast(F32), ALU.subtract).then_inc(taps_ready, 1)
            dve.wait_ge(res_in, 16)
            for j in range(2):
                dve.wait_ge(evicted[2 + j], START["w_out"] + 1)

            def residual(phase, n, scale=None, shift=None, build=None, double=False):

                def add_squares(m):
                    dve.wait_ge(sq_ready, KC * n + m + 1)
                    if m > 1:
                        dve.wait_ge(sq_used, USED[n] + m - 1)
                    ins = TT(lnv[:], sq[:, 0, :] if m == 1 else lnv[:], sq[:, m % 2, :], ALU.add)
                    if double:
                        total = hbuf[:, 2, :]
                        ins = TT(total, hbuf[:, 0, :] if m == 1 else total, hbuf[:, m % 2, :], ALU.add)
                    ins.then_inc(sq_used, 1)

                for c in range(KC):
                    I, j = START[phase] + c // SLOTS, c % SLOTS
                    b = full(I, j)
                    if scale is not None:
                        ins = STT(res[:, c, :], b, scale(c), res[:, c, :], ALU.mult, ALU.add)
                    elif shift is not None:
                        ins = STT(res[:, c, :], b, shift(c), res[:, c, :], ALU.add, ALU.add)
                    else:
                        ins = TT(res[:, c, :], b, res[:, c, :], ALU.add)
                    ins.then_inc(evicted[j], 1)
                    if c >= 2:
                        add_squares(c - 1)
                    if c >= 1 and build is not None:
                        gain_low(build[0], c - 1, *build[1:])
                if build is not None:
                    dve.wait_ge(evicted[SLOTS - 1], START[phase] + KC // SLOTS + 1)
                    gain_low(build[0], KC - 1, *build[1:])

            residual("w_out", RMS_FIRST, scale=lambda c: mod[:, 2 * KC + c:2 * KC + c + 1],
                     build=(X_CONV_IN, lambda c: conv_gain[:, c:c + 1], xb_hi, xb_lo), double=True)
            dve.wait_ge(rel_full, 1)
            nc.vector.tensor_copy(rel_rows[:], aps[0:AH, 3, 0:REACH + 1]).then_inc(rel_copied, 1)
            dve.wait_ge(rstd_ready, RMS_FIRST + 1)
            TT(sq[:, 1, :], aps[:, 1, :], sq[:, 0, :], ALU.mult).then_inc(double_ready, 1)
            dve.wait_ge(second_ready, 1)
            TT(lnv[:], rstd[:], sq[:, 0, :], ALU.mult).then_inc(both_ready, 1)
            dve.wait_ge(sq_ready, KC * RMS_FIRST + KC)

            def normed_residual(c):
                STT(res[:, c, :], res[:, c, :], vcol("final_g", c), rstd[:], ALU.mult, ALU.mult).then_inc(res_ready, 1)

            for c in range(KC):
                normed_residual(c)
            def convolve(chunks):
                for n, c in enumerate(chunks):
                    dve.wait_ge(sig_ready, c + 1)
                    value = glu[:, bass.ds(c, 1), PAD:]
                    own.mark(STT(value, value, vdyn("b_pw1", c), conv[:, bass.ds(c, 1), :], ALU.add, ALU.mult))
                for k in range(TAPS):
                    for n, c in enumerate(chunks):
                        out, src = conv[:, bass.ds(c, 1), :], glu[:, bass.ds(c, 1), k:k + T]
                        w = vdyn("w_dw", c + k * KC)
                        own.wait(own.local - len(chunks) + 1)
                        if k == 0:
                            own.mark(TS(out, src, w, vdyn("b_dw", c), ALU.mult, ALU.add))
                        else:
                            own.mark(STT(out, src, w, out, ALU.mult, ALU.add))
                own.wait()
                dve.sem_inc(conv_done, 1)

            convolve([0])
            with dve.Fori(0, GLU_LOOP) as i:
                own.enter(i, 2 * TAPS + 2)
                convolve([i * 2 + 1, i * 2 + 2])
                own.leave(GLU_LOOP)
            dve.wait_ge(mean_done, 1)
            for c in range(KC):
                STT(conv[:, c, :], aps[:, 1, :], -1.0 / D, conv[:, c, :], ALU.mult, ALU.add).then_inc(center_done, 1)
            dve.wait_ge(center_done, KC)
            dve.wait_ge(x_ready, KC * X_PW2)
            x_build(X_PW2, conv, lambda c: vcol("ln_g", c), xa_hi, xa_lo, through=conv)
            ffn_gain = lambda layer: lambda c: vcol("norm_ffn", layer * KC + c)
            residual("pw2", RMS_FF0, shift=lambda c: vcol("b_pw2", c), build=(X_FF0, ffn_gain(0), xb_hi, xb_lo))

            def ffn(layer, hidden_hi, hidden_lo, norm, n_next, build=None):
                dve.wait_ge(rstd_ready, norm + 1)
                for part, n in enumerate(FF_PARTS):
                    f0 = layer * FF_CHUNKS + sum(FF_PARTS[:part])
                    with dve.Fori(0, n // 2) as i:
                        I = i + START[f"up{layer}{part}"]
                        for m in range(2):
                            h = hbuf[:, 2 * m, :]
                            dve.wait_ge(ff_lo, i * 2 + (f0 + m + 1))
                            TT(sq[:, m, :], full(I, 2 * m), rstd[:], ALU.mult).then_inc(evicted[2 * m], 1)
                            TT(h, full(I, 2 * m + 1), rstd[:], ALU.mult).then_inc(evicted[2 * m + 1], 1)
                            dve.wait_ge(silu_ready, i * 2 + (f0 + m + 1))
                            dve.wait_ge(evicted[2 * m + 1], I + 2)
                            TT(h, h, sq[:, m, :], ALU.mult).then_inc(ff_ready, 1)
                            dve.wait_ge(ff_hi, i * 2 + (f0 + m + 1))
                            TT(hidden_lo[:, bass.ds(i * 2 + m, 1), :], hbuf[:, 2 * m:2 * m + 1, :],
                               hidden_hi[:, bass.ds(i * 2 + m, 1), :].bitcast(F32), ALU.subtract).then_inc(ff_lo, 1)
                    if part < len(FF_PARTS) - 1:
                        with dve.Fori(0, KC // SLOTS) as i:
                            for j in range(SLOTS):
                                r = res[:, bass.ds(i * SLOTS + j, 1), :]
                                full(i + START[f"down{layer}{part}"], j)
                                TT(r, gps[:, j:j + 1, :], r, ALU.add).then_inc(evicted[j], 1)
                residual(f"down{layer}{len(FF_PARTS) - 1}", n_next, build=build)

            ffn(0, xa_hi, xa_lo, RMS_FF0, RMS_ATTN, (X_KV, lambda c: vcol("norm_kv", c), xb_hi, xb_lo))
            for c in range(KC):
                gain_low(X_Q, c, lambda c: vcol("norm_mix", KC + c), xa_hi, xa_lo)
            dve.wait_ge(rstd_ready, RMS_ATTN + 1)
            for j in range(2):
                TT(kT[:, j, :], full(START["kv"], j), rstd[:], ALU.mult).then_inc(evicted[j], 1)
            own.done(nc.vector.memset(scores[:, :, 0, 0:P], NEG))
            dve.wait_ge(bias_in, 16)

            def queries(c):
                STT(qT[:, c % 2, :], full(START["q"] + c // SLOTS, c % SLOTS), HD ** -0.5, rstd[:], ALU.mult, ALU.mult)\
                    .then_inc(evicted[c % SLOTS], 1)

            def attention_max(c):
                for e in range(2):
                    hh = 2 * c + e
                    dve.wait_ge(s_full, hh + 1)
                    TT(scores[:, e, 0, P:], aps[:, 2 * e, P:2 * P], bias[:, hh, P:], ALU.add)
                    TT(scores[:, e, 1, :], aps[:, 2 * e, 2 * P:], bias[:, hh, :], ALU.add)
                    TT(scores[:, e, 2:4, :], aps[:, 2 * e + 1, :].rearrange("p (n k) -> p n k", n=2),
                       bias[:, hh:hh + 1, :].to_broadcast([P, 2, BAND]), ALU.add).then_inc(s_taken, 1)
                    dve.wait_ge(s_taken, hh + 1)
                    own.done(nc.vector.tensor_reduce(row_max[:, e, :], scores[:, e, :, :], AX_X, ALU.max))
                    TS(neg_max[:, e, :], row_max[:, e, :], sink[:, hh:hh + 1], -1.0, ALU.max, ALU.mult)\
                        .then_inc(max_ready, 1)

            def attention_probs(c):
                for e in range(2):
                    hh = 2 * c + e
                    dve.wait_ge(exp_ready, hh + 1)
                    own.done(TT(row_max[:, e, :], row_sum[:, e, :], sink_exp[:, e, :], ALU.add))
                    own.done(nc.vector.reciprocal(row_inv[:, e, :], row_max[:, e, :]))
                    TS(scores[:, e, 0, P:], scores[:, e, 0, P:], row_inv[:, e, 0:1], None, ALU.mult)
                    TT(scores[:, e, 1:, :], scores[:, e, 1:, :], row_inv[:, e, 1:, None].to_broadcast([P, 3, BAND]), ALU.mult)\
                        .then_inc(p_ready, 1)

            def attention_low(c):
                dve.wait_ge(o_hi, c + 1)
                TT(xb_lo[:, c, :], gps[:, (c + 3) % SLOTS, :], xb_hi[:, c, :].bitcast(F32), ALU.subtract).then_inc(o_lo, 1)

            for c in range(KC + 1):
                if c < KC:
                    queries(c)
                if c >= 1:
                    attention_low(c - 1)
                if c < KC:
                    attention_max(c)
                    attention_probs(c)
            residual("w_o", RMS_FF1, build=(X_FF1, ffn_gain(1), xa_hi, xa_lo))
            ffn(1, xb_hi, xb_lo, RMS_FF1, RMS_LAST)
            dve.wait_ge(rstd_ready, RMS_LAST + 1)
            for c in range(KC):
                STT(y[:, c, :], res[:, c, :], vcol("norm_final", c), rstd[:], ALU.mult, ALU.mult).then_inc(y_ready, 1)

        @block.tensor
        def _(pe):
            mm = nc.tensor.matmul
            for j in range(SLOTS):
                pe.sem_inc(tile_done[j], 1)

            def ready(I, j):
                pe.wait_ge(lo_ready[j], I + 2)
                pe.wait_ge(evicted[j], I + 1)

            def dense(I, j, x, blocks=KC, operand=None, part=None):
                k0, k1 = part or (0, blocks)
                if k0 == 0:
                    ready(I, j)
                for k in range(k0, k1):
                    if operand is not None:
                        operand(k)
                    w = slice(k * P, (k + 1) * P)
                    mm(gps[:, j, :], w_hi[:, j, w], x[0][:, k, :], start=k == 0, stop=False)
                    mm(gps[:, j, :], w_hi[:, j, w], x[1][:, k, :], start=False, stop=False)
                    last = mm(gps[:, j, :], w_lo[:, j, w], x[0][:, k, :], start=False, stop=k == blocks - 1)
                if k1 == blocks:
                    last.then_inc(tile_done[j], 1)

            def dense_tokens(I, j, x):
                ready(I, j)
                ready(I, j + 1)
                for t in range(NT):
                    tok = slice(t * P, (t + 1) * P)
                    out = gps[:, j + t // 2, 2 * (t % 2) * P:2 * (t % 2 + 1) * P]
                    for k in range(KC):
                        w = slice(k * P, (k + 1) * P)
                        wh, wl = w_hi[:, j:j + 2, w], w_lo[:, j:j + 2, w]
                        mm(out, x[0][:, k, tok], wh, start=k == 0, stop=False)
                        mm(out, x[1][:, k, tok], wh, start=False, stop=False)
                        last = mm(out, x[0][:, k, tok], wl, start=False, stop=k == KC - 1)
                last.then_inc(tile_done[j + 1], 1)

            def ada(I, j):
                ready(I, j)
                for k in range(KC):
                    w = slice(k * P, (k + 1) * P)
                    mm(gps[:, j, 0:2], w_hi[:, j, w], c_pair[:, k, :], start=k == 0, stop=False)
                    last = mm(gps[:, j, 0:2], w_lo[:, j, w], c_pair[:, k, :], start=False, stop=k == KC - 1)
                last.then_inc(tile_done[j], 1)

            def sum_squares(n, c):
                pe.wait_ge(sq_ready, KC * n + c + 1)
                mm(aps[:, 0, :], ones[:], sq[:, c % 2, :], start=c == 0, stop=c == KC - 1).then_inc(sum_done, 1)

            def sum_running(n, double=False, columns=False):
                pe.wait_ge(sq_used, USED[n] + KC - 2)
                pe.wait_ge(sq_ready, KC * n + KC)
                mm(aps[:, 0, :], ones[:], lnv[:], start=True, stop=False)
                last = mm(aps[:, 0, :], ones[:], sq[:, 1, :], start=False, stop=True)
                if double:
                    mm(aps[:, 1, :], ones[:], hbuf[:, 2, :], start=True, stop=False)
                    last = mm(aps[:, 1, :], ones[:], hbuf[:, 1, :], start=False, stop=True)
                if columns:
                    for t in range(NT):
                        tok = slice(t * P, (t + 1) * P)
                        mm(aps[:, 2, t:t + 1], lnv[:, tok], ones[:, 0:1], start=True, stop=False)
                        last = mm(aps[:, 2, t:t + 1], sq[:, 1, tok], ones[:, 0:1], start=False, stop=True)
                last.then_inc(sum_done, 1)

            def x_wait(b):
                return lambda k: pe.wait_ge(x_ready, KC * b + k + 1)

            xa, xb = (xa_hi, xa_lo), (xb_hi, xb_lo)
            pe.wait_ge(made, 1)
            for c in range(KC):
                sum_squares(RMS_MIX, c)
            pe.wait_ge(c_ready, 1)
            pe.wait_ge(consts_in, CONSTS)

            with pe.Fori(0, PAIRS) as p:
                def at(c):
                    return p * (PAIR_CHUNKS // SLOTS) + (START["pairs"] + c // SLOTS)

                def feature(c):
                    dense(at(c), c % SLOTS, xa, operand=x_wait(X_MIX) if c == 0 else None)

                def bank(u):
                    pe.wait_ge(taken[u % 4], p * USES + (u // 4 + 1))
                    return aps[:, u % 4, :]

                def was_taken(u):
                    pe.wait_ge(taken[u % 4], p * USES + (u // 4 + 2))

                def hgrn_scores(e):
                    pe.wait_ge(prep_done, p * 2 + (e + 1))
                    u = U_LV[e]
                    for n, levels in enumerate(LEVEL_BANKS):
                        b = bank(u + n)
                        for m, level in enumerate(levels):
                            for t in range(NT):
                                h = P // 2
                                o = m * T // 2 + t * h
                                last = mm(b[:, o:o + h], kt[:, level, t * P:(t + 1) * P], qt[:, level, t * h:(t + 1) * h],
                                          start=True, stop=True)
                        last.then_inc(bank_full[(u + n) % 4], 1)
                    u += len(LEVEL_BANKS)
                    b = bank(u)
                    for t in range(NT):
                        s = slice(t * P, (t + 1) * P)
                        last = mm(b[:, s], key[:, e, s], q[:, e, s], start=True, stop=True)
                    last.then_inc(bank_full[u % 4], 1)
                    b = bank(u + 1)
                    mm(b[:, 0:3 * P], k_far[:, 0, :], q_far[:, 0:3, :].rearrange("p n t -> p (n t)"), start=True, stop=True)\
                        .then_inc(bank_full[(u + 1) % 4], 1)
                    b = bank(u + 2)
                    mm(b[:, 0:2 * P], k_far[:, 1, :], q_far[:, 3:5, :].rearrange("p n t -> p (n t)"), start=True, stop=True)
                    mm(b[:, 2 * P:3 * P], k_far[:, 2, :], q_far[:, 5, :], start=True, stop=True)\
                        .then_inc(bank_full[(u + 2) % 4], 1)

                def rotate():
                    for n in range(2):
                        u = U_ROT + n
                        pe.wait_ge(evicted[2 + n], at(6 + n) + 2)
                        mm(bank(u), rot[:], rqk[:, n, :], start=True, stop=True).then_inc(bank_full[u % 4], 1)

                def ret_scores(e):
                    pe.wait_ge(rot_ready, p * 2 + 2)
                    rows = slice(e * RET_DK, (e + 1) * RET_DK)
                    for j in range(NT):
                        u = U_SC[e] + j
                        mm(bank(u)[:, 0:T - j * P], rqk[rows, 1, j * P:(j + 1) * P], rqk[rows, 0, j * P:],
                           start=True, stop=True).then_inc(bank_full[u % 4], 1)

                def attend(e, r):
                    if r == 0:
                        for u in range(U_LV[e], U_LV[e] + 7):
                            if u >= U_LV[e] + 3:
                                was_taken(u)
                    else:
                        for j in range(NT):
                            was_taken(U_SC[e] + j)
                    u = U_AV[e][r]
                    b, at_x = bank(u), (at_h, at_r)[r]
                    for n in range(2):
                        c = (4, 8)[r] + n
                        pe.wait_ge(evicted[c % SLOTS], at(c) + 2)
                    for j in range(NT):
                        last = mm(b[:, j * P:], val[:, j, r, e * P:(e + 1) * P], at_x[:, j * (T + P):(j + 1) * T],
                                  start=j == 0, stop=j == NT - 1)
                    last.then_inc(bank_full[u % 4], 1)

                def head_sum(e, r):
                    u = U_NORM[e][r]
                    pe.wait_ge(osq_ready, p * 4 + (2 * e + r + 1))
                    mm(bank(u), ones[:], hbuf[:, 2 + r, :], start=True, stop=True).then_inc(bank_full[u % 4], 1)

                for c in range(4):
                    feature(c)
                dense_tokens(at(4), 0, xa)
                feature(6)
                feature(7)
                hgrn_scores(0)
                dense_tokens(at(8), 0, xa)
                rotate()
                ada(at(10), 2)
                ada(at(11), 3)
                feature(12)
                feature(13)
                ret_scores(0)
                attend(0, 0)
                feature(14)
                attend(0, 1)
                head_sum(0, 0)
                feature(15)
                head_sum(0, 1)
                feature(16)
                hgrn_scores(1)
                feature(17)
                ret_scores(1)
                attend(1, 0)
                attend(1, 1)
                feature(18)
                head_sum(1, 0)
                head_sum(1, 1)
                feature(19)

            def layer(phase, x, blocks=KC, operand=None, first=0):
                for c in range(first, KC):
                    dense(START[phase] + c // SLOTS, c % SLOTS, x, blocks, operand if c == 0 else None)

            def layer_then(phase, quads, x, operand, between):
                I = START[phase]
                for j in range(SLOTS):
                    dense(I, j, x, operand=operand if j == 0 else None)
                    if j == 0:
                        between()
                with pe.Fori(1, quads) as i:
                    for j in range(SLOTS):
                        dense(i + I, j, x)

            layer("w_out", xa, operand=lambda k: pe.wait_ge(m_lo, k + 1))
            pe.wait_ge(hot_in_sem, 32)
            pe.wait_ge(rel_copied, 1)
            mm(aps[0:AH, 3, 0:REACH + 1], rel[:], hot[:], start=True, stop=True).then_inc(rel_full, 1)
            layer_then("pw1", KC // 2, xb, x_wait(X_CONV_IN), lambda: sum_running(RMS_FIRST, double=True))
            for m in range(PE_CONV):
                pe.wait_ge(glu_low, m + 1)
                if m >= 2:
                    pe.wait_ge(conv_copied, m - 1)
                for k in range(TAPS):
                    if k % TAP_GROUP == 0:
                        pe.wait_ge(diag_ready, m * TAP_GROUPS + k // TAP_GROUP + 1)
                    out, src = aps[:, 2 + m % 2, :], slice(k, k + T)
                    mm(out, diag_hi[:, k, :], glu_hi[:, m % 2, src], start=k == 0, stop=False)
                    mm(out, diag_hi[:, k, :], glu_lo[:, m % 2, src], start=False, stop=False)
                    last = mm(out, diag_lo[:, k, :], glu_hi[:, m % 2, src], start=False, stop=k == TAPS - 1)
                    if k == TAPS - 1:
                        last.then_inc(conv_full, 1)
                    elif k % TAP_GROUP == TAP_GROUP - 1:
                        last.then_inc(diag_used, 1)
            pe.wait_ge(conv_sum, DVE_CONV)
            mm(aps[:, 1, :], ones[:], hbuf[:, 3, :], start=True, stop=False)
            pe.wait_ge(conv_copied, PE_CONV)
            for c in range(DVE_CONV + 1, KC):
                last = mm(aps[:, 1, :], ones[:], conv[:, c, :], start=False, stop=c == KC - 1)
            last.then_inc(mean_done, 1)
            for c in range(KC):
                sum_squares(RMS_LN, c)
            layer("pw2", xa, operand=x_wait(X_PW2))

            def ffn(layer_n, b, norm, x, hidden):
                for part, n in enumerate(FF_PARTS):
                    f0 = layer_n * FF_CHUNKS + sum(FF_PARTS[:part])
                    up = f"up{layer_n}{part}"
                    if part == 0:
                        layer_then(up, n // 2, x, x_wait(b), lambda: sum_running(norm))
                    else:
                        with pe.Fori(0, n // 2) as i:
                            for j in range(SLOTS):
                                dense(i + START[up], j, x)
                    ready_k = lambda k: pe.wait_ge(ff_lo, f0 + k + 3)
                    down = f"down{layer_n}{part}"
                    if part < len(FF_PARTS) - 1:
                        with pe.Fori(0, KC // SLOTS) as i:
                            for j in range(SLOTS):
                                dense(i + START[down], j, hidden, n, ready_k if j == 0 else None)
                    else:
                        layer(down, hidden, n, ready_k)

            ffn(0, X_FF0, RMS_FF0, xb, xa)
            I = START["kv"]
            for j in range(2):
                dense(I, j, xb, operand=x_wait(X_KV) if j == 0 else None)
                if j == 0:
                    sum_running(RMS_ATTN, columns=True)
            dense_tokens(I, 2, xb)

            def band_scores(c):
                for e in range(2):
                    hh = 2 * c + e
                    rows = slice(e * HD, (e + 1) * HD)
                    if e == 0:
                        pe.wait_ge(evicted[c % SLOTS], START["q"] + c // SLOTS + 2)
                    if hh >= 2:
                        pe.wait_ge(pt_ready, hh - 1)
                    for n in range(NT):
                        k0 = max(n - 1, 0) * P
                        o = (n % 2) * BAND + (P if n == 0 else 0)
                        last = mm(aps[:, 2 * e + n // 2, o:(n % 2 + 1) * BAND], qT[rows, c % 2, n * P:(n + 1) * P],
                                  kT[rows, c // 4, k0:(n + 1) * P], start=True, stop=True)
                    last.then_inc(s_full, 1)

            def band_values(c):
                for e in range(2):
                    hh = 2 * c + e
                    pe.wait_ge(p_ready, hh + 1)
                    for x in range(2 * NT - 1):
                        n, half = (x + 1) // 2, (x + 1) % 2
                        last = nc.tensor.transpose(aps[:, 2 * e + x // 4, (x % 4) * P:(x % 4 + 1) * P],
                                                   scores[:, e, n, half * P:(half + 1) * P], ident[:])
                    last.then_inc(pt_full, 1)
                for e in range(2):
                    pe.wait_ge(pt_ready, 2 * c + e + 1)
                    g = 2 * (c // 4) + e
                    for n in range(NT):
                        tiles = [(n, 0)] if n == 0 else [(n - 1, 2 * n - 1), (n, 2 * n)]
                        for m, (kb, x) in enumerate(tiles):
                            last = mm(gps[e * HD:(e + 1) * HD, (c + 3) % SLOTS, n * P:(n + 1) * P], vtok[:, kb, g * HD:(g + 1) * HD],
                                      pT[:, e, x, :], start=m == 0, stop=m == len(tiles) - 1)
                last.then_inc(o_full, 1)

            for c in range(KC):
                if c >= 3:
                    pe.wait_ge(o_lo, c - 2)
                dense(START["q"] + c // SLOTS, c % SLOTS, xa, operand=x_wait(X_Q) if c == 0 else None)
                if c >= 1:
                    band_values(c - 1)
                band_scores(c)
            for j in range(2):
                pe.wait_ge(o_lo, KC - 2 + j)
                dense(START["w_o"], j, xb, operand=lambda k: pe.wait_ge(o_lo, k + 1), part=(0, KC - 1))
            band_values(KC - 1)
            for j in range(2):
                dense(START["w_o"], j, xb, operand=lambda k: pe.wait_ge(o_lo, k + 1), part=(KC - 1, KC))
            layer("w_o", xb, first=2)
            ffn(1, X_FF1, RMS_FF1, xa, xb)
            sum_running(RMS_LAST)



def chunk(w):
    blocks = w.shape[0] // P
    out = np.zeros((P, KC * P), np.float32)
    out[:, :blocks * P] = w.reshape(blocks, P, P).transpose(1, 0, 2).reshape(P, blocks * P)
    return out


def head_order():
    group = AH // KVH
    return [(2 * (c // group) + e) * group + c % group for c in range(KC) for e in range(2)]


def weight_stream(w_ada, w_in, w_out, pw1, pw2, w_kv, w_q, w_o, up, down):
    def cols(w, c):
        return w[:, c * P:(c + 1) * P]

    def tokens(w, c):
        return [cols(w, c), cols(w, c + 1)]

    out = []
    hq, hf, hi, hz = 0, KC, 2 * KC, 3 * KC
    rq, rk = 4 * KC, 4 * KC + KC // 2
    rv, rz, ga, gb = (5 * KC + n * KC for n in range(4))
    for p in range(PAIRS):
        a, b = 2 * p, 2 * p + 1
        out += [cols(w_in, hf + a), cols(w_in, hf + b), cols(w_in, hq + a), cols(w_in, hq + b)]
        out += tokens(w_in, hi + a) + [cols(w_in, rq + p), cols(w_in, rk + p)] + tokens(w_in, rv + a)
        out += [cols(w_ada, 2 * KC + a), cols(w_ada, 2 * KC + b)]
        for z, g in ((hz, ga), (rz, gb)):
            out += [cols(w_in, z + a), cols(w_in, z + b), cols(w_in, g + a), cols(w_in, g + b)]
    out += [cols(w_out, c) for c in range(KC)]
    for c in range(KC):
        out += [cols(pw1, c), cols(pw1, KC + c)]
    out += [cols(pw2, c) for c in range(KC)]
    heads = head_order()
    for layer in range(2):
        if layer == 1:
            out += [cols(w_kv, c) for c in range(4)]
            wq = w_q.reshape(D, AH, HD)[:, heads].reshape(D, D)
            wo = w_o.reshape(AH, HD, D)[heads].reshape(D, D)
            out += [cols(wq, c) for c in range(KC)] + [cols(wo, c) for c in range(KC)]
        f = 0
        for n in FF_PARTS:
            for c in range(f, f + n):
                out += [cols(up[layer], c), cols(up[layer], FF_CHUNKS + c)]
            out += [cols(down[layer][f * P:(f + n) * P], c) for c in range(KC)]
            f += n
    assert len(out) == QUADS * SLOTS
    return np.stack([chunk(w) for w in out])


def ada_chunks(w_ada):
    order = list(range(KC, 2 * KC)) + list(range(KC))
    return np.stack([np.ascontiguousarray(w_ada[:, c * P:(c + 1) * P].T) for c in order])


def shape_constants():
    lin = np.linspace(0.0, 1.0, RET_DK // 2, dtype=np.float32)
    inv = (np.float32(1.0) / np.power(np.float32(10000.0), lin)).astype(np.float32)
    ang = (np.arange(T, dtype=np.float32)[:, None] * inv[None, :]).astype(np.float32)
    cos, sin = (np.tile(f(ang.astype(np.float64)).T, (2, 1)) for f in (np.cos, np.sin))
    tab = np.zeros((PAIRS, P, 4, T))
    t = np.arange(T)
    for h in range(HEADS):
        rows = slice((h % 2) * RET_DK, (h % 2 + 1) * RET_DK)
        gamma = 1.0 - 2.0 ** (-5.0 - h)
        tab[h // 2, rows, 0], tab[h // 2, rows, 1] = cos * gamma ** t, sin * gamma ** t
        back = gamma ** (-t) * RET_DK ** -0.5
        tab[h // 2, rows, 2], tab[h // 2, rows, 3] = cos * back, sin * back
    rot = np.zeros((P, P), np.float32)
    half = RET_DK // 2
    for o in (0, RET_DK):
        for i in range(half):
            rot[o + half + i, o + i] = -1.0
            rot[o + i, o + half + i] = 1.0
    lvl = np.zeros((P, LEVELS, P // 2), np.int32)
    for level in range(LEVELS):
        size = P >> level
        right = [t for t in range(P) if t % size >= size // 2]
        for x, t_ in enumerate(right):
            for s in range(t_ // size * size, t_ // size * size + size // 2):
                lvl[s, level, x] = 1
    tri = (np.arange(T)[None, :] >= np.arange(P)[:, None]).astype(np.float32)
    hot = np.zeros((33, REACH + 1), np.float32)
    exact = 16
    for u in range(REACH + 1):
        d = BAND - 1 - u
        if not 0 <= d < P:
            hot[32, u] = 1.0
            continue
        log = np.float32(np.log(np.float32(max(d, 1)) / np.float32(exact))) / np.float32(np.log(P / exact))
        large = min(exact + int(np.float32(log * np.float32(32 - exact))), 31)
        hot[d if d < exact else large, u] = 1.0
    return {"rot": rot, "ret_tab": tab.astype(np.float32), "lvl": lvl.reshape(P, -1), "eye": np.eye(P, dtype=np.int32),
            "tri": tri, "hot": hot, "ident": np.eye(P, dtype=np.float32)}


def kernel(**inputs):
    import concourse.bacc as bacc
    from concourse.bass_utils import run_bass_kernel_spmd

    a = {k: np.asarray(v) for k, v in inputs.items()}
    columns = {
        "norm_g": a["norm_g"], "b_ada": a["b_ada"], "lb0": a["hg_lb_logits"][0], "lb1": a["hg_lb_logits"][1],
        "hg_norm_g": a["hg_norm_g"], "ret_norm_g": a["ret_norm_g"], "norm_mix": a["norm_mix_2"],
        "norm_ffn": a["norm_ffn_2"], "b_pw1": a["conv_b_pw1_2"], "w_dw": a["conv_w_dw_2"], "b_dw": a["conv_b_dw_2"],
        "ln_g": a["conv_ln_g_2"], "ln_b": a["conv_ln_b_2"], "b_pw2": a["conv_b_pw2_2"], "norm_kv": a["norm_kv_2"],
        "norm_final": a["norm_final_2"], "final_g": a["final_g"], "c": a["c"],
    }
    heads = head_order()
    arrays = {
        "weights": weight_stream(a["w_ada"][0], a["w_in"][0], a["w_out"][0], a["conv_w_pw1_2"][0], a["conv_w_pw2_2"][0],
                                 a["w_kv_2"], a["w_q_2"][0], a["w_o_2"][0], a["ffn_w_up_2"], a["ffn_w_down_2"]),
        "ada_in": ada_chunks(a["w_ada"][0]),
        "c_in": np.ascontiguousarray(a["c"].reshape(1, D)),
        "xT": np.ascontiguousarray(a["x"][0].T),
        "vec_in": np.ascontiguousarray(np.concatenate([columns[n].reshape(-1) for n in VEC]).reshape(VECS, P).T),
        "sinks_in": np.ascontiguousarray(a["sinks_2"].reshape(1, AH)[:, heads]),
        "rel_in": np.ascontiguousarray(a["rel_bias_2"][:, heads]),
    }
    arrays |= {f"{k}_in" if k != "ret_tab" else k: v for k, v in shape_constants().items()}
    nc = bacc.Bacc("TRN2", target_bir_lowering=False, num_devices=1)
    aps = {k: nc.dram_tensor(f"{k}_dram", v.shape, mybir.dt.from_np(v.dtype), kind="ExternalInput").ap()
           for k, v in arrays.items()}
    scratch = nc.dram_tensor("rel_scratch_dram", (AH, P, REACH + 1), F32, kind="Internal").ap()
    outT = nc.dram_tensor("outT_dram", (D, T), F32, kind="ExternalOutput").ap()
    program(nc, rel_scratch=scratch, outT=outT, **aps)
    r = run_bass_kernel_spmd(nc, [{f"{k}_dram": v for k, v in arrays.items()}], core_ids=[0])
    return np.ascontiguousarray(np.asarray(r.results[0]["outT_dram"]).T)[None]
```

```python
from contextlib import ExitStack

import numpy as np
import concourse.bass as bass
from concourse import mybir

F32 = mybir.dt.float32
F32R = mybir.dt.float32r
I32 = mybir.dt.int32
ACT = mybir.ActivationFunctionType
ALU = mybir.AluOpType

P = 128
T = 512
D = 1024
KC = D // P
NT = T // P
SLOTS = 4
EPS = 1e-6

HEADS = 8
PAIRS = HEADS // 2
LEVELS = 7
TINY = 1e-19
RET_DK = 64
ROT_HALF = RET_DK // 2

TAPS = 31
PAD = TAPS - 1
FF_CHUNKS = 22
FF_PARTS = (8, 8, 6)
AH = 16
KVH = 4
HD = 64
BAND = 256
REACH = 383
NEG = -1e30

ADA_CHUNKS = 2 * KC
DVE_CONV = 5
GLU_LOOP = DVE_CONV // 2
PE_CONV = KC - DVE_CONV
TAP_GROUP = 8
TAP_GROUPS = -(-TAPS // TAP_GROUP)

PAIR_CHUNKS = 20
GATE_CHUNKS = (8, 9)


def first_group(m):
    return 1 if m == PE_CONV - 1 else 0


def phase_starts():
    sizes = [("pairs", PAIRS * PAIR_CHUNKS), ("w_out", KC), ("pw1", 2 * KC), ("pw2", KC)]
    for layer in range(2):
        if layer == 1:
            sizes += [("kv", 4), ("q", KC), ("w_o", KC)]
        for part, n in enumerate(FF_PARTS):
            sizes += [(f"up{layer}{part}", 2 * n), (f"down{layer}{part}", KC)]
    at, starts = 0, {}
    for name, n in sizes:
        assert n % SLOTS == 0
        starts[name] = at
        at += n // SLOTS
    return starts, at


START, QUADS = phase_starts()

VEC = {}
_at = 0
for _name, _n in (("norm_g", KC), ("b_ada", 3 * KC), ("lb0", KC), ("lb1", KC), ("hg_norm_g", KC),
                  ("ret_norm_g", KC), ("norm_mix", 2 * KC), ("norm_ffn", 2 * KC), ("b_pw1", 2 * KC),
                  ("w_dw", TAPS * KC), ("b_dw", KC), ("ln_g", KC), ("ln_b", KC), ("b_pw2", KC),
                  ("norm_kv", KC), ("norm_final", KC), ("final_g", KC), ("c", KC)):
    VEC[_name] = _at
    _at += _n
VECS = _at
CONSTS = 16 * 5
LN = "natural_log"
PAIR_STEPS = 39
FIRST_LOW = 2
LAST_LOW = 2


class Steps:

    def __init__(self, eng, sem):
        self.eng, self.sem = eng, sem
        self.base, self.local, self.i, self.per = 0, 0, None, 0

    def enter(self, i, per):
        self.base, self.local, self.i, self.per = self.base + self.local, 0, i, per

    def leave(self, trips):
        assert self.local == self.per, (self.local, self.per)
        self.base, self.local, self.i, self.per = self.base + trips * self.per, 0, None, 0

    def mark(self, ins):
        ins.then_inc(self.sem, 1)
        self.local += 1
        return self.local

    def wait(self, local=None):
        v = self.base + (self.local if local is None else local)
        self.eng.wait_ge(self.sem, v if self.i is None else self.i * self.per + v)

    def done(self, ins):
        self.mark(ins)
        self.wait()


def program(nc, weights, ada_in, c_in, xT, vec_in, sinks_in, rel_in, ret_tab, lvl_in, eye_in, tri_in, hot_in, ident_in,
            rel_scratch, outT):
    ctx = ExitStack()
    with ctx:
        def sb(name, shape, dt=F32, where=ctx):
            return where.enter_context(nc.sbuf_tensor(name, shape, dt))

        def sem(name):
            return ctx.enter_context(nc.semaphore(name))

        w_raw = sb("w_raw", [P, SLOTS, D])
        w_hi = sb("w_hi", [P, SLOTS, D], F32R)
        w_lo = sb("w_lo", [P, SLOTS, D], F32R)
        xa_mem = ExitStack()
        diag_hi = sb("diag_hi", [P, TAP_GROUPS * TAP_GROUP, P], F32R, where=xa_mem)
        low_mem = ExitStack()
        diag_lo = sb("diag_lo", [P, TAP_GROUPS * TAP_GROUP, P], F32R, where=low_mem)
        low_mem.close()
        x0 = sb("x0", [P, KC, T], where=xa_mem)
        xa_mem.close()
        xa_hi = sb("xa_hi", [P, KC, T], F32R)
        xa_lo = sb("xa_lo", [P, KC, T], F32R)
        vec = sb("vec", [P, VECS])
        ones = sb("ones", [P, P])
        ident = sb("ident", [P, P])
        eps_col = sb("eps_col", [P, 1])
        mod = sb("mod", [P, 3 * KC])
        conv_gain = sb("conv_gain", [P, KC])
        r_col = sb("r_col", [P, 2, NT])
        sq = sb("sq", [P, 2, T])
        lnv = sb("lnv", [P, T])
        rstd = sb("rstd", [P, T])
        hbuf = sb("hbuf", [P, 4, T])
        sink = sb("sink", [P, AH])
        neg_max = sb("neg_max", [P, 2, NT])
        row_max = sb("row_max", [P, 2, NT])
        row_sum = sb("row_sum", [P, 2, NT])
        row_inv = sb("row_inv", [P, 2, NT])
        sink_exp = sb("sink_exp", [P, 2, NT])

        first = ExitStack()
        reset = sb("reset", [P, T], where=first)
        tri = sb("tri", [P, T], where=first)
        lvl_mask = sb("lvl_mask", [P, LEVELS, P // 2], I32, where=first)
        eye_mask = sb("eye_mask", [P, P], I32, where=first)
        lower = sb("lower", [P, KC], where=first)
        one_minus = sb("one_minus", [P, KC], where=first)
        mix_gain = sb("mix_gain", [P, KC], where=first)
        lbt = sb("lbt", [P, 4, KC], where=first)
        gate_sum = sb("gate_sum", [P, 2], where=first)
        ada_mem = ExitStack()
        ada_w = sb("ada_w", [P, ADA_CHUNKS, D], where=ada_mem)
        c_wide = sb("c_wide", [P, 2, D], where=ada_mem)
        ada_mem.close()
        mixed = sb("mixed", [P, KC, T], where=first)
        kt = sb("kt", [P, LEVELS, T], where=first)
        qt = sb("qt", [P, LEVELS, T // 2], where=first)
        q = sb("q", [P, 2, T], where=first)
        key = sb("key", [P, 2, T], where=first)
        cum = sb("cum", [P, 2, T], where=first)
        forget = sb("forget", [P, 2, T], where=first)
        q_far = sb("q_far", [P, 6, P], where=first)
        k_far = sb("k_far", [P, 3, P], where=first)
        val = sb("val", [P, NT, 2, 2 * P], where=first)
        rqk = sb("rqk", [P, 2, T], where=first)
        gates = sb("gates", [P, 4, T], where=first)
        unit = sb("unit", [P, 2, T], where=first)
        at_h = sb("at_h", [P, NT * (T + P)], where=first)
        at_r = sb("at_r", [P, NT * (T + P)], where=first)
        first.close()

        second = ExitStack()
        xb_hi = sb("xb_hi", [P, KC, T], F32R, where=second)
        xb_lo = sb("xb_lo", [P, KC, T], F32R, where=second)
        res = sb("res", [P, KC, T], where=second)
        bias = sb("bias", [P, AH, BAND], where=second)
        conv_mem = ExitStack()
        glu = sb("glu", [P, KC, PAD + T], where=conv_mem)
        early_mem = ExitStack()
        hot = sb("hot", [33, REACH + 1], where=early_mem)
        rel = sb("rel", [33, AH], where=early_mem)
        rel_rows = sb("rel_rows", [AH, REACH + 1], where=early_mem)
        early_mem.close()
        glu_hi = sb("glu_hi", [P, 2, PAD + T], F32R, where=conv_mem)
        glu_lo = sb("glu_lo", [P, 2, PAD + T], F32R, where=conv_mem)
        tap_hi = sb("tap_hi", [P, TAP_GROUPS * TAP_GROUP, PE_CONV], F32R, where=conv_mem)
        tap_lo = sb("tap_lo", [P, TAP_GROUPS * TAP_GROUP, PE_CONV], F32R, where=conv_mem)
        conv = sb("conv", [P, KC, T], where=conv_mem)
        conv_mem.close()
        attn_mem = ExitStack()
        kT = sb("kT", [P, 2, T], where=attn_mem)
        vtok = sb("vtok", [P, NT, KVH * HD], where=attn_mem)
        qT = sb("qT", [P, 2, T], where=attn_mem)
        scores = sb("scores", [P, 2, NT, BAND], where=attn_mem)
        pT = sb("pT", [P, 2, 2 * NT - 1, P], where=attn_mem)
        attn_mem.close()
        end_mem = ExitStack()
        y = sb("y", [P, KC, T], where=end_mem)
        end_mem.close()
        second.close()

        gps = ctx.enter_context(nc.psum_tensor("gps", [P, SLOTS, T], F32))
        aps = ctx.enter_context(nc.psum_tensor("aps", [P, 4, T], F32))

        raw_in = [sem(f"raw_in{j}") for j in range(SLOTS)]
        hi_ready = [sem(f"hi_ready{j}") for j in range(SLOTS)]
        lo_ready = [sem(f"lo_ready{j}") for j in range(SLOTS)]
        tile_done = [sem(f"tile_done{j}") for j in range(SLOTS)]
        evicted = [sem(f"evicted{j}") for j in range(SLOTS)]
        bank_full = [sem(f"bank_full{b}") for b in range(4)]
        taken = [sem(f"taken{b}") for b in range(4)]
        act_own = sem("act_own")
        dve_own = sem("dve_own")
        consts_in = sem("consts_in")
        vec_loaded = sem("vec_loaded")
        c_loaded = sem("c_loaded")
        ada_loaded = [sem(f"ada_loaded{n}") for n in range(KC)]
        c_wide_ready = sem("c_wide_ready")
        x_in = [sem(f"x_in{n}") for n in range(2)]
        tabs_in = sem("tabs_in")
        res_in = sem("res_in")
        hot_in_sem = sem("hot_in_sem")
        made = sem("made")
        lb_shift = sem("lb_shift")
        lb_exp = sem("lb_exp")
        sq_ready = sem("sq_ready")
        sq_used = sem("sq_used")
        double_ready = sem("double_ready")
        second_ready = sem("second_ready")
        both_ready = sem("both_ready")
        sum_done = sem("sum_done")
        rstd_ready = sem("rstd_ready")
        h_ready = sem("h_ready")
        xh_ready = sem("xh_ready")
        x_ready = sem("x_ready")
        f_ready = sem("f_ready")
        logf_ready = sem("logf_ready")
        q_sig = sem("q_sig")
        exps_ready = sem("exps_ready")
        decay_ready = sem("decay_ready")
        prep_done = sem("prep_done")
        rot_ready = sem("rot_ready")
        passed = sem("passed")
        osq_ready = sem("osq_ready")
        hnorm = sem("hnorm")
        gate_sig = sem("gate_sig")
        gates_used = sem("gates_used")
        mixed_ready = sem("mixed_ready")
        m_hi = sem("m_hi")
        m_lo = sem("m_lo")
        rel_full = sem("rel_full")
        rel_copied = sem("rel_copied")
        rel_out = sem("rel_out")
        bias_in = sem("bias_in")
        scaled = sem("scaled")
        sig_ready = sem("sig_ready")
        glu_ready = sem("glu_ready")
        glu_high = sem("glu_high")
        glu_low = sem("glu_low")
        taps_high = sem("taps_high")
        taps_ready = sem("taps_ready")
        diag_ready = sem("diag_ready")
        diag_used = sem("diag_used")
        conv_full = sem("conv_full")
        conv_copied = sem("conv_copied")
        conv_done = sem("conv_done")
        conv_sum = sem("conv_sum")
        mean_done = sem("mean_done")
        center_done = sem("center_done")
        s_full = sem("s_full")
        max_ready = sem("max_ready")
        exp_ready = sem("exp_ready")
        p_ready = sem("p_ready")
        pt_full = sem("pt_full")
        pt_ready = sem("pt_ready")
        o_full = sem("o_full")
        o_hi = sem("o_hi")
        o_lo = sem("o_lo")
        silu_ready = sem("silu_ready")
        ff_ready = sem("ff_ready")
        ff_hi = sem("ff_hi")
        ff_lo = sem("ff_lo")
        y_ready = sem("y_ready")
        out_done = sem("out_done")

        def vcol(name, c=0):
            return vec[:, VEC[name] + c:VEC[name] + c + 1]

        def vdyn(name, c):
            return vec[:, bass.ds(c + VEC[name], 1)]

        def diag(at):
            return at[:, :].rearrange("p (t s) -> p t s", s=T + P)[:, :, 0:P]

        def halves(ap, level):
            size = P >> level
            v = ap.rearrange("p (n s) -> p n s", s=size)
            h = size // 2
            return v[:, :, 0:h], v[:, :, h:size], v[:, :, h - 1:h].to_broadcast([P, T // size, h])

        FAR = ((0, 0, 3), (1, 3, 5), (2, 5, 6))
        LEVEL_BANKS = ((0, 1), (2, 3), (4, 5), (6,))
        PREP_SPLIT = 2
        RMS_MIX, RMS_FIRST, RMS_LN, RMS_FF0, RMS_ATTN, RMS_FF1, RMS_LAST = range(7)
        SUMS = {}
        USED = {}
        for n in range(7):
            SUMS[n] = SUMS.get(n - 1, 0) + (KC if n in (RMS_MIX, RMS_LN) else 1)
            USED[n] = USED.get(n - 1, 0) + (KC - 2 if n - 1 in (RMS_FIRST, RMS_FF0, RMS_ATTN, RMS_FF1) else 0)
        X_MIX, X_CONV_IN, X_PW2, X_FF0, X_KV, X_Q, X_FF1 = range(7)
        U_LV = (0, 15)
        U_SC = (7, 22)
        U_AV = ((11, 12), (26, 27))
        U_NORM = ((13, 14), (28, 29))
        USES = (8, 8, 7, 7)

        block = ctx.enter_context(nc.Block())

        @block.sync
        def _(sp):
            def load(I, j):
                sp.dma_start(w_raw[:, j, :], weights[bass.ds(I * SLOTS + j, 1)].rearrange("a p c -> p (a c)"))\
                  .then_inc(raw_in[j], 16)

            for c in range(KC):
                if c < 2:
                    k = slice(c * KC // 2, (c + 1) * KC // 2)
                    sp.dma_start(x0[:, k, :], xT.rearrange("(k p) t -> p k t", p=P)[:, k, :]).then_inc(x_in[c], 16)
                sp.dma_start(ada_w[:, 2 * c:2 * c + 2, :], ada_in[2 * c:2 * c + 2].rearrange("c p k -> p c k"))\
                  .then_inc(ada_loaded[c], 16)
                if 2 <= c < 5:
                    load(0, c - 2)
            load(0, 3)
            sp.dma_start(ident[:], ident_in).then_inc(consts_in, 16)
            sp.dma_start(lvl_mask[:], lvl_in.rearrange("p (l c) -> p l c", l=LEVELS)).then_inc(consts_in, 16)
            sp.dma_start(eye_mask[:], eye_in).then_inc(consts_in, 16)
            sp.dma_start(tri[:], tri_in).then_inc(consts_in, 16)
            sp.dma_start(sink[:], sinks_in.to_broadcast([P, AH])).then_inc(consts_in, 16)
            with sp.Fori(1, QUADS) as i:
                for j in range(SLOTS):
                    sp.wait_ge(lo_ready[j], i + 1)
                    load(i, j)
            for c in range(KC):
                sp.wait_ge(y_ready, c + 1)
                sp.dma_start(outT[c * P:(c + 1) * P, :], y[:, c, :]).then_inc(out_done, 16)
            sp.wait_ge(out_done, 16 * KC)

        @block.gpsimd
        def _(pool):
            TT = nc.gpsimd.tensor_tensor
            for j in range(SLOTS):
                pool.sem_inc(lo_ready[j], 1)

            def w_low(I, j):
                pool.wait_ge(hi_ready[j], I + 1)
                TT(w_lo[:, j, :], w_raw[:, j, :], w_hi[:, j, :].bitcast(F32), ALU.subtract).then_inc(lo_ready[j], 1)

            for c in range(KC - LAST_LOW):
                if c < 3:
                    w_low(0, c)
                pool.wait_ge(xh_ready, c + 1)
                TT(xa_lo[:, c, :], hbuf[:, c % 4, :], xa_hi[:, c, :].bitcast(F32), ALU.subtract).then_inc(x_ready, 1)
            with pool.Fori(0, PAIRS) as p:
                for c in range(SLOTS - 1, PAIR_CHUNKS + SLOTS - 1):
                    if c not in GATE_CHUNKS:
                        w_low(p * (PAIR_CHUNKS // SLOTS) + (START["pairs"] + c // SLOTS), c % SLOTS)
            for c in range(FIRST_LOW):
                pool.wait_ge(m_hi, c + 1)
                TT(xa_lo[:, c, :], mixed[:, c, :], xa_hi[:, c, :].bitcast(F32), ALU.subtract).then_inc(m_lo, 1)
            w_low(START["w_out"], 3)
            with pool.Fori(START["w_out"] + 1, START["pw1"]) as i:
                for j in range(SLOTS):
                    w_low(i, j)
            for j in range(3):
                w_low(START["pw1"], j)

            def scale(I, n, c):
                at = bass.ds(c, 1)
                pool.wait_ge(evicted[2 * n + 1], I + 2)
                pool.sem_inc(passed, 1)
                TT(glu[:, at, PAD:], glu[:, at, PAD:], lnv[:, None, :], ALU.mult)
                TT(conv[:, at, :], conv[:, at, :], lnv[:, None, :], ALU.mult).then_inc(scaled, 1)

            def diagonals(g, m):
                k = slice(g * TAP_GROUP, (g + 1) * TAP_GROUP) if isinstance(g, int) else bass.ds(g * TAP_GROUP, TAP_GROUP)
                shape = [P, TAP_GROUP, P]
                for diag, tap in ((diag_hi, tap_hi), (diag_lo, tap_lo)):
                    last = TT(diag[:, k, :], ident[:, None, :].to_broadcast(shape),
                              tap[:, k, m:m + 1].bitcast(F32).to_broadcast(shape), ALU.mult)
                last.then_inc(diag_ready, 1)

            with pool.Fori(0, GLU_LOOP) as i:
                I = i + START["pw1"]
                w_low(I, 3)
                w_low(I + 1, 0)
                pool.wait_ge(both_ready, 1)
                pool.wait_ge(taps_ready, 1)
                scale(I, 0, i * 2)
                w_low(I + 1, 1)
                w_low(I + 1, 2)
                scale(I, 1, i * 2 + 1)
                diagonals(i, 0)
            I = START["pw1"] + GLU_LOOP

            def product(m):
                c = DVE_CONV + m
                pool.wait_ge(sig_ready, c + 1)
                TT(glu[:, c, PAD:], glu[:, c, PAD:], conv[:, c, :], ALU.mult).then_inc(glu_ready, 1)

            def low(m):
                pool.wait_ge(glu_high, m + 1)
                TT(glu_lo[:, m % 2, :], glu[:, DVE_CONV + m, :], glu_hi[:, m % 2, :].bitcast(F32), ALU.subtract)\
                    .then_inc(glu_low, 1)

            w_low(I, 3)
            w_low(I + 1, 0)
            scale(I, 0, DVE_CONV - 1)
            w_low(I + 1, 1)
            w_low(I + 1, 2)
            scale(I, 1, DVE_CONV)
            product(0)
            w_low(I + 1, 3)
            w_low(I + 2, 0)
            scale(I + 1, 0, DVE_CONV + 1)
            low(0)
            product(1)
            diagonals(GLU_LOOP, 0)
            w_low(I + 2, 1)
            w_low(I + 2, 2)
            scale(I + 1, 1, DVE_CONV + 2)
            for g in range(GLU_LOOP + 1, TAP_GROUPS):
                diagonals(g, 0)
            low(1)
            product(2)
            for m in range(1, PE_CONV):
                for g in range(first_group(m), TAP_GROUPS):
                    if g < TAP_GROUPS - 1:
                        pool.wait_ge(diag_used, (m - 1) * (TAP_GROUPS - 1) + g + 1)
                    else:
                        pool.wait_ge(conv_full, m)
                    diagonals(g, m)
                if m == 1:
                    low(PE_CONV - 1)
            total = hbuf[:, 3, :]
            pool.wait_ge(conv_done, GLU_LOOP)
            last = range(DVE_CONV - 2, DVE_CONV)
            for n, c in enumerate([c for c in range(1, KC - 1) if c not in last] + list(last)):
                if c >= DVE_CONV:
                    pool.wait_ge(conv_copied, c - DVE_CONV + 1)
                elif c == last[0]:
                    pool.wait_ge(conv_done, 1 + GLU_LOOP)
                if n > 0:
                    pool.wait_ge(conv_sum, n)
                TT(total, conv[:, 0, :] if n == 0 else total, conv[:, c, :], ALU.add).then_inc(conv_sum, 1)
            w_low(START["pw2"], 3)
            with pool.Fori(START["pw2"] + 1, QUADS) as i:
                for j in range(SLOTS):
                    w_low(i, j)

        @block.scalar
        def _(act):
            own = Steps(act, act_own)

            def w_high(I, j):
                act.wait_ge(raw_in[j], I * 16 + 16)
                act.wait_ge(tile_done[j], I + 1)
                nc.scalar.copy(w_hi[:, j, :], w_raw[:, j, :]).then_inc(hi_ready[j], 1)

            def ahead(I, j):
                if not isinstance(I, int) or I * SLOTS + j + 3 < QUADS * SLOTS:
                    w_high(I + (j + 3) // SLOTS, (j + 3) % SLOTS)

            def full(I, j):
                act.wait_ge(tile_done[j], I + 2)
                return gps[:, j, :]

            def tables():
                nc.scalar.preload_act_table_set(LN)

            def rms_square(n, c, src):
                if c >= 2:
                    act.wait_ge(sum_done, SUMS[n] - KC + c - 1)
                nc.scalar.activation(sq[:, c % 2, :], src, ACT.Square).then_inc(sq_ready, 1)

            def rms_finish(n):
                act.wait_ge(sum_done, SUMS[n])
                own.done(nc.scalar.activation(lnv[:], aps[:, 0, :], ACT.Ln, bias=eps_col[:], scale=1.0 / D))
                nc.scalar.activation(rstd[:], lnv[:], ACT.Exp, scale=-0.5).then_inc(rstd_ready, 1)

            def gain_high(dst, c, gain):
                nc.scalar.mul(dst[:, c, :], res[:, c, :], gain(c)).then_inc(xh_ready, 1)

            act.dma_start(c_wide[:, 0, :], c_in.to_broadcast([P, D])).then_inc(c_loaded, 16)
            act.dma_start(vec[:], vec_in).then_inc(vec_loaded, 16)

            nc.scalar.preload_act_table(ACT.Sigmoid)
            for c in range(KC):
                if c % (KC // 2) == 0:
                    act.wait_ge(x_in[c // (KC // 2)], 16)
                rms_square(RMS_MIX, c, x0[:, c, :])
                if c == KC // 2 - 1:
                    act.wait_ge(c_loaded, 16)
                    nc.scalar.activation(c_wide[:, 1, :], c_wide[:, 0, :], ACT.Sigmoid).then_inc(c_wide_ready, 1)
            tables()
            act.wait_ge(made, 1)
            rms_finish(RMS_MIX)
            act.wait_ge(lb_shift, 1)
            nc.scalar.activation(lbt[:, 2:4, :], lbt[:, 0:2, :], ACT.Exp).then_inc(lb_exp, 1)
            for c in range(KC):
                if c < 3:
                    w_high(0, c)
                act.wait_ge(h_ready, c + 1)
                own.done(nc.scalar.activation(hbuf[:, c % 4, :], hbuf[:, c % 4, :], ACT.Identity, bias=mod[:, c:c + 1]))
                nc.scalar.copy(xa_hi[:, c, :], hbuf[:, c % 4, :]).then_inc(xh_ready, 1)

            with act.Fori(0, PAIRS) as p:
                def at(c):
                    return p * (PAIR_CHUNKS // SLOTS) + (START["pairs"] + c // SLOTS)

                def chunk(c):
                    ahead(at(c), c % SLOTS)
                    return full(at(c), c % SLOTS)

                def bank(u):
                    act.wait_ge(bank_full[u % 4], p * USES[u % 4] + (u // 4 + 1))
                    return aps[:, u % 4, :]

                def decays(e):
                    act.wait_ge(exps_ready, p * 2 + (e + 1))
                    nc.scalar.activation(kt[:], kt[:], ACT.Exp)
                    nc.scalar.activation(hbuf[:, 0, :], hbuf[:, 0, :], ACT.Exp)
                    nc.scalar.activation(hbuf[:, 1, :], cum[:, e, :], ACT.Exp).then_inc(decay_ready, 1)

                def far_scores(e):
                    u = U_LV[e] + 5
                    nc.scalar.copy(at_h[:, P:T], bank(u)[:, 0:3 * P]).then_inc(taken[u % 4], 1)
                    b = bank(u + 1)
                    nc.scalar.copy(at_h[:, T + 2 * P:2 * T], b[:, 0:2 * P])
                    nc.scalar.copy(at_h[:, 2 * T + 3 * P:3 * T], b[:, 2 * P:3 * P]).then_inc(taken[(u + 1) % 4], 1)

                def head_square(e, r):
                    nc.scalar.activation(hbuf[:, 2 + r, :], bank(U_AV[e][r]), ACT.Square).then_inc(osq_ready, 1)

                def head_rstd(e):
                    for r, dst in enumerate((lnv, rstd)):
                        u = U_NORM[e][r]
                        if e:
                            uo = U_AV[0][r]
                            act.wait_ge(taken[uo % 4], p * USES[uo % 4] + (uo // 4 + 2))
                        nc.scalar.activation(dst[:], bank(u), ACT.Ln, bias=eps_col[:], scale=1.0 / P)\
                            .then_inc(taken[u % 4], 1)
                    for r, dst in enumerate((lnv, rstd)):
                        u = U_NORM[e][r]
                        act.wait_ge(taken[u % 4], p * USES[u % 4] + (u // 4 + 2))
                        nc.scalar.activation(dst[:], dst[:], ACT.Exp, scale=-0.5).then_inc(hnorm, 1)

                for e in range(2):
                    nc.scalar.activation(forget[:, e, :], chunk(e), ACT.Sigmoid).then_inc(evicted[e], 1)
                act.wait_ge(gates_used, p * 4 + 1)
                for e in range(2):
                    nc.scalar.activation(sq[:, e, :], chunk(2 + e), ACT.Sigmoid).then_inc(q_sig, 1)
                tables()
                act.wait_ge(f_ready, p + 1)
                nc.scalar.activation(forget[:], forget[:], ACT.Ln).then_inc(logf_ready, 1)
                act.wait_ge(mixed_ready, p * 2 + 1)
                act.dma_start(gates[:], ret_tab[bass.ds(p, 1)].rearrange("a p n t -> p (a n) t")).then_inc(tabs_in, 16)
                ahead(at(4), 0)
                decays(0)

                def values(c, r):
                    full(at(c + 1), (c + 1) % SLOTS)
                    act.sem_inc(tile_done[c % SLOTS], 1)
                    for n in range(2):
                        b = gps[:, (c + n) % SLOTS, :]
                        nc.scalar.copy(val[:, 2 * n:2 * n + 2, r, :], b.rearrange("p (t v) -> p t v", t=2))\
                          .then_inc(evicted[(c + n) % SLOTS], 1)

                values(4, 0)
                for n in range(2):
                    b = full(at(6 + n), 2 + n)
                    nc.scalar.copy(rqk[:, n, :], b)
                    for r in range(0, P, ROT_HALF):
                        o = r ^ ROT_HALF
                        last = nc.scalar.copy(unit[o:o + ROT_HALF, n, :], b[r:r + ROT_HALF, :])
                    last.then_inc(evicted[2 + n], 1)
                    ahead(at(7 + n), (7 + n) % SLOTS)
                ahead(at(9), 1)
                far_scores(0)
                ahead(at(10), 2)
                decays(1)
                values(10, 1)
                ahead(at(11), 3)

                def gate_product(c, e, first):
                    b = chunk(c) if c < PAIR_CHUNKS - 1 else full(at(c), c % SLOTS)
                    if first:
                        if c >= 16:
                            act.wait_ge(gates_used, p * 4 + (1 + e + 1))
                        nc.scalar.activation(sq[:, e, :], b, ACT.Sigmoid).then_inc(gate_sig, 1)
                    else:
                        act.wait_ge(evicted[(c - 2) % SLOTS], at(c - 2) + 2)
                        nc.scalar.activation(sq[:, e, :], b, ACT.Sigmoid).then_inc(evicted[c % SLOTS], 1)

                gate_product(12, 0, True)
                gate_product(13, 1, True)
                head_square(0, 0)
                gate_product(14, 0, False)
                head_square(0, 1)
                gate_product(15, 1, False)
                tables()
                head_rstd(0)
                gate_product(16, 0, True)
                far_scores(1)
                gate_product(17, 1, True)
                head_square(1, 0)
                head_square(1, 1)
                gate_product(18, 0, False)
                ahead(at(19), 3)
                tables()
                head_rstd(1)
                nc.scalar.preload_act_table(ACT.Sigmoid)
                gate_product(19, 1, False)

            act.dma_start(res[:], xT.rearrange("(k p) t -> p k t", p=P)).then_inc(res_in, 16)
            for c in range(KC):
                if c in (0, KC - 1):
                    act.wait_ge(mixed_ready, 2 * PAIRS + (0 if c == 0 else 1))
                nc.scalar.copy(xa_hi[:, c, :], mixed[:, c, :]).then_inc(m_hi, 1)
            act.dma_start(hot[:], hot_in).then_inc(hot_in_sem, 16)
            act.dma_start(rel[0:32, :], rel_in).then_inc(hot_in_sem, 16)
            taps = vec[:, VEC["w_dw"]:VEC["w_dw"] + TAP_GROUPS * TAP_GROUP * KC].rearrange("p (k c) -> p k c", c=KC)
            nc.scalar.copy(tap_hi[:], taps[:, :, DVE_CONV:]).then_inc(taps_high, 1)

            def residual(phase, n, gain=None, dst=None, double=None):
                tables()
                for c in range(KC):
                    ahead(START[phase] + c // SLOTS, c % SLOTS)
                    act.wait_ge(evicted[c % SLOTS], START[phase] + c // SLOTS + 2)
                    if gain is not None:
                        gain_high(dst, c, gain)
                    if c >= 2:
                        act.wait_ge(sq_used, USED[n] + max(1, c - 2))
                    square = nc.scalar.activation(sq[:, c % 2, :], res[:, c, :], ACT.Square)
                    if double is not None:
                        square = nc.scalar.activation(hbuf[:, c % 2, :], res[:, c, :], ACT.Square, scale=double(c))
                    square.then_inc(sq_ready, 1)

            residual("w_out", RMS_FIRST, lambda c: conv_gain[:, c:c + 1], xb_hi, lambda c: vcol("final_g", c))
            act.wait_ge(sum_done, SUMS[RMS_FIRST])
            own.done(nc.scalar.activation(lnv[:], aps[:, 0, :], ACT.Ln, bias=eps_col[:], scale=1.0 / D))
            nc.scalar.activation(rstd[:], lnv[:], ACT.Exp, scale=-0.5)
            nc.scalar.activation(sq[:, 0, :], lnv[:], ACT.Exp, scale=-1.0).then_inc(rstd_ready, 1)
            act.wait_ge(double_ready, 1)
            act.wait_ge(rstd_ready, RMS_FIRST + 1)
            own.done(nc.scalar.activation(lnv[:], sq[:, 1, :], ACT.Ln, bias=eps_col[:], scale=1.0 / D))
            nc.scalar.activation(sq[:, 0, :], lnv[:], ACT.Exp, scale=-0.5).then_inc(second_ready, 1)
            act.wait_ge(rel_copied, 2)
            act.dma_start(rel_scratch, rel_rows[:, None, :].to_broadcast([AH, P, REACH + 1])).then_inc(rel_out, 16)

            def glu_halves(I, n, c):
                ahead(I, 2 * n)
                ahead(I, 2 * n + 1)
                at = bass.ds(c, 1)
                full(I, 2 * n)
                nc.scalar.copy(glu[:, at, PAD:], gps[:, 2 * n:2 * n + 1, :]).then_inc(evicted[2 * n], 1)
                full(I, 2 * n + 1)
                nc.scalar.copy(conv[:, at, :], gps[:, 2 * n + 1:2 * n + 2, :]).then_inc(evicted[2 * n + 1], 1)

            def glu_gate(c):
                act.wait_ge(scaled, c + 1)
                gate = conv[:, bass.ds(c, 1), :]
                nc.scalar.activation(gate, gate, ACT.Sigmoid, bias=vdyn("b_pw1", c + KC)).then_inc(sig_ready, 1)

            with act.Fori(0, GLU_LOOP) as i:
                I = i + START["pw1"]
                for n in range(2):
                    glu_halves(I, n, i * 2 + n)
                    glu_gate(i * 2 + n)
            glu_halves(START["pw1"] + GLU_LOOP, 0, DVE_CONV - 1)
            glu_gate(DVE_CONV - 1)
            act.wait_ge(rel_out, 16)
            band = bass.AP(rel_scratch.tensor, P - 1, [[REACH, P], [P * (REACH + 1), AH], [1, BAND]])
            act.dma_start(bias[:], band).then_inc(bias_in, 16)

            def split_high(m):
                act.wait_ge(glu_ready, m + 1)
                nc.scalar.copy(glu_hi[:, m % 2, :], glu[:, DVE_CONV + m, :]).then_inc(glu_high, 1)

            for m in range(PE_CONV):
                c = DVE_CONV + m
                glu_halves(START["pw1"] + c // 2, c % 2, c)
                if m > 0:
                    split_high(m - 1)
                act.wait_ge(scaled, c + 1)
                value = glu[:, c, PAD:]
                nc.scalar.activation(value, value, ACT.Identity, bias=vcol("b_pw1", c))
                glu_gate(c)

            def conv_out(m):
                act.wait_ge(conv_full, m + 1)
                nc.scalar.activation(conv[:, DVE_CONV + m, :], aps[:, 2 + m % 2, :], ACT.Identity, bias=vcol("b_dw", DVE_CONV + m))\
                  .then_inc(conv_copied, 1)

            conv_out(0)
            split_high(PE_CONV - 1)
            conv_out(1)
            tables()
            for c in range(KC):
                act.wait_ge(center_done, c + 1)
                rms_square(RMS_LN, c, conv[:, c, :])
            rms_finish(RMS_LN)
            for c in range(KC):
                act.wait_ge(h_ready, KC + c + 1)
                nc.scalar.activation(conv[:, c, :], hbuf[:, c % 4, :], ACT.Silu, bias=vcol("ln_b", c))
                nc.scalar.activation(xa_hi[:, c, :], hbuf[:, c % 4, :], ACT.Silu, bias=vcol("ln_b", c))\
                  .then_inc(xh_ready, 1)
            ffn_gain = lambda layer: lambda c: vcol("norm_ffn", layer * KC + c)
            residual("pw2", RMS_FF0, ffn_gain(0), xb_hi)
            rms_finish(RMS_FF0)

            def ffn(layer, hidden, n_next, gain=None, dst=None):
                for part, n in enumerate(FF_PARTS):
                    f0 = layer * FF_CHUNKS + sum(FF_PARTS[:part])
                    with act.Fori(0, n // 2) as i:
                        I = i + START[f"up{layer}{part}"]
                        for m in range(2):
                            ahead(I, 2 * m)
                            act.wait_ge(evicted[2 * m], I + 2)
                            nc.scalar.activation(sq[:, m, :], sq[:, m, :], ACT.Silu).then_inc(silu_ready, 1)
                            ahead(I, 2 * m + 1)
                            act.wait_ge(ff_ready, i * 2 + (f0 + m + 1))
                            nc.scalar.copy(hidden[:, bass.ds(i * 2 + m, 1), :], hbuf[:, 2 * m:2 * m + 1, :]).then_inc(ff_hi, 1)
                    if part < len(FF_PARTS) - 1:
                        with act.Fori(0, KC // SLOTS) as i:
                            for j in range(SLOTS):
                                ahead(i + START[f"down{layer}{part}"], j)
                residual(f"down{layer}{len(FF_PARTS) - 1}", n_next, gain, dst)

            ffn(0, xa_hi, RMS_ATTN, lambda c: vcol("norm_kv", c), xb_hi)
            I = START["kv"]
            ahead(I, 0)
            for c in range(KC):
                gain_high(xa_hi, c, lambda c: vcol("norm_mix", KC + c))
            ahead(I, 1)
            act.wait_ge(sum_done, SUMS[RMS_ATTN])
            own.done(nc.scalar.activation(r_col[:, 0, :], aps[:, 2, 0:NT], ACT.Ln, bias=eps_col[:], scale=1.0 / D))
            own.done(nc.scalar.activation(r_col[:, 1, :], r_col[:, 0, :], ACT.Exp, scale=-0.5))
            rms_finish(RMS_ATTN)
            ahead(I, 2)
            full(I, 3)
            act.sem_inc(tile_done[2], 1)
            ahead(I, 3)
            for t in range(NT):
                ins = nc.scalar.mul(vtok[:, t, :], gps[:, 2 + t // 2, (t % 2) * 2 * P:(t % 2 + 1) * 2 * P], r_col[:, 1, t:t + 1])
                if t % 2:
                    ins.then_inc(evicted[2 + t // 2], 1)

            def attention_out(c):
                for e in range(2):
                    hh = 2 * c + e
                    act.wait_ge(pt_full, hh + 1)
                    nc.scalar.copy(pT[:, e, 0:4, :], aps[:, 2 * e, :].rearrange("p (n t) -> p n t", t=P))
                    nc.scalar.copy(pT[:, e, 4:7, :], aps[:, 2 * e + 1, 0:3 * P].rearrange("p (n t) -> p n t", t=P))\
                      .then_inc(pt_ready, 1)
                act.wait_ge(o_full, c + 1)
                nc.scalar.copy(xb_hi[:, c, :], gps[:, (c + 3) % SLOTS, :]).then_inc(o_hi, 1)

            def attention_exp(c):
                for e in range(2):
                    hh = 2 * c + e
                    act.wait_ge(max_ready, hh + 1)
                    for n in range(NT):
                        s = scores[:, e, n, P if n == 0 else 0:BAND]
                        nc.scalar.activation(s, s, ACT.Exp, bias=neg_max[:, e, n:n + 1],
                                             accum_out=row_sum[:, e, n:n + 1])
                    nc.scalar.activation(sink_exp[:, e, :], neg_max[:, e, :], ACT.Exp, bias=sink[:, hh:hh + 1])\
                      .then_inc(exp_ready, 1)

            for c in range(KC + 1):
                if c < KC:
                    ahead(START["q"] + c // SLOTS, c % SLOTS)
                if c >= 1:
                    attention_out(c - 1)
                if c < KC:
                    attention_exp(c)
            residual("w_o", RMS_FF1, ffn_gain(1), xa_hi)
            rms_finish(RMS_FF1)
            ffn(1, xb_hi, RMS_LAST)
            rms_finish(RMS_LAST)

        @block.vector
        def _(dve):
            own = Steps(dve, dve_own)
            TT, TS, STT = nc.vector.tensor_tensor, nc.vector.tensor_scalar, nc.vector.scalar_tensor_tensor
            silu_c = mixed[:, KC - 2:, :].rearrange("p k t -> p (k t)")

            def full(I, j):
                dve.wait_ge(tile_done[j], I + 2)
                return gps[:, j, :]

            for j in range(SLOTS):
                dve.sem_inc(evicted[j], 1)
                dve.sem_inc(taken[j], 1)
            dve.sem_inc(gates_used, 1)
            dve.sem_inc(mixed_ready, 1)
            dve.sem_inc(ff_lo, 2)

            def x_build(src, gain, hi, lo):
                dve.wait_ge(rstd_ready, RMS_LN + 1)

                def h(c):
                    STT(hbuf[:, c % 4, :], src[:, c, :], gain(c), rstd[:], ALU.mult, ALU.mult).then_inc(h_ready, 1)

                for c in range(3):
                    h(c)
                for c in range(KC):
                    dve.wait_ge(xh_ready, KC * X_PW2 + c + 1)
                    TT(lo[:, c, :], src[:, c, :], hi[:, c, :].bitcast(F32), ALU.subtract).then_inc(x_ready, 1)
                    if c + 3 < KC:
                        h(c + 3)

            def gain_low(b, c, gain, hi, lo):
                dve.wait_ge(xh_ready, KC * b + c + 1)
                STT(lo[:, c, :], res[:, c, :], gain(c), hi[:, c, :].bitcast(F32), ALU.mult, ALU.subtract).then_inc(x_ready, 1)

            nc.vector.memset(ones[:], 1.0)
            nc.vector.memset(eps_col[:], EPS).then_inc(made, 1)
            own.done(nc.vector.memset(reset[:], 1.0))
            own.done(nc.vector.memset(reset[:, :].rearrange("p (t s) -> p t s", s=P)[:, :, 0:1], 0.0))
            own.done(nc.vector.memset(at_h[:], 0.0))
            dve.wait_ge(vec_loaded, 16)
            l0, l1 = (vec[:, VEC[n]:VEC[n] + KC] for n in ("lb0", "lb1"))
            own.done(TT(lbt[:, 2, :], l0, l1, ALU.max))
            TT(lbt[:, 0, :], l0, lbt[:, 2, :], ALU.subtract)
            TT(lbt[:, 1, :], l1, lbt[:, 2, :], ALU.subtract).then_inc(lb_shift, 1)
            own.done(TT(conv_gain[:], vec[:, VEC["final_g"]:VEC["final_g"] + KC], vec[:, VEC["norm_mix"]:VEC["norm_mix"] + KC],
                        ALU.mult))
            dve.wait_ge(c_wide_ready, 1)
            own.done(TT(c_wide[:, 0, :], c_wide[:, 0, :], c_wide[:, 1, :], ALU.mult))

            def modulation(c):
                dve.wait_ge(ada_loaded[c], 16)
                for n, col in ((2 * c, KC + c), (2 * c + 1, c)):
                    own.mark(nc.vector.tensor_tensor_reduce(
                        ada_w[:, n, :], ada_w[:, n, :], c_wide[:, 0, :], op0=ALU.mult, op1=ALU.add, scale=1.0,
                        scalar=vcol("b_ada", col), accum_out=mod[:, col:col + 1]))
                own.wait()
                own.mark(STT(mix_gain[:, c:c + 1], mod[:, KC + c:KC + c + 1], 1.0, vcol("norm_g", c), ALU.add, ALU.mult))

            def scaled_input(c):
                if c == 0:
                    dve.wait_ge(rstd_ready, RMS_MIX + 1)
                if c >= 4:
                    dve.wait_ge(x_ready, c - 3)
                own.wait()
                STT(hbuf[:, c % 4, :], x0[:, c, :], mix_gain[:, c:c + 1], rstd[:], ALU.mult, ALU.mult).then_inc(h_ready, 1)

            def input_low(c):
                dve.wait_ge(xh_ready, c + 1)
                dve.wait_ge(x_ready, c)
                TT(xa_lo[:, c, :], hbuf[:, c % 4, :], xa_hi[:, c, :].bitcast(F32), ALU.subtract).then_inc(x_ready, 1)

            for c in range(KC):
                modulation(c)
                if c >= 2:
                    for n in range(0, 3) if c == 2 else (c,):
                        scaled_input(n)
            for c in range(KC - LAST_LOW, KC):
                input_low(c)
            own.done(nc.vector.tensor_copy(silu_c, c_wide[:, 0, :]))
            dve.wait_ge(lb_exp, 1)
            own.done(TT(lbt[:, 0, :], lbt[:, 2, :], lbt[:, 3, :], ALU.add))
            own.done(nc.vector.reciprocal(lbt[:, 1, :], lbt[:, 0, :]))
            own.done(TT(lower[:], lbt[:, 2, :], lbt[:, 1, :], ALU.mult))
            own.done(TS(one_minus[:], lower[:], -1.0, 1.0, ALU.mult, ALU.add))

            with dve.Fori(0, PAIRS) as p:
                own.enter(p, PAIR_STEPS)

                def at(c):
                    return p * (PAIR_CHUNKS // SLOTS) + (START["pairs"] + c // SLOTS)

                def chunk(c):
                    return full(at(c), c % SLOTS)

                def was_evicted(c):
                    dve.wait_ge(evicted[c % SLOTS], at(c) + 2)

                def bank(u):
                    dve.wait_ge(bank_full[u % 4], p * USES[u % 4] + (u // 4 + 1))
                    return aps[:, u % 4, :]

                def was_taken(u):
                    dve.wait_ge(taken[u % 4], p * USES[u % 4] + (u // 4 + 2))

                def exponents(e):
                    x = cum[:, e, :]
                    for level in range(LEVELS):
                        left, right, mid = halves(x, level)
                        to_left, to_right, _ = halves(kt[:, level, :], level)
                        TT(to_left, mid, left, ALU.subtract)
                        TT(to_right, right, mid, ALU.subtract)
                    tiles = x.rearrange("p (t s) -> p t s", s=P)
                    TT(hbuf[:, 0, :].rearrange("p (t s) -> p t s", s=P),
                       tiles[:, :, P - 1:P].to_broadcast([P, NT, P]), tiles, ALU.subtract).then_inc(exps_ready, 1)

                def decayed(e):
                    dve.wait_ge(decay_ready, p * 2 + (e + 1))
                    qe, ke, grow = q[:, e, :], key[:, e, :], hbuf[:, 1, :]
                    def keys(l0, l1):
                        TT(kt[:, l0:l1, :], kt[:, l0:l1, :], ke[:, None, :].to_broadcast([P, l1 - l0, T]), ALU.mult)\
                            .then_inc(prep_done, 1)

                    for level in range(LEVELS):
                        _, right, _ = halves(qe, level)
                        _, dec, _ = halves(kt[:, level, :], level)
                        h = (P >> level) // 2
                        own.mark(TT(qt[:, level, :].rearrange("p (n h) -> p n h", h=h), right, dec, ALU.mult))
                    own.wait()
                    keys(0, PREP_SPLIT)
                    keys(PREP_SPLIT, LEVELS)
                    TT(k_far[:, :, :], ke[:, 0:3 * P].rearrange("p (t s) -> p t s", s=P),
                       hbuf[:, 0, 0:3 * P].rearrange("p (t s) -> p t s", s=P), ALU.mult)
                    TT(q_far[:, 0, :], qe[:, P:2 * P], grow[:, P:2 * P], ALU.mult)
                    TT(q_far[:, 3, :], qe[:, 2 * P:3 * P], grow[:, 2 * P:3 * P], ALU.mult)
                    own.done(TT(q_far[:, 5, :], qe[:, 3 * P:], grow[:, 3 * P:], ALU.mult))
                    TS(q_far[:, 1, :], q_far[:, 3, :], grow[:, 2 * P - 1:2 * P], None, ALU.mult)
                    own.done(TS(q_far[:, 4, :], q_far[:, 5, :], grow[:, 3 * P - 1:3 * P], None, ALU.mult))
                    TS(q_far[:, 2, :], q_far[:, 4, :], grow[:, 2 * P - 1:2 * P], None, ALU.mult).then_inc(prep_done, 1)

                def near_scores(e):
                    u = U_LV[e]
                    for n, levels in enumerate(LEVEL_BANKS):
                        b = bank(u + n)
                        dve.sem_inc(passed, 1)
                        for m, level in enumerate(levels):
                            h = (P >> level) // 2
                            out = diag(at_h).rearrange("p t (n s) -> p t n s", s=2 * h)[:, :, :, h:]
                            mask = lvl_mask[:, level, :].rearrange("p (n h) -> p n h", h=h)[:, None, :, :]
                            data = b[:, m * T // 2:(m + 1) * T // 2].rearrange("p (t n h) -> p t n h", t=NT, h=h)
                            ins = nc.vector.copy_predicated(out, mask.to_broadcast([P, NT, P // 2 // h, h]), data)
                            if m < len(levels) - 1:
                                own.done(ins)
                                dve.sem_inc(passed, 1)
                            else:
                                ins.then_inc(taken[(u + n) % 4], 1)
                                was_taken(u + n)
                    u += len(LEVEL_BANKS)
                    b = bank(u)
                    dve.sem_inc(passed, 1)
                    nc.vector.copy_predicated(diag(at_h), eye_mask[:, None, :].to_broadcast([P, NT, P]),
                                              b.rearrange("p (t s) -> p t s", s=P)).then_inc(taken[u % 4], 1)

                def causal(e):
                    for j in range(NT):
                        u = U_SC[e] + j
                        n = T - j * P
                        TT(at_r[:, j * (T + P):(j + 1) * T], bank(u)[:, 0:n], tri[:, 0:n], ALU.mult).then_inc(taken[u % 4], 1)

                def normalize(e, r, dst):
                    u = U_AV[e][r]
                    dve.wait_ge(hnorm, p * 4 + (2 * e + r + 1))
                    TT(dst, aps[:, u % 4, :], (lnv, rstd)[r][:], ALU.mult).then_inc(taken[u % 4], 1)
                    was_taken(u)

                def z_gate(c, e, r, gain):
                    dve.wait_ge(gate_sig, p * 4 + (2 * r + e + 1))
                    STT(gates[:, 2 * r + e, :], gps[:, c % SLOTS, :], vdyn(gain, p * 2 + e), sq[:, e, :],
                        ALU.mult, ALU.mult).then_inc(evicted[c % SLOTS], 1)

                def branch_gate(c, e, r):
                    was_evicted(c)
                    was_evicted(c - 2)
                    TT(gates[:, 2 * r + e, :], gates[:, 2 * r + e, :], sq[:, e, :], ALU.mult).then_inc(gates_used, 1)

                for e in range(2):
                    was_evicted(e)
                    own.mark(TS(forget[:, e, :], forget[:, e, :], one_minus[:, bass.ds(p * 2 + e, 1)],
                                lower[:, bass.ds(p * 2 + e, 1)], ALU.mult, ALU.add))
                own.wait()
                own.done(TS(key[:], forget[:], -1.0, 1.0, ALU.mult, ALU.add))
                TS(forget[:], forget[:], TINY, None, ALU.max).then_inc(f_ready, 1)
                for e in range(2):
                    dve.wait_ge(q_sig, p * 2 + (e + 1))
                    TT(q[:, e, :], gps[:, 2 + e, :], sq[:, e, :], ALU.mult).then_inc(evicted[2 + e], 1)
                dve.wait_ge(logf_ready, p + 1)
                for e in range(2):
                    own.mark(nc.vector.tensor_tensor_scan(cum[:, e, :], reset[:], forget[:, e, :], 0.0, ALU.mult, ALU.add))
                own.wait()
                exponents(0)
                for e in range(2):
                    was_evicted(2 + e)
                decayed(0)
                for e in range(2):
                    c = GATE_CHUNKS[e]
                    dve.wait_ge(raw_in[c % SLOTS], at(c) * 16 + 16)
                    own.done(nc.vector.tensor_tensor_reduce(
                        hbuf[:, 2:4, :].rearrange("p e t -> p (e t)"), w_raw[:, c % SLOTS, :], silu_c, op0=ALU.mult, op1=ALU.add,
                        scale=1.0, scalar=0.0, accum_out=gate_sum[:, e:e + 1]))
                    dve.sem_inc(hi_ready[c % SLOTS], 1)
                    dve.sem_inc(lo_ready[c % SLOTS], 1)
                    TT(mod[:, bass.ds(p * 2 + (2 * KC + e), 1)], gate_sum[:, e:e + 1], vdyn("b_ada", p * 2 + (2 * KC + e)),
                       ALU.add)
                near_scores(0)
                for e in range(2):
                    was_evicted(4 + e)
                    dve.sem_inc(evicted[e], 1)
                dve.wait_ge(tabs_in, p * 16 + 16)
                for n in range(2):
                    was_evicted(6 + n)
                    own.mark(TT(unit[:, n, :], unit[:, n, :], gates[:, 2 * n + 1, :], ALU.mult))
                    own.done(TT(rqk[:, n, :], rqk[:, n, :], gates[:, 2 * n, :], ALU.mult))
                    TT(rqk[:, n, :], rqk[:, n, :], unit[:, n, :], ALU.add).then_inc(rot_ready, 1)
                dve.wait_ge(rot_ready, p * 2 + 2)
                bank(U_LV[0] + 6)
                exponents(1)
                decayed(1)
                causal(0)
                z_gate(12, 0, 0, "hg_norm_g")
                z_gate(13, 1, 0, "hg_norm_g")
                branch_gate(14, 0, 0)
                branch_gate(15, 1, 0)
                normalize(0, 0, unit[:, 0, :])
                normalize(0, 1, unit[:, 1, :])
                dve.wait_ge(gates_used, p * 4 + 3)

                def take_norm(e, r):
                    own.done(TT(gates[:, 2 * r + e, :], gates[:, 2 * r + e, :], unit[:, r, :], ALU.mult))

                take_norm(0, 0)
                z_gate(16, 0, 1, "ret_norm_g")
                near_scores(1)
                was_evicted(16)
                take_norm(0, 1)
                z_gate(17, 1, 1, "ret_norm_g")
                causal(1)
                branch_gate(18, 0, 1)
                dve.wait_ge(gates_used, p * 4 + 4)
                TT(mixed[:, bass.ds(p * 2, 1), :], gates[:, 0:1, :], gates[:, 2:3, :], ALU.add).then_inc(mixed_ready, 1)
                normalize(1, 0, unit[:, 0, :])
                take_norm(1, 0)
                was_evicted(17)
                normalize(1, 1, unit[:, 1, :])
                take_norm(1, 1)
                branch_gate(19, 1, 1)
                dve.wait_ge(gates_used, p * 4 + 5)
                TT(mixed[:, bass.ds(p * 2 + 1, 1), :], gates[:, 1:2, :], gates[:, 3:4, :], ALU.add).then_inc(mixed_ready, 1)
                own.leave(PAIRS)

            dve.wait_ge(m_lo, FIRST_LOW)
            for c in range(FIRST_LOW, KC):
                dve.wait_ge(m_hi, c + 1)
                dve.wait_ge(mixed_ready, 2 * PAIRS + 1)
                TT(xa_lo[:, c, :], mixed[:, c, :], xa_hi[:, c, :].bitcast(F32), ALU.subtract).then_inc(m_lo, 1)
            nc.vector.memset(rel[32:33, :], NEG).then_inc(rel_copied, 1)
            nc.vector.memset(glu[:, :, 0:PAD], 0.0)
            taps = vec[:, VEC["w_dw"]:VEC["w_dw"] + TAP_GROUPS * TAP_GROUP * KC].rearrange("p (k c) -> p k c", c=KC)
            dve.wait_ge(taps_high, 1)
            TT(tap_lo[:], taps[:, :, DVE_CONV:], tap_hi[:].bitcast(F32), ALU.subtract).then_inc(taps_ready, 1)
            dve.wait_ge(res_in, 16)
            for j in range(2):
                dve.wait_ge(evicted[2 + j], START["w_out"] + 1)

            def residual(phase, n, scale=None, shift=None, build=None, double=False):

                def add_squares(m):
                    dve.wait_ge(sq_ready, KC * n + m + 1)
                    if m > 1:
                        dve.wait_ge(sq_used, USED[n] + m - 1)
                    ins = TT(lnv[:], sq[:, 0, :] if m == 1 else lnv[:], sq[:, m % 2, :], ALU.add)
                    if double:
                        total = hbuf[:, 2, :]
                        ins = TT(total, hbuf[:, 0, :] if m == 1 else total, hbuf[:, m % 2, :], ALU.add)
                    ins.then_inc(sq_used, 1)

                for c in range(KC):
                    I, j = START[phase] + c // SLOTS, c % SLOTS
                    b = full(I, j)
                    if scale is not None:
                        ins = STT(res[:, c, :], b, scale(c), res[:, c, :], ALU.mult, ALU.add)
                    elif shift is not None:
                        ins = STT(res[:, c, :], b, shift(c), res[:, c, :], ALU.add, ALU.add)
                    else:
                        ins = TT(res[:, c, :], b, res[:, c, :], ALU.add)
                    ins.then_inc(evicted[j], 1)
                    if c >= 2:
                        add_squares(c - 1)
                    if c >= 1 and build is not None:
                        gain_low(build[0], c - 1, *build[1:])
                if build is not None:
                    dve.wait_ge(evicted[SLOTS - 1], START[phase] + KC // SLOTS + 1)
                    gain_low(build[0], KC - 1, *build[1:])

            residual("w_out", RMS_FIRST, scale=lambda c: mod[:, 2 * KC + c:2 * KC + c + 1],
                     build=(X_CONV_IN, lambda c: conv_gain[:, c:c + 1], xb_hi, xb_lo), double=True)
            dve.wait_ge(rel_full, 1)
            nc.vector.tensor_copy(rel_rows[:], aps[0:AH, 3, 0:REACH + 1]).then_inc(rel_copied, 1)
            dve.wait_ge(rstd_ready, RMS_FIRST + 1)
            TT(sq[:, 1, :], aps[:, 1, :], sq[:, 0, :], ALU.mult).then_inc(double_ready, 1)
            dve.wait_ge(second_ready, 1)
            TT(lnv[:], rstd[:], sq[:, 0, :], ALU.mult).then_inc(both_ready, 1)
            dve.wait_ge(sq_ready, KC * RMS_FIRST + KC)

            def normed_residual(c):
                STT(res[:, c, :], res[:, c, :], vcol("final_g", c), rstd[:], ALU.mult, ALU.mult)

            for c in range(KC):
                normed_residual(c)
            def convolve(chunks):
                for n, c in enumerate(chunks):
                    dve.wait_ge(sig_ready, c + 1)
                    value = glu[:, bass.ds(c, 1), PAD:]
                    own.mark(STT(value, value, vdyn("b_pw1", c), conv[:, bass.ds(c, 1), :], ALU.add, ALU.mult))
                for k in range(TAPS):
                    for n, c in enumerate(chunks):
                        out, src = conv[:, bass.ds(c, 1), :], glu[:, bass.ds(c, 1), k:k + T]
                        w = vdyn("w_dw", c + k * KC)
                        own.wait(own.local - len(chunks) + 1)
                        if k == 0:
                            own.mark(TS(out, src, w, vdyn("b_dw", c), ALU.mult, ALU.add))
                        else:
                            own.mark(STT(out, src, w, out, ALU.mult, ALU.add))
                own.wait()
                dve.sem_inc(conv_done, 1)

            convolve([0])
            with dve.Fori(0, GLU_LOOP) as i:
                own.enter(i, 2 * TAPS + 2)
                convolve([i * 2 + 1, i * 2 + 2])
                own.leave(GLU_LOOP)
            c = KC - 1
            dve.wait_ge(glu_ready, PE_CONV)
            for k in range(TAP_GROUP):
                src, w = glu[:, c, k:k + T], vcol("w_dw", c + k * KC)
                own.done(TS(conv[:, c, :], src, w, vcol("b_dw", c), ALU.mult, ALU.add) if k == 0 else
                         STT(conv[:, c, :], src, w, conv[:, c, :], ALU.mult, ALU.add))
            dve.wait_ge(conv_copied, PE_CONV - 1)
            dve.wait_ge(conv_full, PE_CONV)
            TT(conv[:, c, :], aps[:, 2 + (PE_CONV - 1) % 2, :], conv[:, c, :], ALU.add).then_inc(conv_copied, 1)
            dve.wait_ge(mean_done, 1)
            for c in range(KC):
                STT(conv[:, c, :], aps[:, 1, :], -1.0 / D, conv[:, c, :], ALU.mult, ALU.add).then_inc(center_done, 1)
            dve.wait_ge(center_done, KC)
            dve.wait_ge(x_ready, KC * X_PW2)
            x_build(conv, lambda c: vcol("ln_g", c), xa_hi, xa_lo)
            ffn_gain = lambda layer: lambda c: vcol("norm_ffn", layer * KC + c)
            residual("pw2", RMS_FF0, shift=lambda c: vcol("b_pw2", c), build=(X_FF0, ffn_gain(0), xb_hi, xb_lo))

            def ffn(layer, hidden_hi, hidden_lo, norm, n_next, build=None):
                dve.wait_ge(rstd_ready, norm + 1)
                for part, n in enumerate(FF_PARTS):
                    f0 = layer * FF_CHUNKS + sum(FF_PARTS[:part])
                    with dve.Fori(0, n // 2) as i:
                        I = i + START[f"up{layer}{part}"]
                        for m in range(2):
                            h = hbuf[:, 2 * m, :]
                            dve.wait_ge(ff_lo, i * 2 + (f0 + m + 1))
                            TT(sq[:, m, :], full(I, 2 * m), rstd[:], ALU.mult).then_inc(evicted[2 * m], 1)
                            TT(h, full(I, 2 * m + 1), rstd[:], ALU.mult).then_inc(evicted[2 * m + 1], 1)
                            dve.wait_ge(silu_ready, i * 2 + (f0 + m + 1))
                            dve.wait_ge(evicted[2 * m + 1], I + 2)
                            TT(h, h, sq[:, m, :], ALU.mult).then_inc(ff_ready, 1)
                            dve.wait_ge(ff_hi, i * 2 + (f0 + m + 1))
                            TT(hidden_lo[:, bass.ds(i * 2 + m, 1), :], hbuf[:, 2 * m:2 * m + 1, :],
                               hidden_hi[:, bass.ds(i * 2 + m, 1), :].bitcast(F32), ALU.subtract).then_inc(ff_lo, 1)
                    if part < len(FF_PARTS) - 1:
                        with dve.Fori(0, KC // SLOTS) as i:
                            for j in range(SLOTS):
                                r = res[:, bass.ds(i * SLOTS + j, 1), :]
                                full(i + START[f"down{layer}{part}"], j)
                                TT(r, gps[:, j:j + 1, :], r, ALU.add).then_inc(evicted[j], 1)
                residual(f"down{layer}{len(FF_PARTS) - 1}", n_next, build=build)

            ffn(0, xa_hi, xa_lo, RMS_FF0, RMS_ATTN, (X_KV, lambda c: vcol("norm_kv", c), xb_hi, xb_lo))
            for c in range(KC):
                gain_low(X_Q, c, lambda c: vcol("norm_mix", KC + c), xa_hi, xa_lo)
            dve.wait_ge(rstd_ready, RMS_ATTN + 1)
            for j in range(2):
                TT(kT[:, j, :], full(START["kv"], j), rstd[:], ALU.mult).then_inc(evicted[j], 1)
            dve.wait_ge(bias_in, 16)

            def queries(c):
                STT(qT[:, c % 2, :], full(START["q"] + c // SLOTS, c % SLOTS), HD ** -0.5, rstd[:], ALU.mult, ALU.mult)\
                    .then_inc(evicted[c % SLOTS], 1)

            def attention_max(c):
                for e in range(2):
                    hh = 2 * c + e
                    dve.wait_ge(s_full, hh + 1)
                    for n in range(NT):
                        k = slice(P if n == 0 else 0, BAND)
                        o = (n % 2) * BAND
                        last = nc.vector.tensor_tensor_reduce(
                            scores[:, e, n, k], aps[:, 2 * e + n // 2, o + k.start:o + k.stop], bias[:, hh, k],
                            op0=ALU.add, op1=ALU.max, scale=1.0, scalar=sink[:, hh:hh + 1],
                            accum_out=row_max[:, e, n:n + 1])
                    own.done(last)
                    TS(neg_max[:, e, :], row_max[:, e, :], -1.0, None, ALU.mult).then_inc(max_ready, 1)

            def attention_probs(c):
                for e in range(2):
                    hh = 2 * c + e
                    dve.wait_ge(exp_ready, hh + 1)
                    own.done(TT(row_max[:, e, :], row_sum[:, e, :], sink_exp[:, e, :], ALU.add))
                    own.done(nc.vector.reciprocal(row_inv[:, e, :], row_max[:, e, :]))
                    TS(scores[:, e, 0, P:], scores[:, e, 0, P:], row_inv[:, e, 0:1], None, ALU.mult)
                    TT(scores[:, e, 1:, :], scores[:, e, 1:, :], row_inv[:, e, 1:, None].to_broadcast([P, 3, BAND]), ALU.mult)\
                        .then_inc(p_ready, 1)

            def attention_low(c):
                dve.wait_ge(o_hi, c + 1)
                TT(xb_lo[:, c, :], gps[:, (c + 3) % SLOTS, :], xb_hi[:, c, :].bitcast(F32), ALU.subtract).then_inc(o_lo, 1)

            for c in range(KC + 1):
                if c < KC:
                    queries(c)
                if c >= 1:
                    attention_low(c - 1)
                if c < KC:
                    attention_max(c)
                    attention_probs(c)
            residual("w_o", RMS_FF1, build=(X_FF1, ffn_gain(1), xa_hi, xa_lo))
            ffn(1, xb_hi, xb_lo, RMS_FF1, RMS_LAST)
            dve.wait_ge(rstd_ready, RMS_LAST + 1)
            for c in range(KC):
                STT(y[:, c, :], res[:, c, :], vcol("norm_final", c), rstd[:], ALU.mult, ALU.mult).then_inc(y_ready, 1)

        @block.tensor
        def _(pe):
            mm = nc.tensor.matmul
            for j in range(SLOTS):
                pe.sem_inc(tile_done[j], 1)

            def ready(I, j):
                pe.wait_ge(lo_ready[j], I + 2)
                pe.wait_ge(evicted[j], I + 1)

            def dense(I, j, x, blocks=KC, operand=None, part=None):
                k0, k1 = part or (0, blocks)
                if k0 == 0:
                    ready(I, j)
                for k in range(k0, k1):
                    if operand is not None:
                        operand(k)
                    w = slice(k * P, (k + 1) * P)
                    mm(gps[:, j, :], w_hi[:, j, w], x[0][:, k, :], start=k == 0, stop=False)
                    mm(gps[:, j, :], w_hi[:, j, w], x[1][:, k, :], start=False, stop=False)
                    last = mm(gps[:, j, :], w_lo[:, j, w], x[0][:, k, :], start=False, stop=k == blocks - 1)
                if k1 == blocks:
                    last.then_inc(tile_done[j], 1)

            def dense_behind(I, j, x, high, low):
                ready(I, j)
                for k in range(KC):
                    high(k)
                    w = slice(k * P, (k + 1) * P)
                    mm(gps[:, j, :], w_hi[:, j, w], x[0][:, k, :], start=k == 0, stop=False)
                    mm(gps[:, j, :], w_lo[:, j, w], x[0][:, k, :], start=False, stop=False)
                for k in range(KC):
                    low(k)
                    last = mm(gps[:, j, :], w_hi[:, j, k * P:(k + 1) * P], x[1][:, k, :], start=False, stop=k == KC - 1)
                last.then_inc(tile_done[j], 1)

            def dense_tokens(I, j, x):
                ready(I, j)
                ready(I, j + 1)
                for t in range(NT):
                    tok = slice(t * P, (t + 1) * P)
                    out = gps[:, j + t // 2, 2 * (t % 2) * P:2 * (t % 2 + 1) * P]
                    for k in range(KC):
                        w = slice(k * P, (k + 1) * P)
                        wh, wl = w_hi[:, j:j + 2, w], w_lo[:, j:j + 2, w]
                        mm(out, x[0][:, k, tok], wh, start=k == 0, stop=False)
                        mm(out, x[1][:, k, tok], wh, start=False, stop=False)
                        last = mm(out, x[0][:, k, tok], wl, start=False, stop=k == KC - 1)
                last.then_inc(tile_done[j + 1], 1)

            def sum_squares(n, c):
                pe.wait_ge(sq_ready, KC * n + c + 1)
                mm(aps[:, 0, :], ones[:], sq[:, c % 2, :], start=c == 0, stop=c == KC - 1).then_inc(sum_done, 1)

            def sum_running(n, double=False, columns=False):
                pe.wait_ge(sq_used, USED[n] + KC - 2)
                pe.wait_ge(sq_ready, KC * n + KC)
                mm(aps[:, 0, :], ones[:], lnv[:], start=True, stop=False)
                last = mm(aps[:, 0, :], ones[:], sq[:, 1, :], start=False, stop=True)
                if double:
                    mm(aps[:, 1, :], ones[:], hbuf[:, 2, :], start=True, stop=False)
                    last = mm(aps[:, 1, :], ones[:], hbuf[:, 1, :], start=False, stop=True)
                if columns:
                    for t in range(NT):
                        tok = slice(t * P, (t + 1) * P)
                        mm(aps[:, 2, t:t + 1], lnv[:, tok], ones[:, 0:1], start=True, stop=False)
                        last = mm(aps[:, 2, t:t + 1], sq[:, 1, tok], ones[:, 0:1], start=False, stop=True)
                last.then_inc(sum_done, 1)

            def x_wait(b):
                return lambda k: pe.wait_ge(x_ready, KC * b + k + 1)

            xa, xb = (xa_hi, xa_lo), (xb_hi, xb_lo)
            pe.wait_ge(made, 1)
            for c in range(KC):
                sum_squares(RMS_MIX, c)
            for k in range(KC - 3):
                for c in range(3):
                    dense(START["pairs"], c, xa, operand=x_wait(X_MIX) if c == 0 else None, part=(k, k + 1))
            for c in range(3):
                dense(START["pairs"], c, xa, operand=x_wait(X_MIX) if c == 0 else None, part=(KC - 3, KC))

            def pair(p):
                def at(c):
                    return p * (PAIR_CHUNKS // SLOTS) + (START["pairs"] + c // SLOTS)

                def feature(c):
                    dense(at(c), c % SLOTS, xa)

                def bank(u):
                    pe.wait_ge(taken[u % 4], p * USES[u % 4] + (u // 4 + 1))
                    return aps[:, u % 4, :]

                def was_taken(u):
                    pe.wait_ge(taken[u % 4], p * USES[u % 4] + (u // 4 + 2))

                def hgrn_scores(e):
                    u = U_LV[e]
                    for n, levels in enumerate(LEVEL_BANKS):
                        if n < 2:
                            pe.wait_ge(prep_done, p * 6 + (3 * e + n + 1))
                        b = bank(u + n)
                        for m, level in enumerate(levels):
                            for t in range(NT):
                                h = P // 2
                                o = m * T // 2 + t * h
                                last = mm(b[:, o:o + h], kt[:, level, t * P:(t + 1) * P], qt[:, level, t * h:(t + 1) * h],
                                          start=True, stop=True)
                        last.then_inc(bank_full[(u + n) % 4], 1)
                    u += len(LEVEL_BANKS)
                    b = bank(u)
                    for t in range(NT):
                        s = slice(t * P, (t + 1) * P)
                        last = mm(b[:, s], key[:, e, s], q[:, e, s], start=True, stop=True)
                    last.then_inc(bank_full[u % 4], 1)
                    pe.wait_ge(prep_done, p * 6 + (3 * e + 3))
                    b = bank(u + 1)
                    mm(b[:, 0:3 * P], k_far[:, 0, :], q_far[:, 0:3, :].rearrange("p n t -> p (n t)"), start=True, stop=True)\
                        .then_inc(bank_full[(u + 1) % 4], 1)
                    b = bank(u + 2)
                    mm(b[:, 0:2 * P], k_far[:, 1, :], q_far[:, 3:5, :].rearrange("p n t -> p (n t)"), start=True, stop=True)
                    mm(b[:, 2 * P:3 * P], k_far[:, 2, :], q_far[:, 5, :], start=True, stop=True)\
                        .then_inc(bank_full[(u + 2) % 4], 1)

                def ret_scores(e):
                    pe.wait_ge(rot_ready, p * 2 + 2)
                    rows = slice(e * RET_DK, (e + 1) * RET_DK)
                    for j in range(NT):
                        u = U_SC[e] + j
                        mm(bank(u)[:, 0:T - j * P], rqk[rows, 1, j * P:(j + 1) * P], rqk[rows, 0, j * P:],
                           start=True, stop=True).then_inc(bank_full[u % 4], 1)

                def attend(e, r):
                    if r == 0:
                        for u in range(U_LV[e] + 3, U_LV[e] + 7):
                            was_taken(u)
                    else:
                        for j in range(NT):
                            was_taken(U_SC[e] + j)
                    u = U_AV[e][r]
                    b, at_x = bank(u), (at_h, at_r)[r]
                    for n in range(2):
                        c = (4, 10)[r] + n
                        pe.wait_ge(evicted[c % SLOTS], at(c) + 2)
                    for j in range(NT):
                        last = mm(b[:, j * P:], val[:, j, r, e * P:(e + 1) * P], at_x[:, j * (T + P):(j + 1) * T],
                                  start=j == 0, stop=j == NT - 1)
                    last.then_inc(bank_full[u % 4], 1)

                def head_sum(e, r):
                    u = U_NORM[e][r]
                    pe.wait_ge(osq_ready, p * 4 + (2 * e + r + 1))
                    mm(bank(u), ones[:], hbuf[:, 2 + r, :], start=True, stop=True).then_inc(bank_full[u % 4], 1)

                if isinstance(p, int):
                    feature(3)
                    pe.wait_ge(consts_in, CONSTS)
                else:
                    for c in range(4):
                        feature(c)
                dense_tokens(at(4), 0, xa)
                feature(6)
                feature(7)
                hgrn_scores(0)
                for c in GATE_CHUNKS:
                    pe.sem_inc(tile_done[c % SLOTS], 1)
                dense_tokens(at(10), 2, xa)
                feature(12)
                feature(13)
                ret_scores(0)
                attend(0, 0)
                feature(14)
                attend(0, 1)
                head_sum(0, 0)
                feature(15)
                head_sum(0, 1)
                feature(16)
                hgrn_scores(1)
                feature(17)
                ret_scores(1)
                attend(1, 0)
                attend(1, 1)
                feature(18)
                head_sum(1, 0)
                head_sum(1, 1)
                feature(19)

            pair(0)
            with pe.Fori(1, PAIRS) as p:
                pair(p)

            def layer(phase, x, blocks=KC, operand=None, first=0):
                for c in range(first, KC):
                    dense(START[phase] + c // SLOTS, c % SLOTS, x, blocks, operand if c == 0 else None)

            def layer_then(phase, quads, x, operand, between):
                I = START[phase]
                for j in range(SLOTS):
                    dense(I, j, x, operand=operand if j == 0 else None)
                    if j == 0:
                        between()
                with pe.Fori(1, quads) as i:
                    for j in range(SLOTS):
                        dense(i + I, j, x)

            dense_behind(START["w_out"], 0, xa, lambda k: pe.wait_ge(m_hi, k + 1), lambda k: pe.wait_ge(m_lo, k + 1))
            layer("w_out", xa, first=1)
            pe.wait_ge(hot_in_sem, 32)
            pe.wait_ge(rel_copied, 1)
            mm(aps[0:AH, 3, 0:REACH + 1], rel[:], hot[:], start=True, stop=True).then_inc(rel_full, 1)
            layer_then("pw1", KC // 2, xb, x_wait(X_CONV_IN), lambda: sum_running(RMS_FIRST, double=True))
            for m in range(PE_CONV):
                pe.wait_ge(glu_low, m + 1)
                if m >= 2:
                    pe.wait_ge(conv_copied, m - 1)
                k0 = first_group(m) * TAP_GROUP
                for k in range(k0, TAPS):
                    if k % TAP_GROUP == 0:
                        pe.wait_ge(diag_ready, m * TAP_GROUPS + (k - k0) // TAP_GROUP + 1)
                    out, src = aps[:, 2 + m % 2, :], slice(k, k + T)
                    mm(out, diag_hi[:, k, :], glu_hi[:, m % 2, src], start=k == k0, stop=False)
                    mm(out, diag_hi[:, k, :], glu_lo[:, m % 2, src], start=False, stop=False)
                    last = mm(out, diag_lo[:, k, :], glu_hi[:, m % 2, src], start=False, stop=k == TAPS - 1)
                    if k == TAPS - 1:
                        last.then_inc(conv_full, 1)
                    elif k % TAP_GROUP == TAP_GROUP - 1:
                        last.then_inc(diag_used, 1)
            pe.wait_ge(conv_sum, KC - 2)
            mm(aps[:, 1, :], ones[:], hbuf[:, 3, :], start=True, stop=False)
            pe.wait_ge(conv_copied, PE_CONV)
            mm(aps[:, 1, :], ones[:], conv[:, KC - 1, :], start=False, stop=True).then_inc(mean_done, 1)
            for c in range(KC):
                sum_squares(RMS_LN, c)
            dense_behind(START["pw2"], 0, xa, lambda k: pe.wait_ge(xh_ready, KC * X_PW2 + k + 1), x_wait(X_PW2))
            layer("pw2", xa, first=1)

            def ffn(layer_n, b, norm, x, hidden):
                for part, n in enumerate(FF_PARTS):
                    f0 = layer_n * FF_CHUNKS + sum(FF_PARTS[:part])
                    up = f"up{layer_n}{part}"
                    if part == 0:
                        layer_then(up, n // 2, x, x_wait(b), lambda: sum_running(norm))
                    else:
                        with pe.Fori(0, n // 2) as i:
                            for j in range(SLOTS):
                                dense(i + START[up], j, x)
                    ready_k = lambda k: pe.wait_ge(ff_lo, f0 + k + 3)
                    down = f"down{layer_n}{part}"
                    if part < len(FF_PARTS) - 1:
                        with pe.Fori(0, KC // SLOTS) as i:
                            for j in range(SLOTS):
                                dense(i + START[down], j, hidden, n, ready_k if j == 0 else None)
                    else:
                        layer(down, hidden, n, ready_k)

            ffn(0, X_FF0, RMS_FF0, xb, xa)
            I = START["kv"]
            for j in range(2):
                dense(I, j, xb, operand=x_wait(X_KV) if j == 0 else None)
                if j == 0:
                    sum_running(RMS_ATTN, columns=True)
            dense_tokens(I, 2, xb)

            def band_scores(c):
                for e in range(2):
                    hh = 2 * c + e
                    rows = slice(e * HD, (e + 1) * HD)
                    if e == 0:
                        pe.wait_ge(evicted[c % SLOTS], START["q"] + c // SLOTS + 2)
                    if hh >= 2:
                        pe.wait_ge(pt_ready, hh - 1)
                    for n in range(NT):
                        k0 = max(n - 1, 0) * P
                        o = (n % 2) * BAND + (P if n == 0 else 0)
                        last = mm(aps[:, 2 * e + n // 2, o:(n % 2 + 1) * BAND], qT[rows, c % 2, n * P:(n + 1) * P],
                                  kT[rows, c // 4, k0:(n + 1) * P], start=True, stop=True)
                    last.then_inc(s_full, 1)

            def band_values(c):
                for e in range(2):
                    hh = 2 * c + e
                    pe.wait_ge(p_ready, hh + 1)
                    for x in range(2 * NT - 1):
                        n, half = (x + 1) // 2, (x + 1) % 2
                        last = nc.tensor.transpose(aps[:, 2 * e + x // 4, (x % 4) * P:(x % 4 + 1) * P],
                                                   scores[:, e, n, half * P:(half + 1) * P], ident[:])
                    last.then_inc(pt_full, 1)
                for e in range(2):
                    pe.wait_ge(pt_ready, 2 * c + e + 1)
                    g = 2 * (c // 4) + e
                    for n in range(NT):
                        tiles = [(n, 0)] if n == 0 else [(n - 1, 2 * n - 1), (n, 2 * n)]
                        for m, (kb, x) in enumerate(tiles):
                            last = mm(gps[e * HD:(e + 1) * HD, (c + 3) % SLOTS, n * P:(n + 1) * P], vtok[:, kb, g * HD:(g + 1) * HD],
                                      pT[:, e, x, :], start=m == 0, stop=m == len(tiles) - 1)
                last.then_inc(o_full, 1)

            for c in range(KC):
                if c >= 3:
                    pe.wait_ge(o_lo, c - 2)
                dense(START["q"] + c // SLOTS, c % SLOTS, xa, operand=x_wait(X_Q) if c == 0 else None)
                if c >= 1:
                    band_values(c - 1)
                band_scores(c)
            for j in range(2):
                pe.wait_ge(o_lo, KC - 2 + j)
                dense(START["w_o"], j, xb, operand=lambda k: pe.wait_ge(o_lo, k + 1), part=(0, KC - 1))
            band_values(KC - 1)
            for j in range(2):
                dense(START["w_o"], j, xb, operand=lambda k: pe.wait_ge(o_lo, k + 1), part=(KC - 1, KC))
            layer("w_o", xb, first=2)
            ffn(1, X_FF1, RMS_FF1, xa, xb)
            sum_running(RMS_LAST)



def chunk(w):
    blocks = w.shape[0] // P
    out = np.zeros((P, KC * P), np.float32)
    out[:, :blocks * P] = w.reshape(blocks, P, P).transpose(1, 0, 2).reshape(P, blocks * P)
    return out


def head_order():
    group = AH // KVH
    return [(2 * (c // group) + e) * group + c % group for c in range(KC) for e in range(2)]


def weight_stream(w_ada, w_in, w_out, pw1, pw2, w_kv, w_q, w_o, up, down):
    def cols(w, c):
        return w[:, c * P:(c + 1) * P]

    def tokens(w, c):
        return [cols(w, c), cols(w, c + 1)]

    def turned(w, c):
        return cols(w, c).T.reshape(P, KC, P).transpose(1, 0, 2).reshape(D, P)

    out = []
    hq, hf, hi, hz = 0, KC, 2 * KC, 3 * KC
    rq, rk = 4 * KC, 4 * KC + KC // 2
    rv, rz, ga, gb = (5 * KC + n * KC for n in range(4))
    for p in range(PAIRS):
        a, b = 2 * p, 2 * p + 1
        out += [cols(w_in, hf + a), cols(w_in, hf + b), cols(w_in, hq + a), cols(w_in, hq + b)]
        out += tokens(w_in, hi + a) + [cols(w_in, rq + p), cols(w_in, rk + p)]
        out += [turned(w_ada, 2 * KC + a), turned(w_ada, 2 * KC + b)] + tokens(w_in, rv + a)
        for z, g in ((hz, ga), (rz, gb)):
            out += [cols(w_in, z + a), cols(w_in, z + b), cols(w_in, g + a), cols(w_in, g + b)]
    out += [cols(w_out, c) for c in range(KC)]
    for c in range(KC):
        out += [cols(pw1, c), cols(pw1, KC + c)]
    out += [cols(pw2, c) for c in range(KC)]
    heads = head_order()
    for layer in range(2):
        if layer == 1:
            out += [cols(w_kv, c) for c in range(4)]
            wq = w_q.reshape(D, AH, HD)[:, heads].reshape(D, D)
            wo = w_o.reshape(AH, HD, D)[heads].reshape(D, D)
            out += [cols(wq, c) for c in range(KC)] + [cols(wo, c) for c in range(KC)]
        f = 0
        for n in FF_PARTS:
            for c in range(f, f + n):
                out += [cols(up[layer], c), cols(up[layer], FF_CHUNKS + c)]
            out += [cols(down[layer][f * P:(f + n) * P], c) for c in range(KC)]
            f += n
    assert len(out) == QUADS * SLOTS
    return np.stack([chunk(w) for w in out])


def ada_chunks(w_ada):
    order = [n for c in range(KC) for n in (KC + c, c)]
    return np.stack([np.ascontiguousarray(w_ada[:, c * P:(c + 1) * P].T) for c in order])


def shape_constants():
    lin = np.linspace(0.0, 1.0, RET_DK // 2, dtype=np.float32)
    inv = (np.float32(1.0) / np.power(np.float32(10000.0), lin)).astype(np.float32)
    ang = (np.arange(T, dtype=np.float32)[:, None] * inv[None, :]).astype(np.float32)
    cos, sin = (np.tile(f(ang.astype(np.float64)).T, (2, 1)) for f in (np.cos, np.sin))
    sin[:ROT_HALF] *= -1.0
    tab = np.zeros((PAIRS, P, 4, T))
    t = np.arange(T)
    for h in range(HEADS):
        rows = slice((h % 2) * RET_DK, (h % 2 + 1) * RET_DK)
        gamma = 1.0 - 2.0 ** (-5.0 - h)
        tab[h // 2, rows, 0], tab[h // 2, rows, 1] = cos * gamma ** t, sin * gamma ** t
        back = gamma ** (-t) * RET_DK ** -0.5
        tab[h // 2, rows, 2], tab[h // 2, rows, 3] = cos * back, sin * back
    lvl = np.zeros((P, LEVELS, P // 2), np.int32)
    for level in range(LEVELS):
        size = P >> level
        right = [t for t in range(P) if t % size >= size // 2]
        for x, t_ in enumerate(right):
            for s in range(t_ // size * size, t_ // size * size + size // 2):
                lvl[s, level, x] = 1
    tri = (np.arange(T)[None, :] >= np.arange(P)[:, None]).astype(np.float32)
    hot = np.zeros((33, REACH + 1), np.float32)
    exact = 16
    for u in range(REACH + 1):
        d = BAND - 1 - u
        if not 0 <= d < P:
            hot[32, u] = 1.0
            continue
        log = np.float32(np.log(np.float32(max(d, 1)) / np.float32(exact))) / np.float32(np.log(P / exact))
        large = min(exact + int(np.float32(log * np.float32(32 - exact))), 31)
        hot[d if d < exact else large, u] = 1.0
    return {"ret_tab": tab.astype(np.float32), "lvl": lvl.reshape(P, -1), "eye": np.eye(P, dtype=np.int32),
            "tri": tri, "hot": hot, "ident": np.eye(P, dtype=np.float32)}


def kernel(**inputs):
    import concourse.bacc as bacc
    from concourse.bass_utils import run_bass_kernel_spmd

    a = {k: np.asarray(v) for k, v in inputs.items()}
    columns = {
        "norm_g": a["norm_g"], "b_ada": a["b_ada"], "lb0": a["hg_lb_logits"][0], "lb1": a["hg_lb_logits"][1],
        "hg_norm_g": a["hg_norm_g"], "ret_norm_g": a["ret_norm_g"], "norm_mix": a["norm_mix_2"],
        "norm_ffn": a["norm_ffn_2"], "b_pw1": a["conv_b_pw1_2"], "w_dw": a["conv_w_dw_2"], "b_dw": a["conv_b_dw_2"],
        "ln_g": a["conv_ln_g_2"], "ln_b": a["conv_ln_b_2"], "b_pw2": a["conv_b_pw2_2"], "norm_kv": a["norm_kv_2"],
        "norm_final": a["norm_final_2"], "final_g": a["final_g"], "c": a["c"],
    }
    heads = head_order()
    arrays = {
        "weights": weight_stream(a["w_ada"][0], a["w_in"][0], a["w_out"][0], a["conv_w_pw1_2"][0], a["conv_w_pw2_2"][0],
                                 a["w_kv_2"], a["w_q_2"][0], a["w_o_2"][0], a["ffn_w_up_2"], a["ffn_w_down_2"]),
        "ada_in": ada_chunks(a["w_ada"][0]),
        "c_in": np.ascontiguousarray(a["c"].reshape(1, D)),
        "xT": np.ascontiguousarray(a["x"][0].T),
        "vec_in": np.ascontiguousarray(np.concatenate([columns[n].reshape(-1) for n in VEC]).reshape(VECS, P).T),
        "sinks_in": np.ascontiguousarray(a["sinks_2"].reshape(1, AH)[:, heads]),
        "rel_in": np.ascontiguousarray(a["rel_bias_2"][:, heads]),
    }
    arrays |= {f"{k}_in" if k != "ret_tab" else k: v for k, v in shape_constants().items()}
    nc = bacc.Bacc("TRN2", target_bir_lowering=False, num_devices=1)
    aps = {k: nc.dram_tensor(f"{k}_dram", v.shape, mybir.dt.from_np(v.dtype), kind="ExternalInput").ap()
           for k, v in arrays.items()}
    scratch = nc.dram_tensor("rel_scratch_dram", (AH, P, REACH + 1), F32, kind="Internal").ap()
    outT = nc.dram_tensor("outT_dram", (D, T), F32, kind="ExternalOutput").ap()
    program(nc, rel_scratch=scratch, outT=outT, **aps)
    r = run_bass_kernel_spmd(nc, [{f"{k}_dram": v for k, v in arrays.items()}], core_ids=[0])
    return np.ascontiguousarray(np.asarray(r.results[0]["outT_dram"]).T)[None]
```
